# Optimizing a Trainium2 kernel written in Bass

```python
import jax, jax.numpy as jnp
from jax import lax
import numpy as np

D_MODEL = 1024
BATCH = 1
SEQ = 1024
DEPTH = 1

CHUNK = 64
MEM_LEN = 256
CONV_WIDTH = D_MODEL // 2
CONV_K = 3
SB_HEADS = 8
SB_HEAD_DIM = 64
SB_WIDTH = SB_HEADS * SB_HEAD_DIM
MIX_WIDTH = CONV_WIDTH + SB_WIDTH
Q_BLOCK = 128
XA_HEADS = 4
XA_HEAD_DIM = D_MODEL // XA_HEADS
XA_WIDTH = XA_HEADS * XA_HEAD_DIM
N_EXPERTS = 32
TOP_K = 4
D_EXPERT = D_MODEL
SWIGLU_ALPHA = 1.702
SWIGLU_LIMIT = 7.0
MOE_BLOCK = 128
EPS = 1e-6

kernel_name = "hybrid_shortconv_stickbreaking_memxattn_moe"

def rms_norm(x, g):
    xf = x.astype(jnp.float32)
    y = xf * lax.rsqrt(jnp.mean(xf * xf, axis=-1, keepdims=True) + EPS)
    return (y * g.astype(jnp.float32)).astype(x.dtype)

def short_gated_conv(u, gate_b, gate_c, w_conv):
    v = gate_c * u
    y = lax.conv_general_dilated(
        v, w_conv[:, None, :].astype(v.dtype), window_strides=(1,),
        padding=[(CONV_K - 1, 0)], dimension_numbers=("NWC", "WIO", "NWC"),
        feature_group_count=v.shape[-1])
    return gate_b * y

def stick_breaking_attention(q, k, v):
    S, dh = q.shape[2], q.shape[3]
    scale = dh ** -0.5
    outs = []
    for q0 in range(0, S, Q_BLOCK):
        q1 = q0 + Q_BLOCK
        kb, vb = k[:, :, :q1], v[:, :, :q1]
        z = jnp.einsum("bhqd,bhkd->bhqk", q[:, :, q0:q1], kb).astype(jnp.float32) * scale
        t_pos = jnp.arange(q0, q1)[:, None]
        s_pos = jnp.arange(q1)[None, :]
        mask = s_pos < t_pos
        log_keep = jnp.where(mask, jax.nn.log_sigmoid(-z), 0.0)
        after = lax.cumsum(log_keep, axis=3, reverse=True) - log_keep
        a = jnp.where(mask, jnp.exp(jax.nn.log_sigmoid(z) + after), 0.0)
        outs.append(jnp.einsum("bhqk,bhkd->bhqd", a.astype(vb.dtype), vb))
    return jnp.concatenate(outs, axis=2)

def hybrid_mixer(h, w_in, w_conv, g_conv_out, g_sb_out, w_out):
    bsz, S, _ = h.shape
    proj = h @ w_in
    cw, sw = CONV_WIDTH, SB_WIDTH
    splits = [cw, 2 * cw, 3 * cw, 3 * cw + sw, 3 * cw + 2 * sw]
    u, gate_b, gate_c, q, k, v = jnp.split(proj, splits, axis=-1)
    y_conv = rms_norm(short_gated_conv(u, gate_b, gate_c, w_conv), g_conv_out)

    def heads(t):
        return t.reshape(bsz, S, SB_HEADS, SB_HEAD_DIM).transpose(0, 2, 1, 3)

    o = stick_breaking_attention(heads(q), heads(k), heads(v)).transpose(0, 2, 1, 3)
    y_sb = rms_norm(o, g_sb_out.reshape(SB_HEADS, SB_HEAD_DIM)).reshape(bsz, S, SB_WIDTH)
    return jnp.concatenate([y_conv, y_sb], axis=-1) @ w_out

def memory_cross_attention(h, m, w_xq, w_xkv, w_xo):
    bsz, S, _ = h.shape
    n_mem = m.shape[1]
    q = (h @ w_xq).reshape(bsz, S, XA_HEADS, XA_HEAD_DIM)
    kv = (m @ w_xkv).reshape(bsz, n_mem, 2, XA_HEADS, XA_HEAD_DIM)
    k, v = kv[:, :, 0], kv[:, :, 1]
    s = jnp.einsum("bqhd,bkhd->bhqk", q, k).astype(jnp.float32) * (XA_HEAD_DIM ** -0.5)
    p = jax.nn.softmax(s, axis=-1).astype(v.dtype)
    o = jnp.einsum("bhqk,bkhd->bqhd", p, v).reshape(bsz, S, XA_WIDTH)
    return o @ w_xo

def moe_ffn(h, w_router, b_router, w_gate_up, b_gate_up, w_down, b_down):
    n_tok, d = h.shape
    logits = (h @ w_router).astype(jnp.float32) + b_router.astype(jnp.float32)
    top_val, top_idx = lax.top_k(logits, TOP_K)
    gates = jax.nn.softmax(top_val, axis=-1).astype(h.dtype)
    n_assign = n_tok * TOP_K
    flat_e = top_idx.reshape(-1)
    flat_tok = jnp.arange(n_assign, dtype=jnp.int32) // TOP_K
    flat_g = gates.reshape(-1)
    order = jnp.argsort(flat_e)
    sorted_e = flat_e[order]
    counts = jnp.bincount(flat_e, length=N_EXPERTS)
    group_start = jnp.cumsum(counts) - counts
    padded = (counts + MOE_BLOCK - 1) // MOE_BLOCK * MOE_BLOCK
    padded_end = jnp.cumsum(padded)
    padded_start = padded_end - padded
    dest = padded_start[sorted_e] + jnp.arange(n_assign) - group_start[sorted_e]
    n_blocks = -(-n_assign // MOE_BLOCK) + N_EXPERTS
    n_rows = n_blocks * MOE_BLOCK
    row_tok = jnp.zeros((n_rows,), jnp.int32).at[dest].set(flat_tok[order])
    row_gate = jnp.zeros((n_rows,), h.dtype).at[dest].set(flat_g[order])
    block_e = jnp.minimum(
        jnp.searchsorted(padded_end, jnp.arange(n_blocks) * MOE_BLOCK, side="right"),
        N_EXPERTS - 1)
    xb = h[row_tok].reshape(n_blocks, MOE_BLOCK, d)

    def expert_block(args):
        xe, e = args
        gu = xe @ w_gate_up[e] + b_gate_up[e]
        g = jnp.minimum(gu[:, 0::2], SWIGLU_LIMIT)
        up = jnp.clip(gu[:, 1::2], -SWIGLU_LIMIT, SWIGLU_LIMIT)
        glu = g * jax.nn.sigmoid(g * SWIGLU_ALPHA)
        return ((up + 1.0) * glu) @ w_down[e] + b_down[e]

    yb = lax.map(expert_block, (xb, block_e)).reshape(n_rows, d)
    return jnp.zeros_like(h).at[row_tok].add(yb * row_gate[:, None])

def setup_inputs(seed: int = 0) -> dict:
    key = jax.random.key(seed)
    ks = jax.random.split(key, 24)
    f32 = jnp.float32
    L = DEPTH

    def nrm(k, shape, scale):
        return jax.random.normal(k, shape, f32) * scale

    def gain(k, shape):
        return 1.0 + 0.05 * jax.random.normal(k, shape, f32)

    return {
        "x": nrm(ks[0], (BATCH, SEQ, D_MODEL), 1.0),
        "mem": nrm(ks[1], (BATCH, MEM_LEN, D_MODEL), 1.0),
        "g_mix": gain(ks[2], (L, D_MODEL)),
        "w_in": nrm(ks[3], (L, D_MODEL, 3 * MIX_WIDTH), D_MODEL ** -0.5),
        "w_conv": nrm(ks[4], (L, CONV_K, CONV_WIDTH), CONV_K ** -0.5),
        "g_conv_out": gain(ks[5], (L, CONV_WIDTH)),
        "g_sb_out": gain(ks[6], (L, SB_WIDTH)),
        "w_out": nrm(ks[7], (L, MIX_WIDTH, D_MODEL), MIX_WIDTH ** -0.5),
        "g_xattn": gain(ks[8], (L, D_MODEL)),
        "g_mem": gain(ks[9], (L, D_MODEL)),
        "w_xq": nrm(ks[10], (L, D_MODEL, XA_WIDTH), D_MODEL ** -0.5),
        "w_xkv": nrm(ks[11], (L, D_MODEL, 2 * XA_WIDTH), D_MODEL ** -0.5),
        "w_xo": nrm(ks[12], (L, XA_WIDTH, D_MODEL), XA_WIDTH ** -0.5),
        "g_ffn": gain(ks[13], (L, D_MODEL)),
        "w_router": nrm(ks[14], (L, D_MODEL, N_EXPERTS), D_MODEL ** -0.5),
        "b_router": nrm(ks[15], (L, N_EXPERTS), 0.01),
        "w_gate_up": nrm(ks[16], (L, N_EXPERTS, D_MODEL, 2 * D_EXPERT), D_MODEL ** -0.5),
        "b_gate_up": nrm(ks[17], (L, N_EXPERTS, 2 * D_EXPERT), 0.01),
        "w_down": nrm(ks[18], (L, N_EXPERTS, D_EXPERT, D_MODEL), D_EXPERT ** -0.5),
        "b_down": nrm(ks[19], (L, N_EXPERTS, D_MODEL), 0.01),
        "g_final": gain(ks[20], (D_MODEL,)),
    }

def reference(x, mem, g_mix, w_in, w_conv, g_conv_out, g_sb_out, w_out, g_xattn, g_mem,
              w_xq, w_xkv, w_xo, g_ffn, w_router, b_router, w_gate_up, b_gate_up,
              w_down, b_down, g_final):
    bsz, S, d = x.shape
    for l in range(DEPTH):
        h = rms_norm(x, g_mix[l])
        x = x + hybrid_mixer(h, w_in[l], w_conv[l], g_conv_out[l], g_sb_out[l], w_out[l])
        h = rms_norm(x, g_xattn[l])
        m = rms_norm(mem, g_mem[l])
        x = x + memory_cross_attention(h, m, w_xq[l], w_xkv[l], w_xo[l])
        h = rms_norm(x, g_ffn[l]).reshape(bsz * S, d)
        x = x + moe_ffn(h, w_router[l], b_router[l], w_gate_up[l], b_gate_up[l],
                        w_down[l], b_down[l]).reshape(bsz, S, d)
    return rms_norm(x, g_final)


_drawn_inputs = setup_inputs


def setup_inputs(seed=0):
    import zlib

    import numpy as np

    out = dict(_drawn_inputs(seed))
    spreads = {}
    factors = {'g_xattn': 4.876,
     'g_mem': 3.705,
     'b_router': 11.936,
     'b_gate_up': 33.683,
     'b_down': 39.054}
    for name, (base, spread) in spreads.items():
        noise = np.random.default_rng([zlib.crc32(name.encode()), seed]).standard_normal(out[name].shape)
        drawn = base * np.exp(spread * noise) if base else spread * noise
        out[name] = __import__('jax').numpy.asarray(drawn.astype(out[name].dtype))
    for name, factor in factors.items():
        out[name] = (out[name] * factor).astype(out[name].dtype)
    return out
```

```python
from contextlib import ExitStack

import concourse.bass as bass
from concourse import mybir

f32 = mybir.dt.float32
f32r = mybir.dt.float32r
bf16 = mybir.dt.bfloat16
i32 = mybir.dt.int32
u32 = mybir.dt.uint32
ALU = mybir.AluOpType
ACT = mybir.ActivationFunctionType
AX = mybir.AxisListType.X

P = 128
D = 1024
SEQ = 1024
MEM = 256
KT = D // P
TT = SEQ // P
CW = 512
HEADS, HD = 8, 64
XH, XD = 4, 256
NE, TOPK = 32, 4
EPS = 1e-6
LIMIT, ALPHA = 7.0, 1.702
BLOCK = 128
USED = SEQ * TOPK // BLOCK + NE
NBLK = USED + 1
N = 512
RAW = 4
UNIT = 2048


class Stage(ExitStack):

    cleared = {}

    def __init__(self, nc):
        super().__init__()
        self.nc, self.sems = nc, []

    def sem(self, name):
        self.sems.append(self.nc.alloc_semaphore(name))
        return self.sems[-1]

    def __exit__(self, *exc):
        if exc[0] is None:
            for s in self.sems:
                self.nc.gpsimd.sem_clear(s)
            for s in Stage.cleared.pop(id(self.nc), []):
                self.nc.release_semaphore(s)
            Stage.cleared[id(self.nc)] = self.sems
        return super().__exit__(*exc)


class Ring:

    def __init__(self, nc, ctx, units):
        self.nc, self.units = nc, units
        self.raw = ctx.enter_context(nc.sbuf_tensor("w_raw", [P, RAW, UNIT], f32))
        self.ready = [ctx.enter_context(nc.semaphore(f"w_loaded{s}")) for s in range(RAW)]
        self.hi_done = ctx.enter_context(nc.semaphore("w_hi_done"))
        self.lo_done = ctx.enter_context(nc.semaphore("w_lo_done"))

    def load(self, sp, n):
        if n >= len(self.units):
            return
        if n >= RAW:
            sp.wait_ge(self.lo_done, n - RAW + 1)
        ap = self.units[n]
        dst = self.raw[:, n % RAW, :].rearrange("p (k c) -> p k c", k=ap.shape[1])
        sp.dma_start(dst, ap).then_inc(self.ready[n % RAW], 16)

    def hi(self, act, n, dst):
        act.wait_ge(self.ready[n % RAW], 16 * (n // RAW + 1))
        self.nc.scalar.copy(dst, self.raw[:, n % RAW, :]).then_inc(self.hi_done, 1)

    def lo(self, dve, n, hi, dst):
        dve.wait_ge(self.hi_done, n + 1)
        self.nc.vector.tensor_tensor(dst, self.raw[:, n % RAW, :], hi.bitcast(f32),
                                     ALU.subtract).then_inc(self.lo_done, 1)


def mm3(nc, out, lh, ll, rh, rl, start, stop):
    nc.tensor.matmul(out, ll, rh, start=start, stop=False)
    nc.tensor.matmul(out, lh, rl, start=False, stop=False)
    return nc.tensor.matmul(out, lh, rh, start=False, stop=stop)


class RowNorm:

    def __init__(self, nc, ctx, name, src, ready, gain, gain_ready, ident, eps, banks, dest, hn_free=None, scratch=None):
        self.nc, self.src, self.ready, self.gain, self.gain_ready = nc, src, ready, gain, gain_ready
        self.ident, self.eps, self.banks, self.dest, self.hn_free = ident, eps, banks, dest, hn_free
        if scratch is None:
            self.junk = ctx.enter_context(nc.sbuf_tensor(f"{name}_square", [P, D], f32))
            self.hn = ctx.enter_context(nc.sbuf_tensor(f"{name}_rows", [P, 2, D], f32))
        else:
            self.junk, self.hn = scratch
        self.stat = ctx.enter_context(nc.sbuf_tensor(f"{name}_stat", [P, 3, TT], f32))
        self.sumsq_done, self.rms_done, self.inv_done, self.rows_done, self.turned, self.hi_done, \
            self.lo_done = [ctx.sem(f"{name}_{s}") for s in
                            ("sumsq", "rms", "inv", "rows", "turned", "hi", "lo")]

    def act_stats(self, act, t):
        nc = self.nc
        self.ready(act, t)
        if t:
            act.wait_ge(self.sumsq_done, t)
        nc.scalar.activation(self.junk[:, :], self.src(t), ACT.Square,
                             accum_out=self.stat[:, 0, t:t + 1]).then_inc(self.sumsq_done, 1)
        act.wait_ge(self.sumsq_done, t + 1)
        nc.scalar.activation(self.stat[:, 1, t:t + 1], self.stat[:, 0, t:t + 1], ACT.Sqrt,
                             scale=1.0 / D, bias=self.eps[:, 0:1]).then_inc(self.rms_done, 1)

    def dve_rows(self, dve, t):
        nc = self.nc
        dve.wait_ge(self.rms_done, t + 1)
        nc.vector.reciprocal(self.stat[:, 2, t:t + 1], self.stat[:, 1, t:t + 1]).then_inc(self.inv_done, 1)
        dve.wait_ge(self.inv_done, t + 1)
        self.ready(dve, t)
        if t == 0:
            self.gain_ready(dve)
        if t >= 2:
            dve.wait_ge(self.turned, 2 * (t - 1))
            if self.hn_free:
                self.hn_free(dve, t - 2)
        nc.vector.scalar_tensor_tensor(out=self.hn[:, t % 2, :], in0=self.src(t), scalar=self.stat[:, 2, t:t + 1],
                                       in1=self.gain, op0=ALU.mult, op1=ALU.mult).then_inc(self.rows_done, 1)

    def pe_turn(self, pe, t):
        pe.wait_ge(self.rows_done, t + 1)
        nb = len(self.banks)
        for q in range(2):
            n = 2 * t + q
            if n >= nb:
                pe.wait_ge(self.lo_done, n - nb + 1)
            bank = self.banks[n % nb]
            for k in range(4):
                c = (4 * q + k) * P
                last = self.nc.tensor.transpose(bank[:, k * P:(k + 1) * P], self.hn[:, t % 2, c:c + P],
                                                self.ident[:, :])
            last.then_inc(self.turned, 1)

    def bank(self, t, q):
        return self.banks[(2 * t + q) % len(self.banks)].rearrange("p (k c) -> p k c", k=4)

    def act_hi(self, act, t):
        for q in range(2):
            act.wait_ge(self.turned, 2 * t + q + 1)
            self.nc.scalar.copy(self.dest(t, q)[0], self.bank(t, q)).then_inc(self.hi_done, 1)

    def dve_lo(self, dve, t):
        for q in range(2):
            hi, lo = self.dest(t, q)
            dve.wait_ge(self.hi_done, 2 * t + q + 1)
            self.nc.vector.tensor_tensor(lo, self.bank(t, q), hi.bitcast(f32),
                                         ALU.subtract).then_inc(self.lo_done, 1)


class Kit:
    pass


def constants(nc, ctx, k):
    def sb(name, shape, dt=f32):
        return ctx.enter_context(nc.sbuf_tensor(name, shape, dt))

    k.ident = sb("ident", [P, P])
    k.ident_bf = sb("ident_bf", [P, P], bf16)
    k.eps = sb("eps", [P, 1])
    k.ps = ctx.enter_context(nc.psum_tensor("ps", [P, 8, N], f32))
    made = ctx.enter_context(nc.semaphore("consts_made"))
    with nc.Block() as block:
        @block.gpsimd
        def _(pool):
            nc.gpsimd.memset(k.ident[:, :], 0.0).then_inc(made, 1)
            nc.gpsimd.memset(k.eps[:, :], EPS).then_inc(made, 1)
            pool.wait_ge(made, 2)
            nc.gpsimd.affine_select(out=k.ident[:, :], in_=k.ident[:, :], compare_op=ALU.not_equal, fill=1.0,
                                    base=0, pattern=[[-1, P]], channel_multiplier=1).then_inc(made, 1)
            pool.wait_ge(made, 3)
            nc.gpsimd.tensor_copy(k.ident_bf[:, :], k.ident[:, :]).then_inc(made, 1)


def gain_row(ap):
    return ap[0, :].partition_broadcast(P)


def stage_projections(nc, k, x, g_mix, w_conv):
    with Stage(nc) as ctx:
        def sb(name, shape, dt=f32):
            return ctx.enter_context(nc.sbuf_tensor(name, shape, dt))

        def sem(name):
            return ctx.sem(name)

        SL = 2
        w_hi, w_lo = sb("p_whi", [P, SL, UNIT], f32r), sb("p_wlo", [P, SL, UNIT], f32r)
        acc = sb("conv_acc", [P, N])
        wc = sb("w_conv_t", [P, 3, 4])
        ps = k.ps
        mm_done, ev_act, ev_dve, conv_step, wc_in = (sem(s) for s in ("p_mm", "p_evac_act", "p_evac_dve",
                                                                       "conv_step", "wc_in"))
        x_in = [sem(f"p_x_in{i}") for i in range(2)]
        g_in = sem("p_g_in")
        xt = [k.y[:, 0, :], k.y[:, 1, :]]
        gain = k.y[:, 2, :]
        scratch = (k.y[:, 3, :], k.v[:, 0:4, :].rearrange("p (a b) c -> p a (b c)", a=2))

        def x_ready(eng, t):
            eng.wait_ge(x_in[t % 2], 16 * (t // 2 + 1))

        norm = RowNorm(nc, ctx, "p", lambda t: xt[t % 2], x_ready, gain, lambda e: e.wait_ge(g_in, 16),
                       k.ident, k.eps, [ps[:, b, :] for b in range(2)],
                       lambda t, q: (k.act_hi[:, 4 * q:4 * q + 4, t * P:(t + 1) * P],
                                     k.act_lo[:, 4 * q:4 * q + 4, t * P:(t + 1) * P]), scratch=scratch)

        kinds = ["u", "u", "c", "c", "b", "b", "q", "q", "k", "k", "v", "v"]
        groups = []
        for n, kind in enumerate(kinds):
            if kind == "v":
                groups += [(n, kind, n % 2, t) for t in range(TT)]
            else:
                halves = (1, 0) if kind == "b" else (0, 1)
                groups += [(n, kind, 2 * (n % 2) + m, th) for m in range(2) for th in halves]
        on_act = {"u", "q", "v"}
        count = {"act": 0, "dve": 0}
        done_at, index = [], {}
        for g, (n, kind, f, th) in enumerate(groups):
            e = "act" if kind in on_act else "dve"
            count[e] += 1
            done_at.append((e, count[e]))
            index[(kind, f, th)] = g
        unit_end = [max(g for g, x_ in enumerate(groups) if x_[0] == n) + 1 for n in range(12)]
        sem_of = {"act": ev_act, "dve": ev_dve}
        BK = 6

        def evacuated(eng, g):
            e, v = done_at[g]
            eng.wait_ge(sem_of[e], v)

        with nc.Block() as block:
            @block.sync
            def _(sp):
                sp.dma_start(gain, gain_row(g_mix)).then_inc(g_in, 16)
                for t in range(TT):
                    if t >= 2:
                        sp.wait_ge(norm.rows_done, t - 1)
                        sp.wait_ge(norm.sumsq_done, t - 1)
                    sp.dma_start(xt[t % 2], x[0, t * P:(t + 1) * P, :]).then_inc(x_in[t % 2], 16)
                    if t == 1:
                        for j in range(3):
                            with nc.allow_non_contiguous_dma(reason="512 taps a row, once"):
                                sp.dma_start(wc[:, j, :], w_conv[0, j, :].rearrange("(f p) -> p f", p=P)
                                             ).then_inc(wc_in, 16)
                        for n in range(RAW):
                            k.ring.load(sp, n)
                for n in range(RAW, 12 + RAW):
                    k.ring.load(sp, n)
                sp.wait_ge(wc_in, 48)

            @block.scalar
            def _(act):
                for t in range(TT + 1):
                    if t < TT:
                        norm.act_stats(act, t)
                    if t:
                        norm.act_hi(act, t - 1)
                for n in range(SL):
                    k.ring.hi(act, n, w_hi[:, n, :])
                g = 0
                for n in range(12):
                    while g < len(groups) and groups[g][0] == n:
                        _, kind, f, th = groups[g]
                        if kind in on_act:
                            act.wait_ge(mm_done, g + 1)
                            bank = ps[:, 2 + g % BK, :]
                            if kind == "u":
                                nc.scalar.copy(k.y[:, f, th * N:(th + 1) * N], bank).then_inc(ev_act, 1)
                            elif kind == "q":
                                nc.scalar.activation(k.q[:, f, th * N:(th + 1) * N], bank, ACT.Copy,
                                                     scale=HD ** -0.5).then_inc(ev_act, 1)
                            else:
                                nc.scalar.copy(k.v[:, th, f * 256:(f + 1) * 256], bank[:, 0:256]
                                               ).then_inc(ev_act, 1)
                        g += 1
                    if n + SL < 12:
                        act.wait_ge(mm_done, unit_end[n])
                        k.ring.hi(act, n + SL, w_hi[:, n % SL, :])

            @block.vector
            def _(dve):
                for t in range(TT + 1):
                    if t < TT:
                        norm.dve_rows(dve, t)
                    if t:
                        norm.dve_lo(dve, t - 1)
                for n in range(SL):
                    k.ring.lo(dve, n, w_hi[:, n, :], w_lo[:, n, :])
                dve.wait_ge(wc_in, 48)
                g = steps = 0
                for n in range(12):
                    while g < len(groups) and groups[g][0] == n:
                        _, kind, f, th = groups[g]
                        bank = ps[:, 2 + g % BK, :]
                        c0 = th * N
                        if kind == "c":
                            dve.wait_ge(mm_done, g + 1)
                            evacuated(dve, index[("u", f, th)])
                            here = k.y[:, f, c0:c0 + N]
                            nc.vector.tensor_tensor(here, bank, here, ALU.mult).then_inc(ev_dve, 1)
                        elif kind == "k":
                            dve.wait_ge(mm_done, g + 1)
                            nc.vector.tensor_copy(k.k[:, f, c0:c0 + N], bank).then_inc(ev_dve, 1)
                        elif kind == "b":
                            evacuated(dve, index[("c", f, 1)])
                            if steps:
                                dve.wait_ge(ev_dve, done_at[g - 1][1])
                            nc.vector.tensor_scalar(acc[:, :], k.y[:, f, c0:c0 + N], wc[:, 2, f:f + 1], None,
                                                    ALU.mult).then_inc(conv_step, 1)
                            for back in (1, 2):
                                dve.wait_ge(conv_step, steps + back)
                                o = back if th == 0 else 0
                                nc.vector.scalar_tensor_tensor(
                                    out=acc[:, o:N], in0=k.y[:, f, c0 + o - back:c0 + N - back],
                                    scalar=wc[:, 2 - back, f:f + 1], in1=acc[:, o:N], op0=ALU.mult,
                                    op1=ALU.add).then_inc(conv_step, 1)
                            steps += 3
                            dve.wait_ge(conv_step, steps)
                            dve.wait_ge(mm_done, g + 1)
                            nc.vector.tensor_tensor(k.y[:, f, c0:c0 + N], bank, acc[:, :], ALU.mult
                                                    ).then_inc(ev_dve, 1)
                        g += 1
                    if n + SL < 12:
                        k.ring.lo(dve, n + SL, w_hi[:, n % SL, :], w_lo[:, n % SL, :])

            @block.tensor
            def _(pe):
                for t in range(TT):
                    norm.pe_turn(pe, t)
                pe.wait_ge(norm.lo_done, 2 * TT)
                for g, (n, kind, f, th) in enumerate(groups):
                    if g == 0 or groups[g - 1][0] != n:
                        pe.wait_ge(k.ring.lo_done, n + 1)
                    if g >= BK:
                        evacuated(pe, g - BK)
                    wh = w_hi[:, n % SL, :].rearrange("p (k c) -> p k c", k=KT)
                    wl = w_lo[:, n % SL, :].rearrange("p (k c) -> p k c", k=KT)
                    for kk in range(KT):
                        if kind == "v":
                            out, tok = ps[:, 2 + g % BK, 0:256], slice(th * P, (th + 1) * P)
                            last = mm3(nc, out, k.act_hi[:, kk, tok], k.act_lo[:, kk, tok], wh[:, kk, :],
                                       wl[:, kk, :], kk == 0, kk == KT - 1)
                        else:
                            out, m = ps[:, 2 + g % BK, :], slice((f % 2) * P, (f % 2 + 1) * P)
                            tok = slice(th * N, (th + 1) * N)
                            last = mm3(nc, out, wh[:, kk, m], wl[:, kk, m], k.act_hi[:, kk, tok],
                                       k.act_lo[:, kk, tok], kk == 0, kk == KT - 1)
                    last.then_inc(mm_done, 1)


def stage_stick(nc, k):
    with Stage(nc) as ctx:
        def sb(name, shape, dt=f32):
            return ctx.enter_context(nc.sbuf_tensor(name, shape, dt))

        def sem(name):
            return ctx.sem(name)

        ps = k.ps
        E, L, S, A = (sb(f"stick_{s}", [P, 3, N]) for s in ("e", "l", "sp", "a"))
        later = sb("stick_later", [P, 2, 2, N])
        neg_tri, neg_ones = sb("neg_tri", [P, P]), sb("neg_ones", [P, P])
        mask = sb("mask_bf", [P, P], bf16)
        made, z_done, e_done, cap_done, l_done, sp_done, later_done, cum_done, a_done, av_done, o_done = (
            sem("stick_" + s) for s in ("made", "z", "e", "cap", "l", "sp", "later", "cum", "a", "av", "o"))
        steps = []
        for pair in range(4):
            for T in range(2):
                for j in range(4 * T + 3, -1, -1):
                    for h in range(2):
                        steps.append((pair, T, j, h, max(0, j * P - T * N), j == 4 * T + 3, j == 0))
        NS, ZB = len(steps), 5
        later_count, c = [], 0
        for s in steps:
            c += 0 if s[6] else (1 if s[5] or s[4] == 0 and s[2] * P - s[1] * N < 0 else 2)
            later_count.append(c)

        def z(n):
            return ps[:, n % ZB, :]

        def o_bank(n):
            return 5 + (steps[n][0] * 2 + steps[n][1]) % 2

        with nc.Block() as block:
            @block.gpsimd
            def _(pool):
                nc.gpsimd.memset(neg_ones[:, :], -1.0).then_inc(made, 1)
                nc.gpsimd.memset(mask[:, :], 0.0).then_inc(made, 1)
                pool.wait_ge(made, 2)
                nc.gpsimd.affine_select(out=neg_tri[:, :], in_=neg_ones[:, :], compare_op=ALU.is_ge, fill=0.0,
                                        base=0, pattern=[[-1, P]], channel_multiplier=1).then_inc(made, 1)
                nc.gpsimd.affine_select(out=mask[:, :], in_=mask[:, :], compare_op=ALU.is_ge, fill=-1e30,
                                        base=-1, pattern=[[1, P]], channel_multiplier=-1).then_inc(made, 1)
                for n, (pair, T, j, h, c0, first, final) in enumerate(steps):
                    if final:
                        continue
                    pool.wait_ge(sp_done, n + 1)
                    if n >= 4:
                        pool.wait_ge(cum_done, n - 1)
                    new, old = later[:, h, j % 2, :], later[:, h, (j + 1) % 2, :]
                    if first:
                        nc.gpsimd.tensor_copy(new[:, c0:N], S[:, n % 3, c0:N]).then_inc(later_done, 1)
                        continue
                    p0 = max(0, (j + 1) * P - T * N)
                    pool.wait_ge(later_done, later_count[n - 2])
                    nc.gpsimd.tensor_tensor(new[:, p0:N], old[:, p0:N], S[:, n % 3, p0:N], ALU.add
                                            ).then_inc(later_done, 1)
                    if p0 > c0:
                        nc.gpsimd.tensor_copy(new[:, c0:p0], S[:, n % 3, c0:p0]).then_inc(later_done, 1)

            @block.tensor
            def _(pe):
                pe.wait_ge(made, 4)
                for i in range(NS + 4):
                    if i < NS:
                        pair, T, j, h, c0, first, final = steps[i]
                        if i >= ZB:
                            pe.wait_ge(a_done, i - ZB + 1)
                        r = slice(64 * h, 64 * h + 64)
                        diag = j >= 4 * T
                        last = nc.tensor.matmul(z(i)[:, c0:N], k.k[r, pair, j * P:(j + 1) * P],
                                                k.q[r, pair, T * N + c0:(T + 1) * N], start=True, stop=True)
                        if diag:
                            last = nc.tensor.matmul(z(i)[:, c0:c0 + P], k.ident_bf[:, :], mask[:, :],
                                                    start=False, stop=True, skip_group_check=True)
                        last.then_inc(z_done, 1)
                    n = i - 3
                    if 0 <= n < NS:
                        pair, T, j, h, c0, first, final = steps[n]
                        pe.wait_ge(sp_done, n + 1)
                        last = nc.tensor.matmul(z(n)[:, c0:N], neg_tri[:, :], S[:, n % 3, c0:N], start=False,
                                                stop=True, skip_group_check=True)
                        if not first:
                            p0 = max(0, (j + 1) * P - T * N)
                            pe.wait_ge(later_done, later_count[n - 2])
                            last = nc.tensor.matmul(z(n)[:, p0:N], neg_ones[:, :], later[:, h, (j + 1) % 2, p0:N],
                                                    start=False, stop=True, skip_group_check=True)
                        last.then_inc(cum_done, 1)
                    n = i - 4
                    if 0 <= n < NS:
                        pair, T, j, h, c0, first, final = steps[n]
                        unit = pair * 2 + T
                        if first and unit >= 2:
                            pe.wait_ge(o_done, unit - 1)
                        pe.wait_ge(a_done, n + 1)
                        nc.tensor.matmul(ps[64 * h:64 * h + 64, o_bank(n), c0:N],
                                         k.v[:, j, (2 * pair + h) * HD:(2 * pair + h + 1) * HD],
                                         A[:, n % 3, c0:N], start=first, stop=final,
                                         skip_group_check=True).then_inc(av_done, 1)

            @block.scalar
            def _(act):
                nc.scalar.preload_act_table_set("natural_log_exp_and_others")
                for i in range(NS + 4):
                    if i < NS:
                        c0 = steps[i][4]
                        act.wait_ge(z_done, i + 1)
                        if i >= 3:
                            act.wait_ge(l_done, i - 2)
                        nc.scalar.activation(E[:, i % 3, c0:N], z(i)[:, c0:N], ACT.Exp).then_inc(e_done, 1)
                    n = i - 1
                    if 0 <= n < NS:
                        c0 = steps[n][4]
                        act.wait_ge(cap_done, n + 1)
                        if n >= 3:
                            act.wait_ge(sp_done, n - 2)
                        nc.scalar.activation(L[:, n % 3, c0:N], E[:, n % 3, c0:N], ACT.Ln, bias=1.0
                                             ).then_inc(l_done, 1)
                    n = i - 4
                    if 0 <= n < NS:
                        c0 = steps[n][4]
                        act.wait_ge(cum_done, n + 1)
                        if n >= 3:
                            act.wait_ge(av_done, n - 2)
                        nc.scalar.activation(A[:, n % 3, c0:N], z(n)[:, c0:N], ACT.Exp).then_inc(a_done, 1)

            @block.vector
            def _(dve):
                for i in range(NS + 6):
                    if i < NS:
                        c0 = steps[i][4]
                        dve.wait_ge(e_done, i + 1)
                        nc.vector.tensor_scalar(E[:, i % 3, c0:N], E[:, i % 3, c0:N], 2.0 ** 60, None, ALU.min
                                                ).then_inc(cap_done, 1)
                    n = i - 1
                    if 0 <= n < NS:
                        c0 = steps[n][4]
                        dve.wait_ge(l_done, n + 1)
                        if n >= 3:
                            dve.wait_ge(cum_done, n - 2)
                            dve.wait_ge(later_done, max(1, later_count[n - 3]))
                        nc.vector.tensor_tensor(S[:, n % 3, c0:N], z(n)[:, c0:N], L[:, n % 3, c0:N], ALU.max
                                                ).then_inc(sp_done, 1)
                    n = i - 6
                    if 0 <= n < NS and steps[n][6] and steps[n][3] == 1:
                        pair, T = steps[n][0:2]
                        dve.wait_ge(av_done, n + 1)
                        nc.vector.tensor_copy(k.o[:, pair, T * N:(T + 1) * N], ps[:, o_bank(n), :]
                                              ).then_inc(o_done, 1)


def stage_mixer_norms(nc, k, g_conv, g_sb):
    with Stage(nc) as ctx:
        def sb(name, shape, dt=f32):
            return ctx.enter_context(nc.sbuf_tensor(name, shape, dt))

        def sem(name):
            return ctx.sem(name)

        ps = k.ps
        ones, blk = sb("mn_ones", [P, P]), sb("mn_blocks", [P, P])
        sq = sb("mn_sq", [P, 2, N])
        root, inv = sb("mn_root", [P, 2, N]), sb("mn_inv", [P, 2, N])
        out = sb("mn_out", [P, 2, N])
        gt = sb("mn_gain", [P, 8])
        made, g_in, sq_done, ss_done, root_done, inv_done, out_done, hi_done, lo_done = (
            sem("mn_" + s) for s in ("made", "g_in", "sq", "ss", "root", "inv", "out", "hi", "lo"))
        jobs = []
        for th in range(2):
            jobs.append(([(k.y, f) for f in range(4)], th, ones, CW, 0))
        for pair in range(4):
            for th in range(2):
                jobs.append(([(k.o, pair)], th, blk, HD, 4 + pair))
        sq_at, out_at, a, b = [], [], 0, 0
        for tiles, *_ in jobs:
            sq_at.append(a)
            out_at.append(b)
            a += len(tiles)
            b += len(tiles)

        with nc.Block() as block:
            @block.sync
            def _(sp):
                with nc.allow_non_contiguous_dma(reason="1024 gains, once"):
                    sp.dma_start(gt[:, 0:4], g_conv[0, :].rearrange("(f p) -> p f", p=P)).then_inc(g_in, 16)
                    sp.dma_start(gt[:, 4:8], g_sb[0, :].rearrange("(f p) -> p f", p=P)).then_inc(g_in, 16)
                sp.wait_ge(g_in, 32)

            @block.gpsimd
            def _(pool):
                nc.gpsimd.memset(ones[:, :], 1.0).then_inc(made, 1)
                nc.gpsimd.memset(blk[:, :], 0.0).then_inc(made, 1)
                pool.wait_ge(made, 2)
                nc.gpsimd.memset(blk[0:64, 0:64], 1.0).then_inc(made, 1)
                nc.gpsimd.memset(blk[64:128, 64:128], 1.0).then_inc(made, 1)

            @block.scalar
            def _(act):
                def squares(ji):
                    tiles, th, _, _, _ = jobs[ji]
                    for m, (src, f) in enumerate(tiles):
                        n = sq_at[ji] + m
                        if n >= 2:
                            act.wait_ge(ss_done, n - 1)
                        nc.scalar.activation(sq[:, n % 2, :], src[:, f, th * N:(th + 1) * N], ACT.Square
                                             ).then_inc(sq_done, 1)

                def his(ji):
                    tiles, th, _, _, base = jobs[ji]
                    for m in range(len(tiles)):
                        n = out_at[ji] + m
                        act.wait_ge(out_done, n + 1)
                        nc.scalar.copy(k.act_hi[:, base + m, th * N:(th + 1) * N], out[:, n % 2, :]
                                       ).then_inc(hi_done, 1)

                squares(0)
                for ji, (tiles, th, _, width, _) in enumerate(jobs):
                    act.wait_ge(ss_done, sq_at[ji] + len(tiles))
                    if ji >= 2:
                        act.wait_ge(inv_done, ji - 1)
                    nc.scalar.activation(root[:, ji % 2, :], ps[:, ji % 2, :], ACT.Sqrt, scale=1.0 / width,
                                         bias=k.eps[:, 0:1]).then_inc(root_done, 1)
                    if ji + 1 < len(jobs):
                        squares(ji + 1)
                    his(ji)

            @block.tensor
            def _(pe):
                pe.wait_ge(made, 4)
                for ji, (tiles, th, mat, _, _) in enumerate(jobs):
                    if ji >= 2:
                        pe.wait_ge(root_done, ji - 1)
                    for m in range(len(tiles)):
                        n = sq_at[ji] + m
                        pe.wait_ge(sq_done, n + 1)
                        nc.tensor.matmul(ps[:, ji % 2, :], mat[:, :], sq[:, n % 2, :], start=(m == 0),
                                         stop=(m == len(tiles) - 1)).then_inc(ss_done, 1)

            @block.vector
            def _(dve):
                dve.wait_ge(g_in, 32)
                for ji, (tiles, th, _, _, base) in enumerate(jobs):
                    dve.wait_ge(root_done, ji + 1)
                    if ji >= 2:
                        dve.wait_ge(out_done, out_at[ji - 1])
                    nc.vector.reciprocal(inv[:, ji % 2, :], root[:, ji % 2, :]).then_inc(inv_done, 1)
                    dve.wait_ge(inv_done, ji + 1)
                    for m, (src, f) in enumerate(tiles):
                        n = out_at[ji] + m
                        if n >= 2:
                            dve.wait_ge(lo_done, n - 1)
                        nc.vector.scalar_tensor_tensor(
                            out=out[:, n % 2, :], in0=src[:, f, th * N:(th + 1) * N], scalar=gt[:, base + m:base + m + 1],
                            in1=inv[:, ji % 2, :], op0=ALU.mult, op1=ALU.mult).then_inc(out_done, 1)
                        cols = slice(th * N, (th + 1) * N)
                        dve.wait_ge(hi_done, n + 1)
                        nc.vector.tensor_tensor(k.act_lo[:, base + m, cols], out[:, n % 2, :],
                                                k.act_hi[:, base + m, cols].bitcast(f32), ALU.subtract
                                                ).then_inc(lo_done, 1)


def stage_memory(nc, k, mem, g_mem, first_unit):
    with Stage(nc) as ctx:
        def sb(name, shape, dt=f32):
            return ctx.enter_context(nc.sbuf_tensor(name, shape, dt))

        def sem(name):
            return ctx.sem(name)

        ps = k.ps
        SL = 2
        w_hi, w_lo = sb("m_whi", [P, SL, UNIT], f32r), sb("m_wlo", [P, SL, UNIT], f32r)
        m_hi, m_lo = sb("m_hi", [P, KT, MEM], f32r), sb("m_lo", [P, KT, MEM], f32r)
        xt, gain = sb("m_xt", [P, 2, D]), sb("m_gain", [P, D])
        x_in, g_in, mm_done, evac = (sem("m_" + s) for s in ("x_in", "g_in", "mm", "evac"))
        norm = RowNorm(nc, ctx, "m", lambda t: xt[:, t, :], lambda e, t: e.wait_ge(x_in, 32), gain[:, :],
                       lambda e: e.wait_ge(g_in, 16), k.ident, k.eps, [ps[:, b, :] for b in range(2)],
                       lambda t, q: (m_hi[:, 4 * q:4 * q + 4, t * P:(t + 1) * P],
                                     m_lo[:, 4 * q:4 * q + 4, t * P:(t + 1) * P]))
        BK = 6
        with nc.Block() as block:
            @block.sync
            def _(sp):
                sp.dma_start(gain[:, :], gain_row(g_mem)).then_inc(g_in, 16)
                for t in range(2):
                    sp.dma_start(xt[:, t, :], mem[0, t * P:(t + 1) * P, :]).then_inc(x_in, 16)
                for n in range(first_unit + RAW, first_unit + 8 + RAW):
                    k.ring.load(sp, n)

            @block.scalar
            def _(act):
                for t in range(3):
                    if t < 2:
                        norm.act_stats(act, t)
                    if t:
                        norm.act_hi(act, t - 1)
                for n in range(SL):
                    k.ring.hi(act, first_unit + n, w_hi[:, n, :])
                for n in range(8):
                    for m in range(2):
                        g = 2 * n + m
                        act.wait_ge(mm_done, g + 1)
                        bank = ps[:, 2 + g % BK, 0:256]
                        if n < 4:
                            nc.scalar.copy(k.mk[:, 2 * n + m, :], bank).then_inc(evac, 1)
                        else:
                            nc.scalar.copy(k.mv[:, m, (n - 4) * 256:(n - 3) * 256], bank).then_inc(evac, 1)
                    if n + SL < 8:
                        k.ring.hi(act, first_unit + n + SL, w_hi[:, n % SL, :])

            @block.vector
            def _(dve):
                for t in range(3):
                    if t < 2:
                        norm.dve_rows(dve, t)
                    if t:
                        norm.dve_lo(dve, t - 1)
                for n in range(8):
                    if n >= SL:
                        dve.wait_ge(mm_done, 2 * (n - SL) + 2)
                    k.ring.lo(dve, first_unit + n, w_hi[:, n % SL, :], w_lo[:, n % SL, :])

            @block.tensor
            def _(pe):
                for t in range(2):
                    norm.pe_turn(pe, t)
                pe.wait_ge(norm.lo_done, 4)
                for n in range(8):
                    pe.wait_ge(k.ring.lo_done, first_unit + n + 1)
                    wh = w_hi[:, n % SL, :].rearrange("p (k c) -> p k c", k=KT)
                    wl = w_lo[:, n % SL, :].rearrange("p (k c) -> p k c", k=KT)
                    for m in range(2):
                        g = 2 * n + m
                        if g >= BK:
                            pe.wait_ge(evac, g - BK + 1)
                        out, c = ps[:, 2 + g % BK, 0:256], slice(m * P, (m + 1) * P)
                        for kk in range(KT):
                            if n < 4:
                                last = mm3(nc, out, wh[:, kk, c], wl[:, kk, c], m_hi[:, kk, :], m_lo[:, kk, :],
                                           kk == 0, kk == KT - 1)
                            else:
                                last = mm3(nc, out, m_hi[:, kk, c], m_lo[:, kk, c], wh[:, kk, :], wl[:, kk, :],
                                           kk == 0, kk == KT - 1)
                        last.then_inc(mm_done, 1)


def stage_residual(nc, k, name, x_from, x_to, gain_ap, first_unit, router=None):
    with Stage(nc) as ctx:
        def sb(nm, shape, dt=f32):
            return ctx.enter_context(nc.sbuf_tensor(f"{name}_{nm}", shape, dt))

        def sem(nm):
            return ctx.sem(f"{name}_{nm}")

        ps = k.ps
        w_hi, w_lo = sb("whi", [P, 4, UNIT], f32r), sb("wlo", [P, 4, UNIT], f32r)
        xt, gain = sb("xt", [P, 2, D]), sb("gain", [P, D])
        g_in, mm_done, sum_done = sem("g_in"), sem("mm"), sem("sum")
        x_in = [sem(f"x_in{i}") for i in range(2)]
        stored = [sem(f"stored{i}") for i in range(2)]
        rows_stored = [sem(f"rows_stored{i}") for i in range(2)]
        if router is not None:
            w_router, b_router = router
            ht = sb("ht", [P, 2, KT, P])
            wr, br = sb("wr", [P, KT, NE]), sb("br", [P, NE])
            r_in, turned_out, logit_done, bias_done = sem("r_in"), sem("turned_out"), sem("logit"), sem("biased")

        def summed(eng, t):
            eng.wait_ge(sum_done, 2 * t + 2)

        norm = RowNorm(nc, ctx, name, lambda t: xt[:, t % 2, :], summed, gain[:, :],
                       lambda e: e.wait_ge(g_in, 16), k.ident, k.eps, [ps[:, b, :] for b in range(2)],
                       lambda t, q: (k.act_hi[:, 4 * q:4 * q + 4, t * P:(t + 1) * P],
                                     k.act_lo[:, 4 * q:4 * q + 4, t * P:(t + 1) * P]),
                       hn_free=None if router is None else
                       (lambda e, t: e.wait_ge(rows_stored[t % 2], 16 * (t // 2 + 1))))

        with nc.Block() as block:
            @block.sync
            def _(sp):
                sp.dma_start(gain[:, :], gain_row(gain_ap)).then_inc(g_in, 16)
                if router is not None:
                    sp.dma_start(wr[:, :, :], w_router[0].rearrange("(k p) n -> p k n", p=P)).then_inc(r_in, 16)
                    sp.dma_start(br[:, :], b_router[0, :].partition_broadcast(P)).then_inc(r_in, 16)
                for t in range(2):
                    sp.dma_start(xt[:, t, :], x_from[t * P:(t + 1) * P, :]).then_inc(x_in[t], 16)
                for n in range(first_unit + RAW, first_unit + 4 + RAW):
                    k.ring.load(sp, n)
                for t in range(TT):
                    summed(sp, t)
                    sp.dma_start(x_to[t * P:(t + 1) * P, :], xt[:, t % 2, :]).then_inc(stored[t % 2], 16)
                    sp.wait_ge(norm.rows_done, t + 1)
                    if router is not None:
                        sp.dma_start(k.h_rows[t * P:(t + 1) * P, :], norm.hn[:, t % 2, :]
                                     ).then_inc(rows_stored[t % 2], 16)
                    if t + 2 < TT:
                        sp.wait_ge(norm.sumsq_done, t + 1)
                        sp.wait_ge(stored[t % 2], 16 * (t // 2 + 1))
                        sp.dma_start(xt[:, t % 2, :], x_from[(t + 2) * P:(t + 3) * P, :]
                                     ).then_inc(x_in[t % 2], 16)
                for b in range(2):
                    sp.wait_ge(stored[b], 16 * (TT // 2))
                    if router is not None:
                        sp.wait_ge(rows_stored[b], 16 * (TT // 2))

            @block.scalar
            def _(act):
                for n in range(4):
                    k.ring.hi(act, first_unit + n, w_hi[:, n, :])
                for t in range(TT + 1):
                    if t < TT:
                        norm.act_stats(act, t)
                    if t and router is None:
                        norm.act_hi(act, t - 1)
                    elif t:
                        for q in range(2):
                            act.wait_ge(norm.turned, 2 * (t - 1) + q + 1)
                            if t >= 3:
                                act.wait_ge(logit_done, t - 2)
                            nc.scalar.copy(ht[:, (t - 1) % 2, 4 * q:4 * q + 4, :], norm.bank(t - 1, q)
                                           ).then_inc(norm.lo_done, 1)

            @block.vector
            def _(dve):
                for n in range(4):
                    k.ring.lo(dve, first_unit + n, w_hi[:, n, :], w_lo[:, n, :])
                for t in range(TT + 1):
                    if t < TT:
                        dve.wait_ge(x_in[t % 2], 16 * (t // 2 + 1))
                        for nh in range(2):
                            g = 2 * t + nh
                            dve.wait_ge(mm_done, g + 1)
                            half = xt[:, t % 2, nh * N:(nh + 1) * N]
                            nc.vector.tensor_tensor(half, ps[:, 2 + g % 4, :], half, ALU.add
                                                    ).then_inc(sum_done, 1)
                        norm.dve_rows(dve, t)
                    if t and router is None:
                        norm.dve_lo(dve, t - 1)
                if router is not None:
                    dve.wait_ge(r_in, 32)
                    dve.wait_ge(logit_done, TT)
                    nc.vector.tensor_tensor(
                        k.logits[:, :, :], ps[:, 6, 0:TT * NE].rearrange("p (t e) -> p t e", e=NE),
                        br[:, :].unsqueeze(1).broadcast_to((P, TT, NE)), ALU.add).then_inc(bias_done, 1)

            @block.tensor
            def _(pe):
                pe.wait_ge(k.ring.lo_done, first_unit + 4)
                for t in range(TT + 2):
                    if t < TT:
                        tok = slice(t * P, (t + 1) * P)
                        for nh in range(2):
                            g = 2 * t + nh
                            if g >= 4:
                                pe.wait_ge(sum_done, g - 3)
                            for kk in range(KT):
                                u = 2 * nh + kk // 4
                                c = slice((kk % 4) * N, (kk % 4 + 1) * N)
                                last = mm3(nc, ps[:, 2 + g % 4, :], k.act_hi[:, kk, tok], k.act_lo[:, kk, tok],
                                           w_hi[:, u, c], w_lo[:, u, c], kk == 0, kk == KT - 1)
                            last.then_inc(mm_done, 1)
                    if 1 <= t <= TT:
                        norm.pe_turn(pe, t - 1)
                    if router is not None and t >= 2:
                        if t == 2:
                            pe.wait_ge(r_in, 32)
                        pe.wait_ge(norm.lo_done, 2 * (t - 1))
                        for kk in range(KT):
                            last = nc.tensor.matmul(ps[:, 6, (t - 2) * NE:(t - 1) * NE], ht[:, (t - 2) % 2, kk, :],
                                                    wr[:, kk, :], start=(kk == 0), stop=(kk == KT - 1))
                        last.then_inc(logit_done, 1)


def stage_cross(nc, k, first_unit):
    with Stage(nc) as ctx:
        def sb(nm, shape, dt=f32):
            return ctx.enter_context(nc.sbuf_tensor(f"x_{nm}", shape, dt))

        def sem(nm):
            return ctx.sem(f"x_{nm}")

        ps = k.ps
        SL, BK = 2, 4
        w_hi, w_lo = sb("whi", [P, SL, UNIT], f32r), sb("wlo", [P, SL, UNIT], f32r)
        qt = sb("qt", [P, KT, SEQ])
        p = sb("p", [P, 2, MEM])
        pt = sb("pt", [P, 2, 2, N])
        st = sb("st", [P, 4, XH * TT])
        mm_done, evac, sc_done, max_done, nm_done, exp_done, inv_done, p_done, turned, pt_done, o_done, \
            hi_done, lo_done = (sem(s) for s in ("mm", "evac", "sc", "max", "nm", "exp", "inv", "p", "turned",
                                                 "pt", "o", "hi", "lo"))
        steps = [(h, t) for h in range(XH) for t in range(TT)]
        NSX = len(steps)
        scale = XD ** -0.5

        with nc.Block() as block:
            @block.sync
            def _(sp):
                for n in range(first_unit + RAW, first_unit + 4 + RAW):
                    k.ring.load(sp, n)

            @block.scalar
            def _(act):
                for n in range(SL):
                    k.ring.hi(act, first_unit + n, w_hi[:, n, :])
                for n in range(4):
                    for m in range(4):
                        g = 4 * n + m
                        act.wait_ge(mm_done, g + 1)
                        nc.scalar.copy(qt[:, 2 * n + m // 2, (m % 2) * N:(m % 2 + 1) * N], ps[:, g % BK, :]
                                       ).then_inc(evac, 1)
                    if n + SL < 4:
                        k.ring.hi(act, first_unit + n + SL, w_hi[:, n % SL, :])
                for i in range(NSX + 2):
                    if i < NSX:
                        act.wait_ge(nm_done, i + 1)
                        if i >= 2:
                            act.wait_ge(turned, i - 1)
                        nc.scalar.activation(p[:, i % 2, :], ps[:, 4 + i % 2, 0:MEM], ACT.Exp, scale=scale,
                                             bias=st[:, 1, i:i + 1], accum_out=st[:, 2, i:i + 1]
                                             ).then_inc(exp_done, 1)
                    n = i - 1
                    if 0 <= n < NSX:
                        h, t = steps[n]
                        u = n // 4
                        act.wait_ge(turned, n + 1)
                        if u >= 2:
                            act.wait_ge(o_done, 2 * (u - 1))
                        nc.scalar.copy(pt[:, u % 2, :, (t % 4) * P:(t % 4 + 1) * P],
                                       ps[:, 6 + n % 2, 0:MEM].rearrange("p (m c) -> p m c", m=2)
                                       ).then_inc(pt_done, 1)
                    n = i - 2
                    if 0 <= n < NSX and n % 4 == 3:
                        u = n // 4
                        h, th = u // 2, u % 2
                        for d in range(2):
                            g = 2 * u + d
                            act.wait_ge(o_done, g + 1)
                            nc.scalar.copy(k.act_hi[:, 2 * h + d, th * N:(th + 1) * N], ps[:, g % 4, :]
                                           ).then_inc(hi_done, 1)

            @block.vector
            def _(dve):
                for n in range(4):
                    if n >= SL:
                        dve.wait_ge(mm_done, 4 * (n - SL + 1))
                    k.ring.lo(dve, first_unit + n, w_hi[:, n % SL, :], w_lo[:, n % SL, :])
                for i in range(NSX + 2):
                    if i < NSX:
                        dve.wait_ge(sc_done, i + 1)
                        nc.vector.reduce_max(st[:, 0, i:i + 1], ps[:, 4 + i % 2, 0:MEM], AX).then_inc(max_done, 1)
                        dve.wait_ge(max_done, i + 1)
                        nc.vector.tensor_scalar(st[:, 1, i:i + 1], st[:, 0, i:i + 1], -scale, None, ALU.mult
                                                ).then_inc(nm_done, 1)
                        dve.wait_ge(exp_done, i + 1)
                        nc.vector.reciprocal(st[:, 3, i:i + 1], st[:, 2, i:i + 1]).then_inc(inv_done, 1)
                        dve.wait_ge(inv_done, i + 1)
                        nc.vector.tensor_scalar(p[:, i % 2, :], p[:, i % 2, :], st[:, 3, i:i + 1], None, ALU.mult
                                                ).then_inc(p_done, 1)
                    n = i - 2
                    if 0 <= n < NSX and n % 4 == 3:
                        u = n // 4
                        h, th = u // 2, u % 2
                        for d in range(2):
                            g = 2 * u + d
                            c = slice(th * N, (th + 1) * N)
                            dve.wait_ge(hi_done, g + 1)
                            nc.vector.tensor_tensor(k.act_lo[:, 2 * h + d, c], ps[:, g % 4, :],
                                                    k.act_hi[:, 2 * h + d, c].bitcast(f32), ALU.subtract
                                                    ).then_inc(lo_done, 1)

            @block.tensor
            def _(pe):
                for n in range(4):
                    pe.wait_ge(k.ring.lo_done, first_unit + n + 1)
                    wh = w_hi[:, n % SL, :].rearrange("p (k c) -> p k c", k=KT)
                    wl = w_lo[:, n % SL, :].rearrange("p (k c) -> p k c", k=KT)
                    for m in range(4):
                        g = 4 * n + m
                        if g >= BK:
                            pe.wait_ge(evac, g - BK + 1)
                        c, tok = slice((m // 2) * P, (m // 2 + 1) * P), slice((m % 2) * N, (m % 2 + 1) * N)
                        for kk in range(KT):
                            last = mm3(nc, ps[:, g % BK, :], wh[:, kk, c], wl[:, kk, c], k.act_hi[:, kk, tok],
                                       k.act_lo[:, kk, tok], kk == 0, kk == KT - 1)
                        last.then_inc(mm_done, 1)
                pe.wait_ge(evac, 16)
                for i in range(NSX + 2):
                    if i < NSX:
                        h, t = steps[i]
                        if i >= 2:
                            pe.wait_ge(exp_done, i - 1)
                        for d in range(2):
                            last = nc.tensor.matmul(ps[:, 4 + i % 2, 0:MEM], qt[:, 2 * h + d, t * P:(t + 1) * P],
                                                    k.mk[:, 2 * h + d, :], start=(d == 0), stop=(d == 1))
                        last.then_inc(sc_done, 1)
                    n = i - 1
                    if 0 <= n < NSX:
                        pe.wait_ge(p_done, n + 1)
                        if n >= 2:
                            pe.wait_ge(pt_done, n - 1)
                        for m in range(2):
                            last = nc.tensor.transpose(ps[:, 6 + n % 2, m * P:(m + 1) * P],
                                                       p[:, n % 2, m * P:(m + 1) * P], k.ident[:, :])
                        last.then_inc(turned, 1)
                    n = i - 2
                    if 0 <= n < NSX and n % 4 == 3:
                        u = n // 4
                        h = u // 2
                        pe.wait_ge(pt_done, n + 1)
                        for d in range(2):
                            g = 2 * u + d
                            if g >= 4:
                                pe.wait_ge(lo_done, g - 3)
                            for m in range(2):
                                last = nc.tensor.matmul(ps[:, g % 4, :],
                                                        k.mv[:, m, h * XD + d * P:h * XD + (d + 1) * P],
                                                        pt[:, u % 2, m, :], start=(m == 0), stop=(m == 1))
                            last.then_inc(o_done, 1)


def stage_routing(nc, k):
    with Stage(nc) as ctx:
        def sb(nm, shape, dt=f32):
            return ctx.enter_context(nc.sbuf_tensor(f"r_{nm}", shape, dt))

        def sem(nm):
            return ctx.sem(f"r_{nm}")

        ps = k.ps
        Q = TT * TOPK
        best, besti = sb("best", [P, TT, 8]), sb("besti", [P, TT, 8], u32)
        idf, rel, ex = sb("idf", [P, TT, TOPK]), sb("rel", [P, TT, TOPK]), sb("ex", [P, TT, TOPK])
        tot, inv = sb("tot", [P, TT]), sb("inv", [P, TT])
        count_row = sb("count_row", [P, P])
        part = sb("part", [P, 1])
        mult_row = sb("mult_row", [P, 8])
        tokid = sb("tokid", [P, TT])
        hot = sb("hot", [P, TT, TOPK, NE])
        pick = sb("pick", [P, TT, TOPK, NE])
        member = sb("member", [P, TT, NE])
        upper, ones = sb("upper", [P, P]), sb("ones", [P, P])
        base = sb("base", [P, TT + 1, NE])
        pos = sb("pos", [P, TT, NE])
        cmp8 = sb("cmp8", [P, NE, 8])
        one32 = sb("one32", [P, NE])
        nblk, nitem, end_b, end_i, start_b, start_i = (sb(s, [P, NE]) for s in
                                                       ("nblk", "nitem", "end_b", "end_i", "start_b", "start_i"))
        posj, startj, pb, off, blk, slotf = (sb(s, [P, Q]) for s in ("posj", "startj", "pb", "off", "blk", "slotf"))
        cmpq = sb("cmpq", [P, Q, 8])
        in_blk = sb("in_blk", [P, Q, 64])
        in_off = sb("in_off", [P, Q, P])
        cmpe = sb("cmpe", [P, NE])
        ie, ie3 = sb("ie", [P, 1]), sb("ie3", [P, 3, NE])
        t32 = sb("t32", [P, NE])
        fields = sb("fields", [P, 8])
        si, bi, ni, ji, left = (sb(s, [P, 1]) for s in ("si", "bi", "ni", "ji", "left"))
        fi = sb("fi", [P, 8], i32)
        v, made, ex_done, mm_done, table_io = sem("v"), sem("made"), sem("ex"), sem("mm"), sem("table_io")
        marks = {}

        def bc(ap, shape, *dims):
            for d in dims:
                ap = ap.unsqueeze(d)
            return ap.broadcast_to(shape)

        with nc.Block() as block:
            @block.gpsimd
            def _(pool):
                nc.gpsimd.iota(count_row[:, :], [[1, P]], base=0, channel_multiplier=0,
                               allow_small_or_imprecise_dtypes=True).then_inc(made, 1)
                nc.gpsimd.iota(part[:, :], [[0, 1]], base=0, channel_multiplier=1,
                               allow_small_or_imprecise_dtypes=True).then_inc(made, 1)
                nc.gpsimd.iota(mult_row[:, :], [[P, 8]], base=0, channel_multiplier=0,
                               allow_small_or_imprecise_dtypes=True).then_inc(made, 1)
                nc.gpsimd.iota(tokid[:, :], [[P, TT]], base=0, channel_multiplier=1,
                               allow_small_or_imprecise_dtypes=True).then_inc(made, 1)
                nc.gpsimd.memset(ones[:, :], 1.0).then_inc(made, 1)
                nc.gpsimd.memset(one32[:, :], 1.0).then_inc(made, 1)
                pool.wait_ge(made, 6)
                nc.gpsimd.affine_select(out=upper[:, :], in_=ones[:, :], compare_op=ALU.is_ge, fill=0.0, base=-1,
                                        pattern=[[1, P]], channel_multiplier=-1).then_inc(made, 1)

            @block.vector
            def _(dve):
                n = [0]

                def step(ins, mark=None):
                    n[0] += 1
                    ins.then_inc(v, 1)
                    dve.wait_ge(v, n[0])
                    if mark:
                        marks[mark] = n[0]

                V = nc.vector
                step(V.memset(fields[:, :], 0.0))
                for t in range(TT):
                    step(V.max(best[:, t, :], k.logits[:, t, :]))
                    step(V.max_index(besti[:, t, :], best[:, t, :], k.logits[:, t, :]))
                step(V.tensor_tensor(rel[:, :, :], best[:, :, 0:TOPK],
                                     best[:, :, 0:1].broadcast_to((P, TT, TOPK)), ALU.subtract), "rel")
                step(V.tensor_copy(idf[:, :, :], besti[:, :, 0:TOPK]))
                dve.wait_ge(made, 7)
                step(V.tensor_tensor(hot[:, :, :, :].rearrange("p t j e -> p (t j) e"),
                                     bc(count_row[:, 0:NE], (P, Q, NE), 1),
                                     bc(idf[:, :, :].rearrange("p t j -> p (t j)"), (P, Q, NE), 2), ALU.is_equal))
                step(V.tensor_tensor(member[:, :, :], hot[:, :, 0, :], hot[:, :, 1, :], ALU.add))
                for j in range(2, TOPK):
                    step(V.tensor_tensor(member[:, :, :], member[:, :, :], hot[:, :, j, :], ALU.add))
                marks["member"] = n[0]
                dve.wait_ge(ex_done, 1)
                step(V.tensor_reduce(tot[:, :], ex[:, :, :], AX, ALU.add))
                step(V.reciprocal(inv[:, :], tot[:, :]))
                step(V.tensor_tensor(k.gates[:, :, :], ex[:, :, :], bc(inv[:, :], (P, TT, TOPK), 2), ALU.mult))
                dve.wait_ge(mm_done, 2)
                total = ps[:, 1, 0:TT * NE].rearrange("p (t e) -> p t e", e=NE)
                before = ps[:, 0, 0:TT * NE].rearrange("p (t e) -> p t e", e=NE)
                step(V.memset(base[:, 0, :], 0.0))
                for t in range(TT):
                    step(V.tensor_tensor(base[:, t + 1, :], base[:, t, :], total[:, t, :], ALU.add))
                step(V.tensor_tensor(pos[:, :, :], before, base[:, 0:TT, :], ALU.add))
                counts = base[:, TT, :]
                step(V.tensor_tensor(cmp8[:, :, :], bc(counts, (P, NE, 8), 2), bc(mult_row[:, :], (P, NE, 8), 1),
                                     ALU.is_gt))
                step(V.tensor_reduce(nblk[:, :], cmp8[:, :, :], AX, ALU.add))
                step(V.tensor_reduce(nitem[:, :], cmp8[:, :, 0:8:2], AX, ALU.add))
                step(V.tensor_tensor_scan(end_b[:, :], one32[:, :], nblk[:, :], 0.0, ALU.mult, ALU.add))
                step(V.tensor_tensor_scan(end_i[:, :], one32[:, :], nitem[:, :], 0.0, ALU.mult, ALU.add))
                step(V.tensor_tensor(start_b[:, :], end_b[:, :], nblk[:, :], ALU.subtract))
                step(V.tensor_tensor(start_i[:, :], end_i[:, :], nitem[:, :], ALU.subtract))
                pk = pick[:, :, :, :]
                pk3 = pk.rearrange("p t j e -> p (t j) e")
                for j in range(TOPK):
                    step(V.tensor_tensor(pick[:, :, j, :], hot[:, :, j, :], pos[:, :, :], ALU.mult))
                step(V.tensor_reduce(posj[:, :], pk3, AX, ALU.add))
                step(V.tensor_tensor(pk3, hot[:, :, :, :].rearrange("p t j e -> p (t j) e"),
                                     bc(start_b[:, :], (P, Q, NE), 1), ALU.mult))
                step(V.tensor_reduce(startj[:, :], pk3, AX, ALU.add))
                step(V.tensor_tensor(cmpq[:, :, :], bc(posj[:, :], (P, Q, 8), 2), bc(mult_row[:, :], (P, Q, 8), 1),
                                     ALU.is_ge))
                step(V.tensor_reduce(pb[:, :], cmpq[:, :, :], AX, ALU.add))
                step(V.tensor_scalar(pb[:, :], pb[:, :], -1.0, None, ALU.add))
                step(V.scalar_tensor_tensor(out=off[:, :], in0=pb[:, :], scalar=-float(P), in1=posj[:, :],
                                            op0=ALU.mult, op1=ALU.add))
                step(V.tensor_tensor(blk[:, :], pb[:, :], startj[:, :], ALU.add))
                step(V.scalar_tensor_tensor(out=slotf[:, :], in0=blk[:, :], scalar=float(P), in1=off[:, :],
                                            op0=ALU.mult, op1=ALU.add))
                step(V.tensor_copy(k.slots[:, :], slotf[:, :]))
                step(V.tensor_tensor(in_off[:, :, :], bc(count_row[:, :], (P, Q, P), 1), bc(off[:, :], (P, Q, P), 2),
                                     ALU.is_equal))
                step(V.tensor_tensor(in_blk[:, :, :], bc(count_row[:, 0:64], (P, Q, 64), 1),
                                     bc(blk[:, :], (P, Q, 64), 2), ALU.is_equal))
                blk_by_tile = in_blk[:, :, :].rearrange("p (t j) b -> p t (j b)", j=TOPK)
                step(V.tensor_tensor(blk_by_tile, blk_by_tile, bc(tokid[:, :], (P, TT, TOPK * 64), 2), ALU.mult),
                     "in_blk")
                step(V.tensor_scalar(cmpe[:, :], end_i[:, :], part[:, 0:1], None, ALU.is_le))
                step(V.tensor_reduce(ie[:, :], cmpe[:, :], AX, ALU.add))
                step(V.tensor_tensor(ie3[:, :, :], bc(count_row[:, 0:NE], (P, 3, NE), 1),
                                     bc(ie[:, 0:1], (P, 3, NE), 2), ALU.is_equal), "ie3")
                for row, got in ((start_i, si), (start_b, bi), (nblk, ni)):
                    step(V.tensor_tensor(t32[:, :], ie3[:, 0, :], row[:, :], ALU.mult))
                    step(V.tensor_reduce(got[:, :], t32[:, :], AX, ALU.add))
                step(V.tensor_tensor(ji[:, :], part[:, :], si[:, :], ALU.subtract))
                step(V.scalar_tensor_tensor(out=left[:, :], in0=ji[:, :], scalar=-2.0, in1=ni[:, :], op0=ALU.mult,
                                            op1=ALU.add))
                step(V.tensor_scalar(fields[:, 0:1], ie[:, :], float(NE - 1), None, ALU.min))
                step(V.tensor_scalar(fields[:, 1:2], left[:, :], 2.0, None, ALU.is_ge))
                step(V.scalar_tensor_tensor(out=fields[:, 2:3], in0=ji[:, :], scalar=2.0, in1=bi[:, :], op0=ALU.mult,
                                            op1=ALU.add))
                step(V.tensor_scalar(t32[:, 0:1], ie[:, :], float(NE), None, ALU.is_lt))
                step(V.tensor_tensor(fields[:, 2:3], fields[:, 2:3], t32[:, 0:1], ALU.mult))
                step(V.tensor_scalar(t32[:, 0:1], fields[:, 2:3], 1.0 - (NBLK - 1), None, ALU.add))
                step(V.tensor_tensor(t32[:, 0:1], t32[:, 0:1], fields[:, 1:2], ALU.mult))
                step(V.tensor_scalar(fields[:, 3:4], t32[:, 0:1], float(NBLK - 1), None, ALU.add))
                step(V.tensor_copy(fields[:, 4:5], end_i[:, NE - 1:NE]))
                step(V.tensor_scalar(fields[:, 5:6], end_b[:, NE - 1:NE], -1.0, float(USED), ALU.mult, ALU.add))
                step(V.tensor_copy(fi[:, :], fields[:, :]), "fields")
                dve.wait_ge(mm_done, 3)
                step(V.memset(k.rows[:, USED:NBLK + 1], 0))
                step(V.tensor_copy(k.rows[:, 0:USED], ps[:, 2, 0:USED]))
                dve.wait_ge(mm_done, 4)
                step(V.tensor_copy(k.sel[:, :], ps[0:3 * NE, 3, 0:P]))

            @block.tensor
            def _(pe):
                pe.wait_ge(made, 7)
                pe.wait_ge(v, marks["member"])
                m = member[:, :, :].rearrange("p t e -> p (t e)")
                nc.tensor.matmul(ps[:, 0, 0:TT * NE], upper[:, :], m, start=True, stop=True).then_inc(mm_done, 1)
                nc.tensor.matmul(ps[:, 1, 0:TT * NE], ones[:, :], m, start=True, stop=True).then_inc(mm_done, 1)
                pe.wait_ge(v, marks["in_blk"])
                for q in range(Q):
                    last = nc.tensor.matmul(ps[:, 2, 0:64], in_off[:, q, :], in_blk[:, q, :], start=(q == 0),
                                            stop=(q == Q - 1))
                last.then_inc(mm_done, 1)
                pe.wait_ge(v, marks["ie3"])
                nc.tensor.transpose(ps[0:3 * NE, 3, 0:P], ie3[:, :, :].rearrange("p a e -> p (a e)"), k.ident[:, :]
                                    ).then_inc(mm_done, 1)

            @block.scalar
            def _(act):
                act.wait_ge(v, marks["rel"])
                nc.scalar.activation(ex[:, :, :], rel[:, :, :], ACT.Exp).then_inc(ex_done, 1)

            @block.sync
            def _(sp):
                sp.wait_ge(v, marks["fields"])
                sp.dma_start(k.table_dram, fi[:, :]).then_inc(table_io, 16)
                sp.wait_ge(table_io, 16)
                sp.dma_start(k.table[0:1, :], k.table_dram.rearrange("(o i) f -> o (i f)", o=1)).then_inc(table_io, 16)
                sp.wait_ge(table_io, 32)


def split_biases(nc, bias, b_gate_up, b_down):
    with Stage(nc) as ctx:
        def sb(nm, dt):
            return ctx.enter_context(nc.sbuf_tensor(f"b_{nm}", [NE, 3 * D], dt))

        left, part = sb("left", f32), sb("part", bf16)
        b_in, step = (ctx.sem(f"b_{s}") for s in ("in", "step"))
        with nc.Block() as block:
            @block.sync
            def _(sp):
                sp.dma_start(left[:, 0:2 * D], b_gate_up[0]).then_inc(b_in, 16)
                sp.dma_start(left[:, 2 * D:3 * D], b_down[0]).then_inc(b_in, 16)

            @block.vector
            def _(dve):
                dve.wait_ge(b_in, 32)
                for p in range(3):
                    if p:
                        dve.wait_ge(step, 3 * p)
                    nc.vector.tensor_copy(part[:, :], left[:, :]).then_inc(step, 1)
                    dve.wait_ge(step, 3 * p + 1)
                    nc.vector.tensor_copy(bias[NE * p:NE * (p + 1), :], part[:, :]).then_inc(step, 1)
                    nc.vector.tensor_tensor(left[:, :], left[:, :], part[:, :], ALU.subtract).then_inc(step, 1)


E_FIELD, TWO_FIELD, B0_FIELD, B1_FIELD, N_FIELD, REST_FIELD = range(6)


def stage_experts(nc, k, w_gate_up, b_gate_up, w_down, b_down):
    with Stage(nc) as ctx:
        def sb(nm, shape, dt=f32):
            return ctx.enter_context(nc.sbuf_tensor(f"e_{nm}", shape, dt))

        def sem(nm):
            return ctx.sem(f"e_{nm}")

        ps = k.ps
        NR, NS, NU = RAW, 6, 12
        bias = sb("bias", [3 * NE, 3 * D], bf16)
        split_biases(nc, bias, b_gate_up, b_down)
        w_hi, w_lo = sb("whi", [P, NS, UNIT], f32r), sb("wlo", [P, NS, UNIT], f32r)
        x_hi, x_lo = sb("xhi", [P, KT, 2, P], f32r), sb("xlo", [P, KT, 2, P], f32r)
        a_hi, a_lo = sb("ahi", [P, KT, 2, P], f32r), sb("alo", [P, KT, 2, P], f32r)
        xg = sb("xg", [P, 2, D])
        ridx = sb("ridx", [P, 2], i32)
        y = sb("y", [P, 2, D])
        gt, up, sg = sb("gt", [P, 2, 2, 256]), sb("up", [P, 2, 2, 256]), sb("sg", [P, 2, 2, 256])
        sel = sb("sel", [3 * NE, P], bf16)

        zero = sb("zero", [P, D])
        zeroed, zero_made = sem("zeroed"), sem("zero_made")
        sp_passed, act_passed, pool_passed = sem("sp_passed"), sem("act_passed"), sem("pool_passed")
        w_in = [sem(f"w_in{s}") for s in range(NR)]
        hi_done, lo_done, chunk_done, up_free, y_free = (sem(s) for s in ("w_hi", "w_lo", "chunk", "up_free", "y_free"))
        g_done, u_done, sg_done, t_done, a_done = (sem(s) for s in ("gate", "up", "sigmoid", "prod", "act"))
        at_turned, at_hi, at_lo = sem("at_turned"), sem("at_hi"), sem("at_lo")
        x_in, ridx_done, xt_turned, xt_hi, xt_lo = (sem(s) for s in ("x_in", "ridx", "xt_turned", "xt_hi", "xt_lo"))
        y_done, sel_done = sem("y"), sem("sel")
        y_stored = sem("y_stored")

        def raw(u):
            return k.ring.raw[:, u % NR, :]

        def field(eng, i, f, top):
            return eng.value_load(k.table[0:1, bass.ds(i * 8 + f, 1)], min_val=0, max_val=top)

        def weights(e, u):
            h = u % 2
            w = w_gate_up[0, bass.ds(e, 1)] if u < 8 else w_down[0, bass.ds(e, 1)]
            c = (u // 2) if u < 8 else (u - 8) // 2
            return w.rearrange("o (k p) n -> (o p) k n", p=P)[:, 4 * h:4 * h + 4, c * N:(c + 1) * N]

        def load(sp, e, u):
            sp.dma_start(raw(u).rearrange("p (k c) -> p k c", k=4), weights(e, u)).then_inc(w_in[u % NR], 16)

        def pgu(c):
            return ps[:, 2 * (c % 2):2 * (c % 2) + 2, :]

        def split_hi(act, i, u):
            act.wait_ge(w_in[u % NR], 16 * (NU // NR * i + u // NR + 1))
            nc.scalar.copy(w_hi[:, u % NS, :], raw(u)).then_inc(hi_done, 1)

        def split_lo(dve, i, u):
            dve.wait_ge(hi_done, NU * i + u + 1)
            nc.vector.tensor_tensor(w_lo[:, u % NS, :], raw(u), w_hi[:, u % NS, :].bitcast(f32), ALU.subtract
                                    ).then_inc(lo_done, 1)

        def x_bank(q):
            return ps[:, 6 + q % 2, :].rearrange("p (k b c) -> p k b c", k=2, b=2)

        def a_bank(c):
            return ps[:, 4 + c % 2, :].rearrange("p (k b c) -> p k b c", k=2, b=2)

        def x_hi_part(act, j, q):
            act.wait_ge(xt_turned, 4 * j + q + 1)
            nc.scalar.copy(x_hi[:, 2 * q:2 * q + 2, :, :], x_bank(q)).then_inc(xt_hi, 1)

        def x_lo_part(dve, j, q):
            dve.wait_ge(xt_hi, 4 * j + q + 1)
            nc.vector.tensor_tensor(x_lo[:, 2 * q:2 * q + 2, :, :], x_bank(q),
                                    x_hi[:, 2 * q:2 * q + 2, :, :].bitcast(f32), ALU.subtract).then_inc(xt_lo, 1)

        def a_hi_part(act, i, c):
            act.wait_ge(at_turned, 4 * i + c + 1)
            nc.scalar.copy(a_hi[:, 2 * c:2 * c + 2, :, :], a_bank(c)).then_inc(at_hi, 1)

        def a_lo_part(dve, i, c):
            dve.wait_ge(at_hi, 4 * i + c + 1)
            nc.vector.tensor_tensor(a_lo[:, 2 * c:2 * c + 2, :, :], a_bank(c),
                                    a_hi[:, 2 * c:2 * c + 2, :, :].bitcast(f32), ALU.subtract).then_inc(at_lo, 1)

        def x_turn(pe, j, q):
            if q == 0:
                pe.wait_ge(x_in, 32 * (j + 1))
            pe.wait_ge(xt_lo, 4 * j + q + 1)
            for kk in range(2):
                for b in range(2):
                    c = (2 * q + kk) * P
                    last = nc.tensor.transpose(x_bank(q)[:, kk, b, :], xg[:, b, c:c + P], k.ident[:, :])
            last.then_inc(xt_turned, 1)

        def fetch_rows(pool, j):
            b0 = field(pool, j, B0_FIELD, NBLK - 2)
            nc.gpsimd.tensor_copy(ridx[:, :], k.rows[:, bass.ds(b0, 2)]).then_inc(ridx_done, 1)
            pool.wait_ge(ridx_done, j + 1)
            pool.sem_inc(pool_passed, 1)
            for b in range(2):
                nc.gpsimd.indirect_dma_start(
                    out=xg[:, b, :], out_offset=None, in_=k.h_rows,
                    in_offset=bass.IndirectOffsetOnAxis(ap=ridx[:, b:b + 1], axis=0)).then_inc(x_in, 16)

        def part_products(pe, c, b, ks, start, stop_bias):
            src_hi, src_lo = (x_hi, x_lo) if c < 4 else (a_hi, a_lo)
            out = ps[:, 2 * (c % 2) + b, :]
            for kk in ks:
                u = 2 * c + kk // 4
                cols = slice((kk % 4) * N, (kk % 4 + 1) * N)
                last = mm3(nc, out, src_hi[:, kk, b, :], src_lo[:, kk, b, :], w_hi[:, u % NS, cols],
                           w_lo[:, u % NS, cols], start and kk == ks[0], False)
            if stop_bias:
                last = nc.tensor.matmul(out, sel[:, :], bias[:, c * N:(c + 1) * N], start=False, stop=True)
            return last

        with nc.Block() as block:
            @block.sync
            def _(sp):
                e0 = field(sp, 0, E_FIELD, NE - 1)
                for u in range(NR):
                    load(sp, e0, u)
                sp.wait_ge(zero_made, 1)
                rest = sp.value_load(k.table[0:1, REST_FIELD:REST_FIELD + 1], min_val=1, max_val=USED - 1)
                with sp.Fori(0, rest) as b:
                    sp.dma_start(k.y_rows[bass.ds((USED - 1) - b, 1)].rearrange("o p n -> (o p) n"), zero[:, :]).then_inc(zeroed, 16)
                items = sp.value_load(k.table[0:1, N_FIELD:N_FIELD + 1], min_val=1, max_val=48)
                with sp.Fori(0, items) as i:
                    e = field(sp, i, E_FIELD, NE - 1)
                    e_next = field(sp, i + 1, E_FIELD, NE - 1)
                    for u in range(NU):
                        sp.wait_ge(lo_done, NU * i + u + 1)
                        v_ = u + NR
                        load(sp, e if v_ < NU else e_next, v_ % NU)
                e_past = field(sp, items, E_FIELD, NE - 1)
                for u in range(NR, NS):
                    sp.wait_ge(lo_done, NU * items + u - NR + 1)
                    load(sp, e_past, u)
                for s in range(NR):
                    sp.wait_ge(w_in[s], items * (16 * (NU // NR)) + (32 if s < NS - NR else 16))
                    sp.sem_inc(sp_passed, 1)
                sp.wait_ge(zeroed, rest * 16)
                sp.sem_inc(sp_passed, 1)

            @block.gpsimd
            def _(pool):
                nc.gpsimd.memset(zero[:, :], 0.0).then_inc(zero_made, 1)
                fetch_rows(pool, 0)
                items = pool.value_load(k.table[0:1, N_FIELD:N_FIELD + 1], min_val=1, max_val=48)
                with pool.Fori(0, items) as i:
                    pool.wait_ge(xt_turned, 4 * i + 4)
                    fetch_rows(pool, i + 1)
                    for c in range(4):
                        pool.wait_ge(sg_done, 4 * i + c + 1)
                        pool.wait_ge(t_done, 4 * i + c + 1)
                        nc.gpsimd.tensor_tensor(gt[:, c % 2, :, :], up[:, c % 2, :, :], sg[:, c % 2, :, :], ALU.mult
                                                ).then_inc(a_done, 1)
                pool.wait_ge(x_in, items * 32 + 32)
                pool.sem_inc(pool_passed, 1)

            @block.scalar
            def _(act):
                nc.scalar.preload_act_table_set("sigmoid_and_others")
                for u in range(NS):
                    split_hi(act, 0, u)
                    if u == 1:
                        for q in range(4):
                            x_hi_part(act, 0, q)
                items = act.value_load(k.table[0:1, N_FIELD:N_FIELD + 1], min_val=1, max_val=48)
                with act.Fori(0, items) as i:
                    for c in range(4):
                        act.wait_ge(g_done, 4 * i + c + 1)
                        nc.scalar.activation(sg[:, c % 2, :, :], gt[:, c % 2, :, :], ACT.Sigmoid, scale=ALPHA
                                             ).then_inc(sg_done, 1)
                        if c >= 1:
                            a_hi_part(act, i, c - 1)
                        if c < 3:
                            split_hi(act, i, 2 * c + 6)
                            split_hi(act, i, 2 * c + 7)
                    x_hi_part(act, i + 1, 0)
                    x_hi_part(act, i + 1, 1)
                    split_hi(act, i, 12)
                    a_hi_part(act, i, 3)
                    x_hi_part(act, i + 1, 2)
                    x_hi_part(act, i + 1, 3)
                    split_hi(act, i, 13)
                    for c in (4, 5):
                        act.wait_ge(chunk_done, 6 * i + c + 1)
                        if c == 4:
                            act.wait_ge(y_stored, 32 * i)
                        nc.scalar.copy(y[:, :, (c - 4) * N:(c - 3) * N], pgu(c)).then_inc(y_free, 1)
                        if c == 5:
                            act.wait_ge(y_free, 2 * i + 4)
                            b0 = field(act, i, B0_FIELD, NBLK - 2)
                            b1 = field(act, i, B1_FIELD, NBLK - 1)
                            act.dma_start(k.y_rows[bass.ds(b0, 1)].rearrange("o p n -> (o p) n"), y[:, 0, :]
                                          ).then_inc(y_stored, 16)
                            act.dma_start(k.y_rows[bass.ds(b1, 1)].rearrange("o p n -> (o p) n"), y[:, 1, :]
                                          ).then_inc(y_stored, 16)
                        split_hi(act, i, 2 * c + 6)
                        split_hi(act, i, 2 * c + 7)
                act.wait_ge(y_stored, items * 32)
                act.sem_inc(act_passed, 1)

            @block.vector
            def _(dve):
                V = nc.vector
                V.memset(ps[:, 0:4, :], 0.0).then_inc(y_free, 2)
                V.memset(ps[:, 6:8, :], 0.0).then_inc(xt_lo, 2)
                V.tensor_copy(sel[:, :], k.sel[:, 0:1].broadcast_to((3 * NE, P))).then_inc(sel_done, 1)
                for u in range(NS):
                    split_lo(dve, 0, u)
                    if u == 1:
                        for q in range(4):
                            x_lo_part(dve, 0, q)
                items = dve.value_load(k.table[0:1, N_FIELD:N_FIELD + 1], min_val=1, max_val=48)
                with dve.Fori(0, items) as i:
                    for c in range(4):
                        n = 4 * i + c + 1
                        dve.wait_ge(chunk_done, 6 * i + c + 1)
                        bank = pgu(c)
                        V.tensor_scalar(gt[:, c % 2, :, :], bank[:, :, 0:N:2], LIMIT, None, ALU.min).then_inc(g_done, 1)
                        V.tensor_scalar(up[:, c % 2, :, :], bank[:, :, 1:N:2], LIMIT, -LIMIT, ALU.min, ALU.max
                                        ).then_inc(up_free, 1)
                        dve.wait_ge(up_free, n)
                        dve.wait_ge(g_done, n)
                        V.scalar_tensor_tensor(out=up[:, c % 2, :, :], in0=up[:, c % 2, :, :], scalar=1.0,
                                               in1=gt[:, c % 2, :, :], op0=ALU.add, op1=ALU.mult).then_inc(t_done, 1)
                        if c >= 1:
                            a_lo_part(dve, i, c - 1)
                        if c < 3:
                            split_lo(dve, i, 2 * c + 6)
                            split_lo(dve, i, 2 * c + 7)
                    x_lo_part(dve, i + 1, 0)
                    x_lo_part(dve, i + 1, 1)
                    split_lo(dve, i, 12)
                    a_lo_part(dve, i, 3)
                    x_lo_part(dve, i + 1, 2)
                    x_lo_part(dve, i + 1, 3)
                    split_lo(dve, i, 13)
                    for c in (4, 5):
                        dve.wait_ge(chunk_done, 6 * i + c + 1)
                        if c == 5:
                            V.tensor_copy(sel[:, :], k.sel[:, bass.ds(i + 1, 1)].broadcast_to((3 * NE, P))
                                          ).then_inc(sel_done, 1)
                        split_lo(dve, i, 2 * c + 6)
                        split_lo(dve, i, 2 * c + 7)

            @block.tensor
            def _(pe):
                for q in range(4):
                    x_turn(pe, 0, q)
                items = pe.value_load(k.table[0:1, N_FIELD:N_FIELD + 1], min_val=1, max_val=48)
                with pe.Fori(0, items) as i:
                    two = field(pe, i, TWO_FIELD, 1)

                    def products(c, ks, start, stop):
                        with pe.If(two > 0):
                            part_products(pe, c, 1, ks, start, stop)
                        return part_products(pe, c, 0, ks, start, stop)

                    def act_turn(c):
                        pe.wait_ge(a_done, 4 * i + c + 1)
                        if c >= 2:
                            pe.wait_ge(at_lo, 4 * i + c - 1)
                        for kk in range(2):
                            for b in range(2):
                                last = nc.tensor.transpose(a_bank(c)[:, kk, b, :], gt[:, c % 2, b, kk * P:(kk + 1) * P],
                                                           k.ident[:, :])
                        last.then_inc(at_turned, 1)

                    def parts_ready(u):
                        pe.wait_ge(lo_done, NU * i + u + 1)

                    for c in range(4):
                        if c == 0:
                            pe.wait_ge(xt_lo, 4 * i + 6)
                            pe.wait_ge(sel_done, i + 1)
                        if c < 2:
                            pe.wait_ge(y_free, 2 * i + c + 1)
                        else:
                            pe.wait_ge(up_free, 4 * i + c - 1)
                        parts_ready(2 * c + 1)
                        products(c, list(range(KT)), True, True).then_inc(chunk_done, 1)
                        if c >= 1:
                            act_turn(c - 1)
                    x_turn(pe, i + 1, 0)
                    x_turn(pe, i + 1, 1)
                    pe.wait_ge(up_free, 4 * i + 3)
                    pe.wait_ge(at_lo, 4 * i + 3)
                    parts_ready(9)
                    products(4, list(range(6)), True, False)
                    act_turn(3)
                    x_turn(pe, i + 1, 2)
                    x_turn(pe, i + 1, 3)
                    pe.wait_ge(up_free, 4 * i + 4)
                    parts_ready(10)
                    products(5, list(range(4)), True, False)
                    pe.wait_ge(at_lo, 4 * i + 4)
                    products(4, [6, 7], False, True).then_inc(chunk_done, 1)
                    parts_ready(11)
                    products(5, [4, 5, 6, 7], False, True).then_inc(chunk_done, 1)


def stage_combine(nc, k, x_from, g_final, out):
    with Stage(nc) as ctx:
        def sb(nm, shape, dt=f32):
            return ctx.enter_context(nc.sbuf_tensor(f"c_{nm}", shape, dt))

        def sem(nm):
            return ctx.sem(f"c_{nm}")

        GB, XB = 8, 3
        got = sb("got", [P, GB, D])
        xt, gain, junk, stat = sb("xt", [P, XB, D]), sb("gain", [P, D]), sb("junk", [P, D]), sb("stat", [P, 3, TT])
        row_in = [sem(f"row_in{i}") for i in range(GB)]
        x_in = [sem(f"x_in{i}") for i in range(XB)]
        g_in, added, sumsq, root, inv, scaled = (sem(s) for s in ("g_in", "added", "sumsq", "root", "inv", "scaled"))
        stored = [sem(f"stored{i}") for i in range(XB)]
        Q = TT * TOPK
        with nc.Block() as block:
            @block.gpsimd
            def _(pool):
                for q in range(Q):
                    if q >= GB:
                        pool.wait_ge(added, q - GB + 1)
                    nc.gpsimd.indirect_dma_start(
                        out=got[:, q % GB, :], out_offset=None, in_=k.y_rows[0:USED].rearrange("b p n -> (b p) n"),
                        in_offset=bass.IndirectOffsetOnAxis(ap=k.slots[:, q:q + 1], axis=0)
                    ).then_inc(row_in[q % GB], 16)

            @block.sync
            def _(sp):
                sp.dma_start(gain[:, :], gain_row(g_final)).then_inc(g_in, 16)
                for t in range(TT + XB):
                    if t >= XB:
                        sp.wait_ge(scaled, t - XB + 1)
                        sp.dma_start(out[0, (t - XB) * P:(t - XB + 1) * P, :], xt[:, t % XB, :]
                                     ).then_inc(stored[t % XB], 16)
                        if t < TT:
                            sp.wait_ge(stored[t % XB], 16 * (t // XB))
                    if t < TT:
                        sp.dma_start(xt[:, t % XB, :], x_from[t * P:(t + 1) * P, :]).then_inc(x_in[t % XB], 16)
                for b in range(XB):
                    sp.wait_ge(stored[b], 16 * ((TT - 1 - b) // XB + 1))

            @block.scalar
            def _(act):
                for t in range(TT):
                    act.wait_ge(added, TOPK * (t + 1))
                    if t:
                        act.wait_ge(sumsq, t)
                    nc.scalar.activation(junk[:, :], xt[:, t % XB, :], ACT.Square, accum_out=stat[:, 0, t:t + 1]
                                         ).then_inc(sumsq, 1)
                    act.wait_ge(sumsq, t + 1)
                    nc.scalar.activation(stat[:, 1, t:t + 1], stat[:, 0, t:t + 1], ACT.Sqrt, scale=1.0 / D,
                                         bias=k.eps[:, 0:1]).then_inc(root, 1)

            @block.vector
            def _(dve):
                def finish(t):
                    dve.wait_ge(root, t + 1)
                    nc.vector.reciprocal(stat[:, 2, t:t + 1], stat[:, 1, t:t + 1]).then_inc(inv, 1)
                    dve.wait_ge(inv, t + 1)
                    nc.vector.scalar_tensor_tensor(out=xt[:, t % XB, :], in0=xt[:, t % XB, :],
                                                   scalar=stat[:, 2, t:t + 1], in1=gain[:, :], op0=ALU.mult,
                                                   op1=ALU.mult).then_inc(scaled, 1)

                dve.wait_ge(g_in, 16)
                for t in range(TT):
                    dve.wait_ge(x_in[t % XB], 16 * (t // XB + 1))
                    for j in range(TOPK):
                        q = TOPK * t + j
                        dve.wait_ge(row_in[q % GB], 16 * (q // GB + 1))
                        if j:
                            dve.wait_ge(added, q)
                        nc.vector.scalar_tensor_tensor(out=xt[:, t % XB, :], in0=got[:, q % GB, :],
                                                       scalar=k.gates[:, t, j:j + 1], in1=xt[:, t % XB, :],
                                                       op0=ALU.mult, op1=ALU.add).then_inc(added, 1)
                    if t:
                        finish(t - 1)
                finish(TT - 1)


def program(nc, x, mem, g_mix, w_in, w_conv, g_conv_out, g_sb_out, w_out, g_xattn, g_mem, w_xq, w_xkv, w_xo,
            g_ffn, w_router, b_router, w_gate_up, b_gate_up, w_down, b_down, g_final, out, until=99):
    k = Kit()

    def cols(w, width):
        v = w[0].rearrange("(k p) n -> p k n", p=P)
        return [v[:, :, c:c + 256] for c in range(0, width, 256)]

    def halves(w):
        v = w[0].rearrange("(k p) n -> p k n", p=P)
        return [v[:, 4 * h:4 * h + 4, n * N:(n + 1) * N] for n in range(2) for h in range(2)]

    w_in_units = cols(w_in, 3 * D)
    order = [0, 1, 4, 5, 2, 3, 6, 7, 8, 9, 10, 11]
    units = [w_in_units[i] for i in order] + cols(w_xkv, 2 * D) + halves(w_out) + cols(w_xq, D) + halves(w_xo)

    def dram(name, shape, dt=f32):
        return nc.dram_tensor(name, shape, dt, kind="Internal").ap()

    x1, x2, k.h_rows = dram("x_mixed", (SEQ, D)), dram("x_crossed", (SEQ, D)), dram("expert_inputs", (SEQ, D))
    k.y_rows = dram("expert_rows", (NBLK, BLOCK, D))
    k.table_dram = dram("item_table", (P, 8), i32)

    with ExitStack() as ctx:
        def sb(scope, name, shape, dt=f32):
            return scope.enter_context(nc.sbuf_tensor(name, shape, dt))

        k.logits = sb(ctx, "logits", [P, TT, NE])
        k.gates = sb(ctx, "gates", [P, TT, TOPK])
        k.slots = sb(ctx, "slots", [P, TT * TOPK], i32)
        k.rows = sb(ctx, "rows_of_slots", [P, NBLK + 1], i32)
        k.sel = sb(ctx, "expert_of_item", [3 * NE, P], bf16)
        k.table = sb(ctx, "item_row", [1, P * 8], i32)
        constants(nc, ctx, k)
        k.ring = Ring(nc, ctx, units)
        with ExitStack() as dense:
            k.act_hi = sb(dense, "act_hi", [P, KT, SEQ], f32r)
            k.act_lo = sb(dense, "act_lo", [P, KT, SEQ], f32r)
            with ExitStack() as mixer:
                k.y, k.q, k.k = (sb(mixer, s, [P, 4, SEQ]) for s in ("mix_y", "mix_q", "mix_k"))
                k.v = sb(mixer, "mix_v", [P, TT, 512])
                k.o = k.q
                stage_projections(nc, k, x, g_mix, w_conv)
                if until >= 2:
                    stage_stick(nc, k)
                    stage_mixer_norms(nc, k, g_conv_out, g_sb_out)
            with ExitStack() as cross:
                if until >= 3:
                    k.mk = sb(cross, "mem_k", [P, KT, MEM])
                    k.mv = sb(cross, "mem_v", [P, 2, D])
                    stage_memory(nc, k, mem, g_mem, 12)
                    stage_residual(nc, k, "mix", x[0], x1, g_xattn, 20)
                if until >= 4:
                    stage_cross(nc, k, 24)
            if until >= 4:
                stage_residual(nc, k, "ffn", x1, x2, g_ffn, 28, router=(w_router, b_router))
        if until >= 5:
            stage_routing(nc, k)
        if until >= 6:
            stage_experts(nc, k, w_gate_up, b_gate_up, w_down, b_down)
            stage_combine(nc, k, x2, g_final, out)


_INS = ["x", "mem", "g_mix", "w_in", "w_conv", "g_conv_out", "g_sb_out", "w_out", "g_xattn", "g_mem", "w_xq", "w_xkv",
        "w_xo", "g_ffn", "w_router", "b_router", "w_gate_up", "b_gate_up", "w_down", "b_down", "g_final"]
_OUTS = [((1, SEQ, D), "float32")]


def kernel(**inputs):
    import numpy as _np
    import concourse.bacc as _bacc
    from concourse import mybir as _mybir
    from concourse.bass_utils import run_bass_kernel_spmd as _run

    nc = _bacc.Bacc("TRN2", target_bir_lowering=False, num_devices=1)
    arrays, args = {}, []
    for name in _INS:
        a = _np.ascontiguousarray(inputs[name])
        if a.ndim == 1:
            a = a.reshape(1, -1)
        arrays[f"in_{name}_dram"] = a
        args.append(nc.dram_tensor(f"in_{name}_dram", a.shape, _mybir.dt.from_np(a.dtype), kind="ExternalInput").ap())
    for i, (shape, dtype) in enumerate(_OUTS):
        dt = _mybir.dt.from_np(_np.dtype(dtype))
        args.append(nc.dram_tensor(f"out_{i}_dram", shape, dt, kind="ExternalOutput").ap())
    program(nc, *args)
    r = _run(nc, [arrays], core_ids=[0])
    return r.results[0]["out_0_dram"]
```

```python
from contextlib import ExitStack

import concourse.bass as bass
from concourse import mybir

f32 = mybir.dt.float32
f32r = mybir.dt.float32r
bf16 = mybir.dt.bfloat16
i32 = mybir.dt.int32
u32 = mybir.dt.uint32
ALU = mybir.AluOpType
ACT = mybir.ActivationFunctionType
AX = mybir.AxisListType.X

P = 128
D = 1024
SEQ = 1024
MEM = 256
KT = D // P
TT = SEQ // P
CW = 512
HEADS, HD = 8, 64
XH, XD = 4, 256
NE, TOPK = 32, 4
EPS = 1e-6
LIMIT, ALPHA = 7.0, 1.702
BLOCK = 128
REST = 64
CAP = BLOCK + REST
SOME_LO = 2
MAX_ITEMS = SEQ * TOPK // CAP + NE
N = 512
RAW = 4
UNIT = 2048


class Stage(ExitStack):

    cleared = {}

    def __init__(self, nc):
        super().__init__()
        self.nc, self.sems = nc, []

    def sem(self, name):
        self.sems.append(self.nc.alloc_semaphore(name))
        return self.sems[-1]

    def __exit__(self, *exc):
        if exc[0] is None:
            for s in self.sems:
                self.nc.gpsimd.sem_clear(s)
            for s in Stage.cleared.pop(id(self.nc), []):
                self.nc.release_semaphore(s)
            Stage.cleared[id(self.nc)] = self.sems
        return super().__exit__(*exc)


class Ring:

    def __init__(self, nc, ctx, units):
        self.nc, self.units = nc, units
        self.raw = ctx.enter_context(nc.sbuf_tensor("w_raw", [P, RAW, UNIT], f32))
        self.ready = [ctx.enter_context(nc.semaphore(f"w_loaded{s}")) for s in range(RAW)]
        self.hi_done = ctx.enter_context(nc.semaphore("w_hi_done"))
        self.lo_done = ctx.enter_context(nc.semaphore("w_lo_done"))

    def load(self, sp, n):
        if n >= len(self.units):
            return
        if n >= RAW:
            sp.wait_ge(self.lo_done, n - RAW + 1)
        ap = self.units[n]
        dst = self.raw[:, n % RAW, :].rearrange("p (k c) -> p k c", k=ap.shape[1])
        sp.dma_start(dst, ap).then_inc(self.ready[n % RAW], 16)

    def hi(self, act, n, dst):
        act.wait_ge(self.ready[n % RAW], 16 * (n // RAW + 1))
        self.nc.scalar.copy(dst, self.raw[:, n % RAW, :]).then_inc(self.hi_done, 1)

    def lo(self, dve, n, hi, dst):
        dve.wait_ge(self.hi_done, n + 1)
        self.nc.vector.tensor_tensor(dst, self.raw[:, n % RAW, :], hi.bitcast(f32),
                                     ALU.subtract).then_inc(self.lo_done, 1)


def mm3(nc, out, lh, ll, rh, rl, start, stop):
    nc.tensor.matmul(out, ll, rh, start=start, stop=False)
    nc.tensor.matmul(out, lh, rl, start=False, stop=False)
    return nc.tensor.matmul(out, lh, rh, start=False, stop=stop)


class RowNorm:

    def __init__(self, nc, ctx, name, src, ready, gain, gain_ready, ident, eps, banks, dest, hn_free=None, scratch=None):
        self.nc, self.src, self.ready, self.gain, self.gain_ready = nc, src, ready, gain, gain_ready
        self.ident, self.eps, self.banks, self.dest, self.hn_free = ident, eps, banks, dest, hn_free
        if scratch is None:
            self.junk = ctx.enter_context(nc.sbuf_tensor(f"{name}_square", [P, D], f32))
            self.hn = ctx.enter_context(nc.sbuf_tensor(f"{name}_rows", [P, 2, D], f32))
        else:
            self.junk, self.hn = scratch
        self.stat = ctx.enter_context(nc.sbuf_tensor(f"{name}_stat", [P, 3, TT], f32))
        self.sumsq_done, self.rms_done, self.inv_done, self.rows_done, self.turned, self.hi_done, \
            self.lo_done = [ctx.sem(f"{name}_{s}") for s in
                            ("sumsq", "rms", "inv", "rows", "turned", "hi", "lo")]

    def act_stats(self, act, t):
        nc = self.nc
        self.ready(act, t)
        if t:
            act.wait_ge(self.sumsq_done, t)
        nc.scalar.activation(self.junk[:, :], self.src(t), ACT.Square,
                             accum_out=self.stat[:, 0, t:t + 1]).then_inc(self.sumsq_done, 1)
        act.wait_ge(self.sumsq_done, t + 1)
        nc.scalar.activation(self.stat[:, 1, t:t + 1], self.stat[:, 0, t:t + 1], ACT.Sqrt,
                             scale=1.0 / D, bias=self.eps[:, 0:1]).then_inc(self.rms_done, 1)

    def dve_rows(self, dve, t):
        nc = self.nc
        dve.wait_ge(self.rms_done, t + 1)
        nc.vector.reciprocal(self.stat[:, 2, t:t + 1], self.stat[:, 1, t:t + 1]).then_inc(self.inv_done, 1)
        dve.wait_ge(self.inv_done, t + 1)
        self.ready(dve, t)
        if t == 0:
            self.gain_ready(dve)
        if t >= 2:
            dve.wait_ge(self.turned, 2 * (t - 1))
            if self.hn_free:
                self.hn_free(dve, t - 2)
        nc.vector.scalar_tensor_tensor(out=self.hn[:, t % 2, :], in0=self.src(t), scalar=self.stat[:, 2, t:t + 1],
                                       in1=self.gain, op0=ALU.mult, op1=ALU.mult).then_inc(self.rows_done, 1)

    def pe_turn(self, pe, t):
        pe.wait_ge(self.rows_done, t + 1)
        nb = len(self.banks)
        for q in range(2):
            n = 2 * t + q
            if n >= nb:
                pe.wait_ge(self.lo_done, n - nb + 1)
            bank = self.banks[n % nb]
            for k in range(4):
                c = (4 * q + k) * P
                last = self.nc.tensor.transpose(bank[:, k * P:(k + 1) * P], self.hn[:, t % 2, c:c + P],
                                                self.ident[:, :])
            last.then_inc(self.turned, 1)

    def bank(self, t, q):
        return self.banks[(2 * t + q) % len(self.banks)].rearrange("p (k c) -> p k c", k=4)

    def act_hi(self, act, t):
        for q in range(2):
            act.wait_ge(self.turned, 2 * t + q + 1)
            self.nc.scalar.copy(self.dest(t, q)[0], self.bank(t, q)).then_inc(self.hi_done, 1)

    def dve_lo(self, dve, t):
        for q in range(2):
            hi, lo = self.dest(t, q)
            dve.wait_ge(self.hi_done, 2 * t + q + 1)
            self.nc.vector.tensor_tensor(lo, self.bank(t, q), hi.bitcast(f32),
                                         ALU.subtract).then_inc(self.lo_done, 1)


class Kit:
    pass


def constants(nc, ctx, k):
    def sb(name, shape, dt=f32):
        return ctx.enter_context(nc.sbuf_tensor(name, shape, dt))

    k.ident = sb("ident", [P, P])
    k.ident_bf = sb("ident_bf", [P, P], bf16)
    k.eps = sb("eps", [P, 1])
    k.ps = ctx.enter_context(nc.psum_tensor("ps", [P, 8, N], f32))
    made = ctx.enter_context(nc.semaphore("consts_made"))
    with nc.Block() as block:
        @block.gpsimd
        def _(pool):
            nc.gpsimd.memset(k.ident[:, :], 0.0).then_inc(made, 1)
            nc.gpsimd.memset(k.eps[:, :], EPS).then_inc(made, 1)
            pool.wait_ge(made, 2)
            nc.gpsimd.affine_select(out=k.ident[:, :], in_=k.ident[:, :], compare_op=ALU.not_equal, fill=1.0,
                                    base=0, pattern=[[-1, P]], channel_multiplier=1).then_inc(made, 1)
            pool.wait_ge(made, 3)
            nc.gpsimd.tensor_copy(k.ident_bf[:, :], k.ident[:, :]).then_inc(made, 1)


def gain_row(ap):
    return ap[0, :].partition_broadcast(P)


def stage_projections(nc, k, x, g_mix, w_conv):
    with Stage(nc) as ctx:
        def sb(name, shape, dt=f32):
            return ctx.enter_context(nc.sbuf_tensor(name, shape, dt))

        def sem(name):
            return ctx.sem(name)

        SL = 2
        w_hi, w_lo = sb("p_whi", [P, SL, UNIT], f32r), sb("p_wlo", [P, SL, UNIT], f32r)
        acc = sb("conv_acc", [P, N])
        wc = sb("w_conv_t", [P, 3, 4])
        ps = k.ps
        mm_done, ev_act, ev_dve, conv_step, wc_in = (sem(s) for s in ("p_mm", "p_evac_act", "p_evac_dve",
                                                                       "conv_step", "wc_in"))
        x_in = [sem(f"p_x_in{i}") for i in range(2)]
        g_in = sem("p_g_in")
        xt = [k.y[:, 0, :], k.y[:, 1, :]]
        gain = k.y[:, 2, :]
        scratch = (k.y[:, 3, :], k.v[:, 0:4, :].rearrange("p (a b) c -> p a (b c)", a=2))

        def x_ready(eng, t):
            eng.wait_ge(x_in[t % 2], 16 * (t // 2 + 1))

        norm = RowNorm(nc, ctx, "p", lambda t: xt[t % 2], x_ready, gain, lambda e: e.wait_ge(g_in, 16),
                       k.ident, k.eps, [ps[:, b, :] for b in range(2)],
                       lambda t, q: (k.act_hi[:, 4 * q:4 * q + 4, t * P:(t + 1) * P],
                                     k.act_lo[:, 4 * q:4 * q + 4, t * P:(t + 1) * P]), scratch=scratch)

        kinds = ["u", "u", "c", "c", "b", "b", "q", "q", "k", "k", "v", "v"]
        groups = []
        for n, kind in enumerate(kinds):
            if kind == "v":
                groups += [(n, kind, n % 2, t) for t in range(TT)]
            else:
                halves = (1, 0) if kind == "b" else (0, 1)
                groups += [(n, kind, 2 * (n % 2) + m, th) for m in range(2) for th in halves]
        on_act = {"u", "q", "v"}
        count = {"act": 0, "dve": 0}
        done_at, index = [], {}
        for g, (n, kind, f, th) in enumerate(groups):
            e = "act" if kind in on_act else "dve"
            count[e] += 1
            done_at.append((e, count[e]))
            index[(kind, f, th)] = g
        unit_end = [max(g for g, x_ in enumerate(groups) if x_[0] == n) + 1 for n in range(12)]
        sem_of = {"act": ev_act, "dve": ev_dve}
        BK = 6

        def evacuated(eng, g):
            e, v = done_at[g]
            eng.wait_ge(sem_of[e], v)

        with nc.Block() as block:
            @block.sync
            def _(sp):
                sp.dma_start(gain, gain_row(g_mix)).then_inc(g_in, 16)
                for t in range(TT):
                    if t >= 2:
                        sp.wait_ge(norm.rows_done, t - 1)
                        sp.wait_ge(norm.sumsq_done, t - 1)
                    sp.dma_start(xt[t % 2], x[0, t * P:(t + 1) * P, :]).then_inc(x_in[t % 2], 16)
                    if t == 1:
                        for j in range(3):
                            with nc.allow_non_contiguous_dma(reason="512 taps a row, once"):
                                sp.dma_start(wc[:, j, :], w_conv[0, j, :].rearrange("(f p) -> p f", p=P)
                                             ).then_inc(wc_in, 16)
                        for n in range(RAW):
                            k.ring.load(sp, n)
                for n in range(RAW, 12 + RAW):
                    k.ring.load(sp, n)
                sp.wait_ge(wc_in, 48)

            @block.scalar
            def _(act):
                for t in range(TT + 1):
                    if t < TT:
                        norm.act_stats(act, t)
                    if t:
                        norm.act_hi(act, t - 1)
                for n in range(SL):
                    k.ring.hi(act, n, w_hi[:, n, :])
                g = 0
                for n in range(12):
                    while g < len(groups) and groups[g][0] == n:
                        _, kind, f, th = groups[g]
                        if kind in on_act:
                            act.wait_ge(mm_done, g + 1)
                            bank = ps[:, 2 + g % BK, :]
                            if kind == "u":
                                nc.scalar.copy(k.y[:, f, th * N:(th + 1) * N], bank).then_inc(ev_act, 1)
                            elif kind == "q":
                                nc.scalar.activation(k.q[:, f, th * N:(th + 1) * N], bank, ACT.Copy,
                                                     scale=HD ** -0.5).then_inc(ev_act, 1)
                            else:
                                nc.scalar.copy(k.v[:, th, f * 256:(f + 1) * 256], bank[:, 0:256]
                                               ).then_inc(ev_act, 1)
                        g += 1
                    if n + SL < 12:
                        act.wait_ge(mm_done, unit_end[n])
                        k.ring.hi(act, n + SL, w_hi[:, n % SL, :])

            @block.vector
            def _(dve):
                for t in range(TT + 1):
                    if t < TT:
                        norm.dve_rows(dve, t)
                    if t:
                        norm.dve_lo(dve, t - 1)
                for n in range(SL):
                    k.ring.lo(dve, n, w_hi[:, n, :], w_lo[:, n, :])
                dve.wait_ge(wc_in, 48)
                g = steps = 0
                for n in range(12):
                    while g < len(groups) and groups[g][0] == n:
                        _, kind, f, th = groups[g]
                        bank = ps[:, 2 + g % BK, :]
                        c0 = th * N
                        if kind == "c":
                            dve.wait_ge(mm_done, g + 1)
                            evacuated(dve, index[("u", f, th)])
                            here = k.y[:, f, c0:c0 + N]
                            nc.vector.tensor_tensor(here, bank, here, ALU.mult).then_inc(ev_dve, 1)
                        elif kind == "k":
                            dve.wait_ge(mm_done, g + 1)
                            nc.vector.tensor_copy(k.k[:, f, c0:c0 + N], bank).then_inc(ev_dve, 1)
                        elif kind == "b":
                            evacuated(dve, index[("c", f, 1)])
                            if steps:
                                dve.wait_ge(ev_dve, done_at[g - 1][1])
                            nc.vector.tensor_scalar(acc[:, :], k.y[:, f, c0:c0 + N], wc[:, 2, f:f + 1], None,
                                                    ALU.mult).then_inc(conv_step, 1)
                            for back in (1, 2):
                                dve.wait_ge(conv_step, steps + back)
                                o = back if th == 0 else 0
                                nc.vector.scalar_tensor_tensor(
                                    out=acc[:, o:N], in0=k.y[:, f, c0 + o - back:c0 + N - back],
                                    scalar=wc[:, 2 - back, f:f + 1], in1=acc[:, o:N], op0=ALU.mult,
                                    op1=ALU.add).then_inc(conv_step, 1)
                            steps += 3
                            dve.wait_ge(conv_step, steps)
                            dve.wait_ge(mm_done, g + 1)
                            nc.vector.tensor_tensor(k.y[:, f, c0:c0 + N], bank, acc[:, :], ALU.mult
                                                    ).then_inc(ev_dve, 1)
                        g += 1
                    if n + SL < 12:
                        k.ring.lo(dve, n + SL, w_hi[:, n % SL, :], w_lo[:, n % SL, :])

            @block.tensor
            def _(pe):
                for t in range(TT):
                    norm.pe_turn(pe, t)
                pe.wait_ge(norm.lo_done, 2 * TT)
                for g, (n, kind, f, th) in enumerate(groups):
                    if g == 0 or groups[g - 1][0] != n:
                        pe.wait_ge(k.ring.lo_done, n + 1)
                    if g >= BK:
                        evacuated(pe, g - BK)
                    wh = w_hi[:, n % SL, :].rearrange("p (k c) -> p k c", k=KT)
                    wl = w_lo[:, n % SL, :].rearrange("p (k c) -> p k c", k=KT)
                    for kk in range(KT):
                        if kind == "v":
                            out, tok = ps[:, 2 + g % BK, 0:256], slice(th * P, (th + 1) * P)
                            last = mm3(nc, out, k.act_hi[:, kk, tok], k.act_lo[:, kk, tok], wh[:, kk, :],
                                       wl[:, kk, :], kk == 0, kk == KT - 1)
                        else:
                            out, m = ps[:, 2 + g % BK, :], slice((f % 2) * P, (f % 2 + 1) * P)
                            tok = slice(th * N, (th + 1) * N)
                            last = mm3(nc, out, wh[:, kk, m], wl[:, kk, m], k.act_hi[:, kk, tok],
                                       k.act_lo[:, kk, tok], kk == 0, kk == KT - 1)
                    last.then_inc(mm_done, 1)


def stage_stick(nc, k):
    with Stage(nc) as ctx:
        def sb(name, shape, dt=f32):
            return ctx.enter_context(nc.sbuf_tensor(name, shape, dt))

        def sem(name):
            return ctx.sem(name)

        ps = k.ps
        E, L, S, A = (sb(f"stick_{s}", [P, 3, N]) for s in ("e", "l", "sp", "a"))
        later = sb("stick_later", [P, 2, 2, N])
        neg_tri, neg_ones = sb("neg_tri", [P, P]), sb("neg_ones", [P, P])
        mask = sb("mask_bf", [P, P], bf16)
        made, z_done, e_done, cap_done, l_done, sp_done, later_done, cum_done, a_done, av_done, o_done = (
            sem("stick_" + s) for s in ("made", "z", "e", "cap", "l", "sp", "later", "cum", "a", "av", "o"))
        steps = []
        for pair in range(4):
            for T in range(2):
                for j in range(4 * T + 3, -1, -1):
                    for h in range(2):
                        steps.append((pair, T, j, h, max(0, j * P - T * N), j == 4 * T + 3, j == 0))
        NS, ZB = len(steps), 5
        later_count, c = [], 0
        for s in steps:
            c += 0 if s[6] else (1 if s[5] or s[4] == 0 and s[2] * P - s[1] * N < 0 else 2)
            later_count.append(c)

        def z(n):
            return ps[:, n % ZB, :]

        def o_bank(n):
            return 5 + (steps[n][0] * 2 + steps[n][1]) % 2

        with nc.Block() as block:
            @block.gpsimd
            def _(pool):
                nc.gpsimd.memset(neg_ones[:, :], -1.0).then_inc(made, 1)
                nc.gpsimd.memset(mask[:, :], 0.0).then_inc(made, 1)
                pool.wait_ge(made, 2)
                nc.gpsimd.affine_select(out=neg_tri[:, :], in_=neg_ones[:, :], compare_op=ALU.is_ge, fill=0.0,
                                        base=0, pattern=[[-1, P]], channel_multiplier=1).then_inc(made, 1)
                nc.gpsimd.affine_select(out=mask[:, :], in_=mask[:, :], compare_op=ALU.is_ge, fill=-1e30,
                                        base=-1, pattern=[[1, P]], channel_multiplier=-1).then_inc(made, 1)
                for n, (pair, T, j, h, c0, first, final) in enumerate(steps):
                    if final:
                        continue
                    pool.wait_ge(sp_done, n + 1)
                    if n >= 4:
                        pool.wait_ge(cum_done, n - 1)
                    new, old = later[:, h, j % 2, :], later[:, h, (j + 1) % 2, :]
                    if first:
                        nc.gpsimd.tensor_copy(new[:, c0:N], S[:, n % 3, c0:N]).then_inc(later_done, 1)
                        continue
                    p0 = max(0, (j + 1) * P - T * N)
                    pool.wait_ge(later_done, later_count[n - 2])
                    nc.gpsimd.tensor_tensor(new[:, p0:N], old[:, p0:N], S[:, n % 3, p0:N], ALU.add
                                            ).then_inc(later_done, 1)
                    if p0 > c0:
                        nc.gpsimd.tensor_copy(new[:, c0:p0], S[:, n % 3, c0:p0]).then_inc(later_done, 1)

            @block.tensor
            def _(pe):
                pe.wait_ge(made, 4)
                for i in range(NS + 4):
                    if i < NS:
                        pair, T, j, h, c0, first, final = steps[i]
                        if i >= ZB:
                            pe.wait_ge(a_done, i - ZB + 1)
                        r = slice(64 * h, 64 * h + 64)
                        diag = j >= 4 * T
                        last = nc.tensor.matmul(z(i)[:, c0:N], k.k[r, pair, j * P:(j + 1) * P],
                                                k.q[r, pair, T * N + c0:(T + 1) * N], start=True, stop=True)
                        if diag:
                            last = nc.tensor.matmul(z(i)[:, c0:c0 + P], k.ident_bf[:, :], mask[:, :],
                                                    start=False, stop=True, skip_group_check=True)
                        last.then_inc(z_done, 1)
                    n = i - 3
                    if 0 <= n < NS:
                        pair, T, j, h, c0, first, final = steps[n]
                        pe.wait_ge(sp_done, n + 1)
                        last = nc.tensor.matmul(z(n)[:, c0:N], neg_tri[:, :], S[:, n % 3, c0:N], start=False,
                                                stop=True, skip_group_check=True)
                        if not first:
                            p0 = max(0, (j + 1) * P - T * N)
                            pe.wait_ge(later_done, later_count[n - 2])
                            last = nc.tensor.matmul(z(n)[:, p0:N], neg_ones[:, :], later[:, h, (j + 1) % 2, p0:N],
                                                    start=False, stop=True, skip_group_check=True)
                        last.then_inc(cum_done, 1)
                    n = i - 4
                    if 0 <= n < NS:
                        pair, T, j, h, c0, first, final = steps[n]
                        unit = pair * 2 + T
                        if first and unit >= 2:
                            pe.wait_ge(o_done, unit - 1)
                        pe.wait_ge(a_done, n + 1)
                        nc.tensor.matmul(ps[64 * h:64 * h + 64, o_bank(n), c0:N],
                                         k.v[:, j, (2 * pair + h) * HD:(2 * pair + h + 1) * HD],
                                         A[:, n % 3, c0:N], start=first, stop=final,
                                         skip_group_check=True).then_inc(av_done, 1)

            @block.scalar
            def _(act):
                nc.scalar.preload_act_table_set("natural_log_exp_and_others")
                for i in range(NS + 4):
                    if i < NS:
                        c0 = steps[i][4]
                        act.wait_ge(z_done, i + 1)
                        if i >= 3:
                            act.wait_ge(l_done, i - 2)
                        nc.scalar.activation(E[:, i % 3, c0:N], z(i)[:, c0:N], ACT.Exp).then_inc(e_done, 1)
                    n = i - 1
                    if 0 <= n < NS:
                        c0 = steps[n][4]
                        act.wait_ge(cap_done, n + 1)
                        if n >= 3:
                            act.wait_ge(sp_done, n - 2)
                        nc.scalar.activation(L[:, n % 3, c0:N], E[:, n % 3, c0:N], ACT.Ln, bias=1.0
                                             ).then_inc(l_done, 1)
                    n = i - 4
                    if 0 <= n < NS:
                        c0 = steps[n][4]
                        act.wait_ge(cum_done, n + 1)
                        if n >= 3:
                            act.wait_ge(av_done, n - 2)
                        nc.scalar.activation(A[:, n % 3, c0:N], z(n)[:, c0:N], ACT.Exp).then_inc(a_done, 1)

            @block.vector
            def _(dve):
                for i in range(NS + 6):
                    if i < NS:
                        c0 = steps[i][4]
                        dve.wait_ge(e_done, i + 1)
                        nc.vector.tensor_scalar(E[:, i % 3, c0:N], E[:, i % 3, c0:N], 2.0 ** 60, None, ALU.min
                                                ).then_inc(cap_done, 1)
                    n = i - 1
                    if 0 <= n < NS:
                        c0 = steps[n][4]
                        dve.wait_ge(l_done, n + 1)
                        if n >= 3:
                            dve.wait_ge(cum_done, n - 2)
                            dve.wait_ge(later_done, max(1, later_count[n - 3]))
                        nc.vector.tensor_tensor(S[:, n % 3, c0:N], z(n)[:, c0:N], L[:, n % 3, c0:N], ALU.max
                                                ).then_inc(sp_done, 1)
                    n = i - 6
                    if 0 <= n < NS and steps[n][6] and steps[n][3] == 1:
                        pair, T = steps[n][0:2]
                        dve.wait_ge(av_done, n + 1)
                        nc.vector.tensor_copy(k.o[:, pair, T * N:(T + 1) * N], ps[:, o_bank(n), :]
                                              ).then_inc(o_done, 1)


def stage_mixer_norms(nc, k, g_conv, g_sb):
    with Stage(nc) as ctx:
        def sb(name, shape, dt=f32):
            return ctx.enter_context(nc.sbuf_tensor(name, shape, dt))

        def sem(name):
            return ctx.sem(name)

        ps = k.ps
        ones, blk = sb("mn_ones", [P, P]), sb("mn_blocks", [P, P])
        sq = sb("mn_sq", [P, 2, N])
        root, inv = sb("mn_root", [P, 2, N]), sb("mn_inv", [P, 2, N])
        out = sb("mn_out", [P, 2, N])
        gt = sb("mn_gain", [P, 8])
        made, g_in, sq_done, ss_done, root_done, inv_done, out_done, hi_done, lo_done = (
            sem("mn_" + s) for s in ("made", "g_in", "sq", "ss", "root", "inv", "out", "hi", "lo"))
        jobs = []
        for th in range(2):
            jobs.append(([(k.y, f) for f in range(4)], th, ones, CW, 0))
        for pair in range(4):
            for th in range(2):
                jobs.append(([(k.o, pair)], th, blk, HD, 4 + pair))
        sq_at, out_at, a, b = [], [], 0, 0
        for tiles, *_ in jobs:
            sq_at.append(a)
            out_at.append(b)
            a += len(tiles)
            b += len(tiles)

        with nc.Block() as block:
            @block.sync
            def _(sp):
                with nc.allow_non_contiguous_dma(reason="1024 gains, once"):
                    sp.dma_start(gt[:, 0:4], g_conv[0, :].rearrange("(f p) -> p f", p=P)).then_inc(g_in, 16)
                    sp.dma_start(gt[:, 4:8], g_sb[0, :].rearrange("(f p) -> p f", p=P)).then_inc(g_in, 16)
                sp.wait_ge(g_in, 32)

            @block.gpsimd
            def _(pool):
                nc.gpsimd.memset(ones[:, :], 1.0).then_inc(made, 1)
                nc.gpsimd.memset(blk[:, :], 0.0).then_inc(made, 1)
                pool.wait_ge(made, 2)
                nc.gpsimd.memset(blk[0:64, 0:64], 1.0).then_inc(made, 1)
                nc.gpsimd.memset(blk[64:128, 64:128], 1.0).then_inc(made, 1)

            @block.scalar
            def _(act):
                def squares(ji):
                    tiles, th, _, _, _ = jobs[ji]
                    for m, (src, f) in enumerate(tiles):
                        n = sq_at[ji] + m
                        if n >= 2:
                            act.wait_ge(ss_done, n - 1)
                        nc.scalar.activation(sq[:, n % 2, :], src[:, f, th * N:(th + 1) * N], ACT.Square
                                             ).then_inc(sq_done, 1)

                def his(ji):
                    tiles, th, _, _, base = jobs[ji]
                    for m in range(len(tiles)):
                        n = out_at[ji] + m
                        act.wait_ge(out_done, n + 1)
                        nc.scalar.copy(k.act_hi[:, base + m, th * N:(th + 1) * N], out[:, n % 2, :]
                                       ).then_inc(hi_done, 1)

                squares(0)
                for ji, (tiles, th, _, width, _) in enumerate(jobs):
                    act.wait_ge(ss_done, sq_at[ji] + len(tiles))
                    if ji >= 2:
                        act.wait_ge(inv_done, ji - 1)
                    nc.scalar.activation(root[:, ji % 2, :], ps[:, ji % 2, :], ACT.Sqrt, scale=1.0 / width,
                                         bias=k.eps[:, 0:1]).then_inc(root_done, 1)
                    if ji + 1 < len(jobs):
                        squares(ji + 1)
                    his(ji)

            @block.tensor
            def _(pe):
                pe.wait_ge(made, 4)
                for ji, (tiles, th, mat, _, _) in enumerate(jobs):
                    if ji >= 2:
                        pe.wait_ge(root_done, ji - 1)
                    for m in range(len(tiles)):
                        n = sq_at[ji] + m
                        pe.wait_ge(sq_done, n + 1)
                        nc.tensor.matmul(ps[:, ji % 2, :], mat[:, :], sq[:, n % 2, :], start=(m == 0),
                                         stop=(m == len(tiles) - 1)).then_inc(ss_done, 1)

            @block.vector
            def _(dve):
                dve.wait_ge(g_in, 32)
                for ji, (tiles, th, _, _, base) in enumerate(jobs):
                    dve.wait_ge(root_done, ji + 1)
                    if ji >= 2:
                        dve.wait_ge(out_done, out_at[ji - 1])
                    nc.vector.reciprocal(inv[:, ji % 2, :], root[:, ji % 2, :]).then_inc(inv_done, 1)
                    dve.wait_ge(inv_done, ji + 1)
                    for m, (src, f) in enumerate(tiles):
                        n = out_at[ji] + m
                        if n >= 2:
                            dve.wait_ge(lo_done, n - 1)
                        nc.vector.scalar_tensor_tensor(
                            out=out[:, n % 2, :], in0=src[:, f, th * N:(th + 1) * N], scalar=gt[:, base + m:base + m + 1],
                            in1=inv[:, ji % 2, :], op0=ALU.mult, op1=ALU.mult).then_inc(out_done, 1)
                        cols = slice(th * N, (th + 1) * N)
                        dve.wait_ge(hi_done, n + 1)
                        nc.vector.tensor_tensor(k.act_lo[:, base + m, cols], out[:, n % 2, :],
                                                k.act_hi[:, base + m, cols].bitcast(f32), ALU.subtract
                                                ).then_inc(lo_done, 1)


def stage_memory(nc, k, mem, g_mem, first_unit):
    with Stage(nc) as ctx:
        def sb(name, shape, dt=f32):
            return ctx.enter_context(nc.sbuf_tensor(name, shape, dt))

        def sem(name):
            return ctx.sem(name)

        ps = k.ps
        SL = 2
        w_hi, w_lo = sb("m_whi", [P, SL, UNIT], f32r), sb("m_wlo", [P, SL, UNIT], f32r)
        m_hi, m_lo = sb("m_hi", [P, KT, MEM], f32r), sb("m_lo", [P, KT, MEM], f32r)
        xt, gain = sb("m_xt", [P, 2, D]), sb("m_gain", [P, D])
        x_in, g_in, mm_done, evac = (sem("m_" + s) for s in ("x_in", "g_in", "mm", "evac"))
        norm = RowNorm(nc, ctx, "m", lambda t: xt[:, t, :], lambda e, t: e.wait_ge(x_in, 32), gain[:, :],
                       lambda e: e.wait_ge(g_in, 16), k.ident, k.eps, [ps[:, b, :] for b in range(2)],
                       lambda t, q: (m_hi[:, 4 * q:4 * q + 4, t * P:(t + 1) * P],
                                     m_lo[:, 4 * q:4 * q + 4, t * P:(t + 1) * P]))
        BK = 6
        with nc.Block() as block:
            @block.sync
            def _(sp):
                sp.dma_start(gain[:, :], gain_row(g_mem)).then_inc(g_in, 16)
                for t in range(2):
                    sp.dma_start(xt[:, t, :], mem[0, t * P:(t + 1) * P, :]).then_inc(x_in, 16)
                for n in range(first_unit + RAW, first_unit + 8 + RAW):
                    k.ring.load(sp, n)

            @block.scalar
            def _(act):
                for t in range(3):
                    if t < 2:
                        norm.act_stats(act, t)
                    if t:
                        norm.act_hi(act, t - 1)
                for n in range(SL):
                    k.ring.hi(act, first_unit + n, w_hi[:, n, :])
                for n in range(8):
                    for m in range(2):
                        g = 2 * n + m
                        act.wait_ge(mm_done, g + 1)
                        bank = ps[:, 2 + g % BK, 0:256]
                        if n < 4:
                            nc.scalar.copy(k.mk[:, 2 * n + m, :], bank).then_inc(evac, 1)
                        else:
                            nc.scalar.copy(k.mv[:, m, (n - 4) * 256:(n - 3) * 256], bank).then_inc(evac, 1)
                    if n + SL < 8:
                        k.ring.hi(act, first_unit + n + SL, w_hi[:, n % SL, :])

            @block.vector
            def _(dve):
                for t in range(3):
                    if t < 2:
                        norm.dve_rows(dve, t)
                    if t:
                        norm.dve_lo(dve, t - 1)
                for n in range(8):
                    if n >= SL:
                        dve.wait_ge(mm_done, 2 * (n - SL) + 2)
                    k.ring.lo(dve, first_unit + n, w_hi[:, n % SL, :], w_lo[:, n % SL, :])

            @block.tensor
            def _(pe):
                for t in range(2):
                    norm.pe_turn(pe, t)
                pe.wait_ge(norm.lo_done, 4)
                for n in range(8):
                    pe.wait_ge(k.ring.lo_done, first_unit + n + 1)
                    wh = w_hi[:, n % SL, :].rearrange("p (k c) -> p k c", k=KT)
                    wl = w_lo[:, n % SL, :].rearrange("p (k c) -> p k c", k=KT)
                    for m in range(2):
                        g = 2 * n + m
                        if g >= BK:
                            pe.wait_ge(evac, g - BK + 1)
                        out, c = ps[:, 2 + g % BK, 0:256], slice(m * P, (m + 1) * P)
                        for kk in range(KT):
                            if n < 4:
                                last = mm3(nc, out, wh[:, kk, c], wl[:, kk, c], m_hi[:, kk, :], m_lo[:, kk, :],
                                           kk == 0, kk == KT - 1)
                            else:
                                last = mm3(nc, out, m_hi[:, kk, c], m_lo[:, kk, c], wh[:, kk, :], wl[:, kk, :],
                                           kk == 0, kk == KT - 1)
                        last.then_inc(mm_done, 1)


def stage_residual(nc, k, name, x_from, x_to, gain_ap, first_unit, router=None):
    with Stage(nc) as ctx:
        def sb(nm, shape, dt=f32):
            return ctx.enter_context(nc.sbuf_tensor(f"{name}_{nm}", shape, dt))

        def sem(nm):
            return ctx.sem(f"{name}_{nm}")

        ps = k.ps
        w_hi, w_lo = sb("whi", [P, 4, UNIT], f32r), sb("wlo", [P, 4, UNIT], f32r)
        xt, gain = sb("xt", [P, 2, D]), sb("gain", [P, D])
        g_in, mm_done, sum_done = sem("g_in"), sem("mm"), sem("sum")
        x_in = [sem(f"x_in{i}") for i in range(2)]
        stored = [sem(f"stored{i}") for i in range(2)]
        rows_stored = [sem(f"rows_stored{i}") for i in range(2)]
        if router is not None:
            w_router, b_router = router
            ht = sb("ht", [P, 2, KT, P])
            wr, br = sb("wr", [P, KT, NE]), sb("br", [P, NE])
            zero = sb("zero", [P, D])
            r_in, zero_made, logit_done, bias_done = sem("r_in"), sem("zero_made"), sem("logit"), sem("biased")

        def summed(eng, t):
            eng.wait_ge(sum_done, 2 * t + 2)

        norm = RowNorm(nc, ctx, name, lambda t: xt[:, t % 2, :], summed, gain[:, :],
                       lambda e: e.wait_ge(g_in, 16), k.ident, k.eps, [ps[:, b, :] for b in range(2)],
                       lambda t, q: (k.act_hi[:, 4 * q:4 * q + 4, t * P:(t + 1) * P],
                                     k.act_lo[:, 4 * q:4 * q + 4, t * P:(t + 1) * P]),
                       hn_free=None if router is None else
                       (lambda e, t: e.wait_ge(rows_stored[t % 2], 16 * (t // 2 + 1))))

        with nc.Block() as block:
            @block.sync
            def _(sp):
                sp.dma_start(gain[:, :], gain_row(gain_ap)).then_inc(g_in, 16)
                if router is not None:
                    sp.wait_ge(zero_made, 1)
                    for spare in (x_to, k.h_rows):
                        sp.dma_start(spare[SEQ:SEQ + P, :], zero[:, :]).then_inc(r_in, 16)
                    sp.dma_start(wr[:, :, :], w_router[0].rearrange("(k p) n -> p k n", p=P)).then_inc(r_in, 16)
                    sp.dma_start(br[:, :], b_router[0, :].partition_broadcast(P)).then_inc(r_in, 16)
                for t in range(2):
                    sp.dma_start(xt[:, t, :], x_from[t * P:(t + 1) * P, :]).then_inc(x_in[t], 16)
                for n in range(first_unit + RAW, first_unit + 4 + RAW):
                    k.ring.load(sp, n)
                for t in range(TT):
                    summed(sp, t)
                    sp.dma_start(x_to[t * P:(t + 1) * P, :], xt[:, t % 2, :]).then_inc(stored[t % 2], 16)
                    sp.wait_ge(norm.rows_done, t + 1)
                    if router is not None:
                        sp.dma_start(k.h_rows[t * P:(t + 1) * P, :], norm.hn[:, t % 2, :]
                                     ).then_inc(rows_stored[t % 2], 16)
                    if t + 2 < TT:
                        sp.wait_ge(norm.sumsq_done, t + 1)
                        sp.wait_ge(stored[t % 2], 16 * (t // 2 + 1))
                        sp.dma_start(xt[:, t % 2, :], x_from[(t + 2) * P:(t + 3) * P, :]
                                     ).then_inc(x_in[t % 2], 16)
                for b in range(2):
                    sp.wait_ge(stored[b], 16 * (TT // 2))
                    if router is not None:
                        sp.wait_ge(rows_stored[b], 16 * (TT // 2))

            @block.gpsimd
            def _(pool):
                if router is not None:
                    nc.gpsimd.memset(zero[:, :], 0.0).then_inc(zero_made, 1)

            @block.scalar
            def _(act):
                for n in range(4):
                    k.ring.hi(act, first_unit + n, w_hi[:, n, :])
                for t in range(TT + 1):
                    if t < TT:
                        norm.act_stats(act, t)
                    if t and router is None:
                        norm.act_hi(act, t - 1)
                    elif t:
                        for q in range(2):
                            act.wait_ge(norm.turned, 2 * (t - 1) + q + 1)
                            if t >= 3:
                                act.wait_ge(logit_done, t - 2)
                            nc.scalar.copy(ht[:, (t - 1) % 2, 4 * q:4 * q + 4, :], norm.bank(t - 1, q)
                                           ).then_inc(norm.lo_done, 1)

            @block.vector
            def _(dve):
                for n in range(4):
                    k.ring.lo(dve, first_unit + n, w_hi[:, n, :], w_lo[:, n, :])
                for t in range(TT + 1):
                    if t < TT:
                        dve.wait_ge(x_in[t % 2], 16 * (t // 2 + 1))
                        for nh in range(2):
                            g = 2 * t + nh
                            dve.wait_ge(mm_done, g + 1)
                            half = xt[:, t % 2, nh * N:(nh + 1) * N]
                            nc.vector.tensor_tensor(half, ps[:, 2 + g % 4, :], half, ALU.add
                                                    ).then_inc(sum_done, 1)
                        norm.dve_rows(dve, t)
                    if t and router is None:
                        norm.dve_lo(dve, t - 1)
                if router is not None:
                    dve.wait_ge(r_in, 64)
                    dve.wait_ge(logit_done, TT)
                    nc.vector.tensor_tensor(
                        k.logits[:, :, :], ps[:, 6, 0:TT * NE].rearrange("p (t e) -> p t e", e=NE),
                        br[:, :].unsqueeze(1).broadcast_to((P, TT, NE)), ALU.add).then_inc(bias_done, 1)

            @block.tensor
            def _(pe):
                pe.wait_ge(k.ring.lo_done, first_unit + 4)
                for t in range(TT + 2):
                    if t < TT:
                        tok = slice(t * P, (t + 1) * P)
                        for nh in range(2):
                            g = 2 * t + nh
                            if g >= 4:
                                pe.wait_ge(sum_done, g - 3)
                            for kk in range(KT):
                                u = 2 * nh + kk // 4
                                c = slice((kk % 4) * N, (kk % 4 + 1) * N)
                                last = mm3(nc, ps[:, 2 + g % 4, :], k.act_hi[:, kk, tok], k.act_lo[:, kk, tok],
                                           w_hi[:, u, c], w_lo[:, u, c], kk == 0, kk == KT - 1)
                            last.then_inc(mm_done, 1)
                    if 1 <= t <= TT:
                        norm.pe_turn(pe, t - 1)
                    if router is not None and t >= 2:
                        if t == 2:
                            pe.wait_ge(r_in, 64)
                        pe.wait_ge(norm.lo_done, 2 * (t - 1))
                        for kk in range(KT):
                            last = nc.tensor.matmul(ps[:, 6, (t - 2) * NE:(t - 1) * NE], ht[:, (t - 2) % 2, kk, :],
                                                    wr[:, kk, :], start=(kk == 0), stop=(kk == KT - 1))
                        last.then_inc(logit_done, 1)


def stage_cross(nc, k, first_unit):
    with Stage(nc) as ctx:
        def sb(nm, shape, dt=f32):
            return ctx.enter_context(nc.sbuf_tensor(f"x_{nm}", shape, dt))

        def sem(nm):
            return ctx.sem(f"x_{nm}")

        ps = k.ps
        SL, BK = 2, 4
        w_hi, w_lo = sb("whi", [P, SL, UNIT], f32r), sb("wlo", [P, SL, UNIT], f32r)
        qt = sb("qt", [P, KT, SEQ])
        p = sb("p", [P, 2, MEM])
        pt = sb("pt", [P, 2, 2, N])
        st = sb("st", [P, 4, XH * TT])
        mm_done, evac, sc_done, max_done, nm_done, exp_done, inv_done, p_done, turned, pt_done, o_done, \
            hi_done, lo_done = (sem(s) for s in ("mm", "evac", "sc", "max", "nm", "exp", "inv", "p", "turned",
                                                 "pt", "o", "hi", "lo"))
        steps = [(h, t) for h in range(XH) for t in range(TT)]
        NSX = len(steps)
        scale = XD ** -0.5

        with nc.Block() as block:
            @block.sync
            def _(sp):
                for n in range(first_unit + RAW, first_unit + 4 + RAW):
                    k.ring.load(sp, n)

            @block.scalar
            def _(act):
                for n in range(SL):
                    k.ring.hi(act, first_unit + n, w_hi[:, n, :])
                for n in range(4):
                    for m in range(4):
                        g = 4 * n + m
                        act.wait_ge(mm_done, g + 1)
                        nc.scalar.copy(qt[:, 2 * n + m // 2, (m % 2) * N:(m % 2 + 1) * N], ps[:, g % BK, :]
                                       ).then_inc(evac, 1)
                    if n + SL < 4:
                        k.ring.hi(act, first_unit + n + SL, w_hi[:, n % SL, :])
                for i in range(NSX + 2):
                    if i < NSX:
                        act.wait_ge(nm_done, i + 1)
                        if i >= 2:
                            act.wait_ge(turned, i - 1)
                        nc.scalar.activation(p[:, i % 2, :], ps[:, 4 + i % 2, 0:MEM], ACT.Exp, scale=scale,
                                             bias=st[:, 1, i:i + 1], accum_out=st[:, 2, i:i + 1]
                                             ).then_inc(exp_done, 1)
                    n = i - 1
                    if 0 <= n < NSX:
                        h, t = steps[n]
                        u = n // 4
                        act.wait_ge(turned, n + 1)
                        if u >= 2:
                            act.wait_ge(o_done, 2 * (u - 1))
                        nc.scalar.copy(pt[:, u % 2, :, (t % 4) * P:(t % 4 + 1) * P],
                                       ps[:, 6 + n % 2, 0:MEM].rearrange("p (m c) -> p m c", m=2)
                                       ).then_inc(pt_done, 1)
                    n = i - 2
                    if 0 <= n < NSX and n % 4 == 3:
                        u = n // 4
                        h, th = u // 2, u % 2
                        for d in range(2):
                            g = 2 * u + d
                            act.wait_ge(o_done, g + 1)
                            nc.scalar.copy(k.act_hi[:, 2 * h + d, th * N:(th + 1) * N], ps[:, g % 4, :]
                                           ).then_inc(hi_done, 1)

            @block.vector
            def _(dve):
                for n in range(4):
                    if n >= SL:
                        dve.wait_ge(mm_done, 4 * (n - SL + 1))
                    k.ring.lo(dve, first_unit + n, w_hi[:, n % SL, :], w_lo[:, n % SL, :])
                for i in range(NSX + 2):
                    if i < NSX:
                        dve.wait_ge(sc_done, i + 1)
                        nc.vector.reduce_max(st[:, 0, i:i + 1], ps[:, 4 + i % 2, 0:MEM], AX).then_inc(max_done, 1)
                        dve.wait_ge(max_done, i + 1)
                        nc.vector.tensor_scalar(st[:, 1, i:i + 1], st[:, 0, i:i + 1], -scale, None, ALU.mult
                                                ).then_inc(nm_done, 1)
                        dve.wait_ge(exp_done, i + 1)
                        nc.vector.reciprocal(st[:, 3, i:i + 1], st[:, 2, i:i + 1]).then_inc(inv_done, 1)
                        dve.wait_ge(inv_done, i + 1)
                        nc.vector.tensor_scalar(p[:, i % 2, :], p[:, i % 2, :], st[:, 3, i:i + 1], None, ALU.mult
                                                ).then_inc(p_done, 1)
                    n = i - 2
                    if 0 <= n < NSX and n % 4 == 3:
                        u = n // 4
                        h, th = u // 2, u % 2
                        for d in range(2):
                            g = 2 * u + d
                            c = slice(th * N, (th + 1) * N)
                            dve.wait_ge(hi_done, g + 1)
                            nc.vector.tensor_tensor(k.act_lo[:, 2 * h + d, c], ps[:, g % 4, :],
                                                    k.act_hi[:, 2 * h + d, c].bitcast(f32), ALU.subtract
                                                    ).then_inc(lo_done, 1)

            @block.tensor
            def _(pe):
                for n in range(4):
                    pe.wait_ge(k.ring.lo_done, first_unit + n + 1)
                    wh = w_hi[:, n % SL, :].rearrange("p (k c) -> p k c", k=KT)
                    wl = w_lo[:, n % SL, :].rearrange("p (k c) -> p k c", k=KT)
                    for m in range(4):
                        g = 4 * n + m
                        if g >= BK:
                            pe.wait_ge(evac, g - BK + 1)
                        c, tok = slice((m // 2) * P, (m // 2 + 1) * P), slice((m % 2) * N, (m % 2 + 1) * N)
                        for kk in range(KT):
                            last = mm3(nc, ps[:, g % BK, :], wh[:, kk, c], wl[:, kk, c], k.act_hi[:, kk, tok],
                                       k.act_lo[:, kk, tok], kk == 0, kk == KT - 1)
                        last.then_inc(mm_done, 1)
                pe.wait_ge(evac, 16)
                for i in range(NSX + 2):
                    if i < NSX:
                        h, t = steps[i]
                        if i >= 2:
                            pe.wait_ge(exp_done, i - 1)
                        for d in range(2):
                            last = nc.tensor.matmul(ps[:, 4 + i % 2, 0:MEM], qt[:, 2 * h + d, t * P:(t + 1) * P],
                                                    k.mk[:, 2 * h + d, :], start=(d == 0), stop=(d == 1))
                        last.then_inc(sc_done, 1)
                    n = i - 1
                    if 0 <= n < NSX:
                        pe.wait_ge(p_done, n + 1)
                        if n >= 2:
                            pe.wait_ge(pt_done, n - 1)
                        for m in range(2):
                            last = nc.tensor.transpose(ps[:, 6 + n % 2, m * P:(m + 1) * P],
                                                       p[:, n % 2, m * P:(m + 1) * P], k.ident[:, :])
                        last.then_inc(turned, 1)
                    n = i - 2
                    if 0 <= n < NSX and n % 4 == 3:
                        u = n // 4
                        h = u // 2
                        pe.wait_ge(pt_done, n + 1)
                        for d in range(2):
                            g = 2 * u + d
                            if g >= 4:
                                pe.wait_ge(lo_done, g - 3)
                            for m in range(2):
                                last = nc.tensor.matmul(ps[:, g % 4, :],
                                                        k.mv[:, m, h * XD + d * P:h * XD + (d + 1) * P],
                                                        pt[:, u % 2, m, :], start=(m == 0), stop=(m == 1))
                            last.then_inc(o_done, 1)


def expert_unit(w, n):
    c, h = n // 2, n % 2
    return w.rearrange("o (k p) n -> (o p) k n", p=P)[:, 4 * h:4 * h + 4, c * N:(c + 1) * N]


def stage_routing(nc, k, w_gate_up, b_gate_up, b_down):
    with Stage(nc) as ctx:
        def sb(nm, shape, dt=f32):
            return ctx.enter_context(nc.sbuf_tensor(f"r_{nm}", shape, dt))

        def sem(nm):
            return ctx.sem(f"r_{nm}")

        ps = k.ps
        Q = TT * TOPK
        ITEMS = MAX_ITEMS + 1
        best, besti = sb("best", [P, TT, 8]), sb("besti", [P, TT, 8], u32)
        idf, rel, ex = sb("idf", [P, TT, TOPK]), sb("rel", [P, TT, TOPK]), sb("ex", [P, TT, TOPK])
        tot, inv = sb("tot", [P, TT]), sb("inv", [P, TT])
        count_row = sb("count_row", [P, CAP])
        part = sb("part", [P, 1])
        mult_row = sb("mult_row", [P, 8])
        tokid = sb("tokid", [P, Q])
        hot = sb("hot", [P, TT, TOPK, NE])
        pick = sb("pick", [P, TT, TOPK, NE])
        member = sb("member", [P, TT, NE])
        upper, ones = sb("upper", [P, P]), sb("ones", [P, P])
        base = sb("base", [P, TT + 1, NE])
        pos = sb("pos", [P, TT, NE])
        cmp8 = sb("cmp8", [P, NE, 8])
        one32 = sb("one32", [P, NE])
        some, nitem, end_i, start_i = (sb(s, [P, NE]) for s in ("some", "nitem", "end_i", "start_i"))
        posj, startj, pb, off, itemj = (sb(s, [P, Q]) for s in ("posj", "startj", "pb", "off", "itemj"))
        cmpq = sb("cmpq", [P, Q, 8])
        in_item = sb("in_item", [P, Q, ITEMS])
        worth = sb("worth", [P, Q, 2, ITEMS])
        spare = sb("spare", [P, ITEMS, 2])
        in_off = sb("in_off", [P, Q, CAP])
        cmpe = sb("cmpe", [P, NE])
        ie, ie3 = sb("ie", [P, 1]), sb("ie3", [P, 3, NE])
        t32 = sb("t32", [P, NE])
        fields = sb("fields", [P, 8])
        si, ni, ji, left = (sb(s, [P, 1]) for s in ("si", "ni", "ji", "left"))
        fi = sb("fi", [P, 8], i32)
        b_left, b_part = sb("b_left", [NE, 3 * D]), sb("b_part", [NE, D], bf16)
        b_in, b_copied, b_less = sem("b_in"), sem("b_copied"), sem("b_less")
        w_in = [sem(f"w_in{s}") for s in range(RAW)]
        w_hi_done, w_lo_done = sem("w_hi"), sem("w_lo")
        v, made, ex_done, mm_done, table_io = sem("v"), sem("made"), sem("ex"), sem("mm"), sem("table_io")
        marks = {}

        def bc(ap, shape, *dims):
            for d in dims:
                ap = ap.unsqueeze(d)
            return ap.broadcast_to(shape)

        with nc.Block() as block:
            @block.gpsimd
            def _(pool):
                nc.gpsimd.iota(count_row[:, :], [[1, CAP]], base=0, channel_multiplier=0,
                               allow_small_or_imprecise_dtypes=True).then_inc(made, 1)
                nc.gpsimd.iota(part[:, :], [[0, 1]], base=0, channel_multiplier=1,
                               allow_small_or_imprecise_dtypes=True).then_inc(made, 1)
                nc.gpsimd.iota(mult_row[:, :], [[CAP, 8]], base=0, channel_multiplier=0,
                               allow_small_or_imprecise_dtypes=True).then_inc(made, 1)
                nc.gpsimd.iota(tokid[:, :], [[P, TT], [0, TOPK]], base=-SEQ, channel_multiplier=1,
                               allow_small_or_imprecise_dtypes=True).then_inc(made, 1)
                nc.gpsimd.memset(ones[:, :], 1.0).then_inc(made, 1)
                nc.gpsimd.memset(one32[:, :], 1.0).then_inc(made, 1)
                pool.wait_ge(made, 6)
                nc.gpsimd.affine_select(out=upper[:, :], in_=ones[:, :], compare_op=ALU.is_ge, fill=0.0, base=-1,
                                        pattern=[[1, P]], channel_multiplier=-1).then_inc(made, 1)
                for c in range(3):
                    for p, part_ in enumerate((k.bias[0:NE, c * D:(c + 1) * D], b_part[:, :])):
                        pool.wait_ge(b_copied, 4 * c + 1 + 2 * p)
                        nc.gpsimd.tensor_tensor(b_left[:, c * D:(c + 1) * D], b_left[:, c * D:(c + 1) * D], part_, ALU.subtract
                                                ).then_inc(b_less, 1)

            @block.vector
            def _(dve):
                n = [0]

                def step(ins, mark=None):
                    n[0] += 1
                    ins.then_inc(v, 1)
                    dve.wait_ge(v, n[0])
                    if mark:
                        marks[mark] = n[0]

                V = nc.vector

                def split_lo(u):
                    dve.wait_ge(w_hi_done, u + 1)
                    V.tensor_tensor(k.w_lo[:, u, :], k.ring.raw[:, u, :], k.w_hi[:, u, :].bitcast(f32), ALU.subtract
                                    ).then_inc(w_lo_done, 1)

                step(V.memset(fields[:, :], 0.0))
                for t in range(TT):
                    step(V.max(best[:, t, :], k.logits[:, t, :]))
                    step(V.max_index(besti[:, t, :], best[:, t, :], k.logits[:, t, :]))
                step(V.tensor_tensor(rel[:, :, :], best[:, :, 0:TOPK],
                                     best[:, :, 0:1].broadcast_to((P, TT, TOPK)), ALU.subtract), "rel")
                step(V.tensor_copy(idf[:, :, :], besti[:, :, 0:TOPK]))
                dve.wait_ge(made, 7)
                step(V.tensor_tensor(hot[:, :, :, :].rearrange("p t j e -> p (t j) e"),
                                     bc(count_row[:, 0:NE], (P, Q, NE), 1),
                                     bc(idf[:, :, :].rearrange("p t j -> p (t j)"), (P, Q, NE), 2), ALU.is_equal))
                step(V.tensor_tensor(member[:, :, :], hot[:, :, 0, :], hot[:, :, 1, :], ALU.add))
                for j in range(2, TOPK):
                    step(V.tensor_tensor(member[:, :, :], member[:, :, :], hot[:, :, j, :], ALU.add))
                marks["member"] = n[0]
                dve.wait_ge(ex_done, 1)
                step(V.tensor_reduce(tot[:, :], ex[:, :, :], AX, ALU.add))
                step(V.reciprocal(inv[:, :], tot[:, :]))
                step(V.tensor_tensor(k.gates[:, :, :], ex[:, :, :], bc(inv[:, :], (P, TT, TOPK), 2), ALU.mult))
                dve.wait_ge(mm_done, 2)
                total = ps[:, 1, 0:TT * NE].rearrange("p (t e) -> p t e", e=NE)
                before = ps[:, 0, 0:TT * NE].rearrange("p (t e) -> p t e", e=NE)
                step(V.memset(base[:, 0, :], 0.0))
                for t in range(TT):
                    step(V.tensor_tensor(base[:, t + 1, :], base[:, t, :], total[:, t, :], ALU.add))
                step(V.tensor_tensor(pos[:, :, :], before, base[:, 0:TT, :], ALU.add))
                counts = base[:, TT, :]
                step(V.tensor_scalar(some[:, :], counts, 1.0, None, ALU.max))
                step(V.tensor_tensor(cmp8[:, :, :], bc(some[:, :], (P, NE, 8), 2), bc(mult_row[:, :], (P, NE, 8), 1),
                                     ALU.is_gt))
                step(V.tensor_reduce(nitem[:, :], cmp8[:, :, :], AX, ALU.add))
                step(V.tensor_tensor_scan(end_i[:, :], one32[:, :], nitem[:, :], 0.0, ALU.mult, ALU.add))
                step(V.tensor_tensor(start_i[:, :], end_i[:, :], nitem[:, :], ALU.subtract))
                pk = pick[:, :, :, :]
                pk3 = pk.rearrange("p t j e -> p (t j) e")
                for j in range(TOPK):
                    step(V.tensor_tensor(pick[:, :, j, :], hot[:, :, j, :], pos[:, :, :], ALU.mult))
                step(V.tensor_reduce(posj[:, :], pk3, AX, ALU.add))
                step(V.tensor_tensor(pk3, hot[:, :, :, :].rearrange("p t j e -> p (t j) e"),
                                     bc(start_i[:, :], (P, Q, NE), 1), ALU.mult))
                step(V.tensor_reduce(startj[:, :], pk3, AX, ALU.add))
                step(V.tensor_tensor(cmpq[:, :, :], bc(posj[:, :], (P, Q, 8), 2), bc(mult_row[:, :], (P, Q, 8), 1),
                                     ALU.is_ge))
                step(V.tensor_reduce(pb[:, :], cmpq[:, :, :], AX, ALU.add))
                step(V.tensor_scalar(pb[:, :], pb[:, :], -1.0, None, ALU.add))
                step(V.scalar_tensor_tensor(out=off[:, :], in0=pb[:, :], scalar=-float(CAP), in1=posj[:, :],
                                            op0=ALU.mult, op1=ALU.add))
                step(V.tensor_tensor(itemj[:, :], pb[:, :], startj[:, :], ALU.add))
                for h in range(0, Q, Q // 4):
                    q4 = slice(h, h + Q // 4)
                    off4, item4, tok4, gate4 = (ap[:, q4] for ap in (
                        off, itemj, tokid, k.gates[:, :, :].rearrange("p t j -> p (t j)")))
                    wide, narrow = (P, Q // 4, CAP), (P, Q // 4, ITEMS)
                    V.tensor_tensor(in_off[:, q4, :], bc(count_row[:, :], wide, 1), bc(off4, wide, 2), ALU.is_equal)
                    step(V.tensor_tensor(in_item[:, q4, :], bc(count_row[:, 0:ITEMS], narrow, 1),
                                         bc(item4, narrow, 2), ALU.is_equal))
                    V.tensor_tensor(worth[:, q4, 0, :], in_item[:, q4, :], bc(tok4, narrow, 2), ALU.mult)
                    step(V.tensor_tensor(worth[:, q4, 1, :], in_item[:, q4, :], bc(gate4, narrow, 2), ALU.mult),
                         f"worth{h}")
                step(V.tensor_scalar(cmpe[:, :], end_i[:, :], part[:, 0:1], None, ALU.is_le))
                step(V.tensor_reduce(ie[:, :], cmpe[:, :], AX, ALU.add))
                step(V.tensor_tensor(ie3[:, :, :], bc(count_row[:, 0:NE], (P, 3, NE), 1),
                                     bc(ie[:, 0:1], (P, 3, NE), 2), ALU.is_equal), "ie3")
                for row, got in ((start_i[:, :], si), (counts, ni)):
                    step(V.tensor_tensor(t32[:, :], ie3[:, 0, :], row, ALU.mult))
                    step(V.tensor_reduce(got[:, :], t32[:, :], AX, ALU.add))
                step(V.tensor_tensor(ji[:, :], part[:, :], si[:, :], ALU.subtract))
                step(V.scalar_tensor_tensor(out=left[:, :], in0=ji[:, :], scalar=-float(CAP), in1=ni[:, :], op0=ALU.mult,
                                            op1=ALU.add))
                step(V.tensor_scalar(fields[:, 0:1], ie[:, :], float(NE - 1), None, ALU.min))
                step(V.tensor_scalar(fields[:, 1:2], left[:, :], float(BLOCK), None, ALU.is_gt))
                step(V.tensor_copy(fields[:, 2:3], end_i[:, NE - 1:NE]))
                step(V.tensor_copy(fi[:, :], fields[:, :]), "fields")
                for u in range(SOME_LO):
                    split_lo(u)
                dve.wait_ge(mm_done, 3)
                step(V.memset(k.rows[:, :, 1], 0))
                step(V.memset(k.slot_gate[:, :, 1], 0))
                for b, n_at in ((0, BLOCK), (1, REST)):
                    token, gate = (ps[0:n_at, 2 + b, c * ITEMS:(c + 1) * ITEMS] for c in range(2))
                    step(V.tensor_copy(k.slot_gate[0:n_at, :, b], gate))
                    step(V.tensor_scalar(spare[0:n_at, :, b], token, 0.0, part[0:n_at, 0:1], ALU.is_ge, ALU.mult))
                    step(V.scalar_tensor_tensor(out=k.rows[0:n_at, :, b], in0=token, scalar=float(SEQ),
                                                in1=spare[0:n_at, :, b], op0=ALU.add, op1=ALU.add))
                dve.wait_ge(mm_done, 4)
                step(V.tensor_copy(k.sel[:, :], ps[0:3 * NE, 4, 0:P]))

            @block.tensor
            def _(pe):
                pe.wait_ge(made, 7)
                pe.wait_ge(v, marks["member"])
                m = member[:, :, :].rearrange("p t e -> p (t e)")
                nc.tensor.matmul(ps[:, 0, 0:TT * NE], upper[:, :], m, start=True, stop=True).then_inc(mm_done, 1)
                nc.tensor.matmul(ps[:, 1, 0:TT * NE], ones[:, :], m, start=True, stop=True).then_inc(mm_done, 1)
                for q in range(Q):
                    if q % (Q // 4) == 0:
                        pe.wait_ge(v, marks[f"worth{q}"])
                    for b, at in ((0, slice(0, BLOCK)), (1, slice(BLOCK, CAP))):
                        last = nc.tensor.matmul(ps[0:at.stop - at.start, 2 + b, 0:2 * ITEMS], in_off[:, q, at],
                                                worth[:, q, :, :].rearrange("p a b -> p (a b)"), start=(q == 0),
                                                stop=(q == Q - 1))
                last.then_inc(mm_done, 1)
                pe.wait_ge(v, marks["ie3"])
                nc.tensor.transpose(ps[0:3 * NE, 4, 0:P], ie3[:, :, :].rearrange("p a e -> p (a e)"), k.ident[:, :]
                                    ).then_inc(mm_done, 1)

            @block.scalar
            def _(act):
                nc.scalar.preload_act_table_set("natural_log_exp_and_others")

                def biases(c):
                    cols, n = slice(c * D, (c + 1) * D), 4 * c
                    nc.scalar.copy(k.bias[0:NE, cols], b_left[:, c * D:(c + 1) * D]).then_inc(b_copied, 1)
                    act.wait_ge(b_less, 2 * c + 1)
                    nc.scalar.copy(b_part[:, :], b_left[:, c * D:(c + 1) * D]).then_inc(b_copied, 1)
                    act.wait_ge(b_copied, n + 2)
                    nc.scalar.copy(k.bias[NE:2 * NE, cols], b_part[:, :]).then_inc(b_copied, 1)
                    act.wait_ge(b_less, 2 * c + 2)
                    nc.scalar.copy(k.bias[2 * NE:3 * NE, cols], b_left[:, c * D:(c + 1) * D]).then_inc(b_copied, 1)

                def split_hi(u):
                    act.wait_ge(w_in[u], 16)
                    nc.scalar.copy(k.w_hi[:, u, :], k.ring.raw[:, u, :]).then_inc(w_hi_done, 1)

                act.wait_ge(v, marks["rel"])
                nc.scalar.activation(ex[:, :, :], rel[:, :, :], ACT.Exp).then_inc(ex_done, 1)
                act.wait_ge(b_in, 32)
                for u in range(RAW):
                    split_hi(u)
                    if u < 3:
                        biases(u)

            @block.sync
            def _(sp):
                for u in range(RAW):
                    sp.dma_start(k.ring.raw[:, u, :].rearrange("p (k c) -> p k c", k=4),
                                 expert_unit(w_gate_up[0, 0:1], u)).then_inc(w_in[u], 16)
                    if u == 0:
                        sp.dma_start(b_left[:, 0:2 * D], b_gate_up[0]).then_inc(b_in, 16)
                        sp.dma_start(b_left[:, 2 * D:3 * D], b_down[0]).then_inc(b_in, 16)
                sp.wait_ge(v, marks["fields"])
                sp.dma_start(k.table_dram, fi[:, :]).then_inc(table_io, 16)
                sp.wait_ge(table_io, 16)
                sp.dma_start(k.table[0:1, :], k.table_dram.rearrange("(o i) f -> o (i f)", o=1)).then_inc(table_io, 16)
                sp.wait_ge(table_io, 32)


E_FIELD, REST_FIELD, N_FIELD = range(3)


def stage_experts(nc, k, x_acc, w_gate_up, w_down):
    with Stage(nc) as ctx:
        def sb(nm, shape, dt=f32):
            return ctx.enter_context(nc.sbuf_tensor(f"e_{nm}", shape, dt))

        def sem(nm):
            return ctx.sem(f"e_{nm}")

        ps = k.ps
        NR, NS, NU = 6, 6, 12
        ROWS = (BLOCK, REST)
        B_HI, R_HI = slice(0, BLOCK), slice(BLOCK, CAP)
        R_LO, B_LO = slice(CAP, CAP + REST), slice(CAP + REST, 2 * CAP)
        R_BOTH = slice(BLOCK, CAP + REST)
        bias = k.bias
        xp, ap_ = sb("x_parts", [P, KT, 2 * CAP], f32r), sb("a_parts", [P, KT, 2 * CAP], f32r)
        fold = sb("fold", [REST, N])
        xg = sb("xg", [P, 2, D])
        ridx, sidx = sb("ridx", [P, 2], i32), sb("sidx", [P, 2], i32)
        y = sb("y", [P, 2, D])
        gt, up, sg = sb("gt", [P, 2, 2, 256]), sb("up", [P, 2, 256]), sb("sg", [P, 2, 256])
        sel = sb("sel", [3 * NE, P], bf16)
        more_raw = sb("more_raw", [P, NR - RAW, UNIT])
        more_hi, more_lo = (sb(f"more_{s}", [P, NS - n, UNIT], f32r) for s, n in (("hi", RAW), ("lo", SOME_LO)))
        raws, w_hi, w_lo = ([a[:, s, :] if s < n else b[:, s - n, :] for s in range(m)] for a, b, n, m in (
            (k.ring.raw, more_raw, RAW, NR), (k.w_hi, more_hi, RAW, NS), (k.w_lo, more_lo, SOME_LO, NS)))

        w_in = [sem(f"w_in{s}") for s in range(NR)]
        hi_done, lo_done, chunk_done, up_free, y_free = (sem(s) for s in ("w_hi", "w_lo", "chunk", "up_free", "y_free"))
        g_done, sg_done, t_done, a_done = (sem(s) for s in ("gate", "sigmoid", "prod", "act"))
        at_turned, at_hi, at_lo = sem("at_turned"), sem("at_hi"), sem("at_lo")
        x_in, ridx_done, xt_turned, xt_hi, xt_lo = (sem(s) for s in ("x_in", "ridx", "xt_turned", "xt_hi", "xt_lo"))
        sel_done, sidx_done, added, folded = sem("sel"), sem("sidx"), sem("added"), sem("folded")
        y_taken, halved = sem("y_taken"), sem("halved")
        xg_made = sem("xg_made")
        sp_passed, pool_passed, act_passed = sem("sp_passed"), sem("pool_passed"), sem("act_passed")

        def field(eng, i, f, top):
            return eng.value_load(k.table[0:1, bass.ds(i * 8 + f, 1)], min_val=0, max_val=top)

        def n_items(eng):
            return eng.value_load(k.table[0:1, N_FIELD:N_FIELD + 1], min_val=1, max_val=MAX_ITEMS)

        def load(sp, e, u):
            if u < 8:
                src = expert_unit(w_gate_up[0, bass.ds(e, 1)], u)
            else:
                src = expert_unit(w_down[0, bass.ds(e, 1)], u - 8)
            sp.dma_start(raws[u % NR].rearrange("p (k c) -> p k c", k=4), src).then_inc(w_in[u % NR], 16)

        def split_hi(act, i, u):
            act.wait_ge(w_in[u % NR], 16 * (NU // NR * i + u // NR + 1))
            nc.scalar.copy(w_hi[u % NS], raws[u % NR]).then_inc(hi_done, 1)

        def split_lo(dve, i, u):
            dve.wait_ge(hi_done, NU * i + u + 1)
            nc.vector.tensor_tensor(w_lo[u % NS], raws[u % NR], w_hi[u % NS].bitcast(f32),
                                    ALU.subtract).then_inc(lo_done, 1)

        def x_bank(q):
            return ps[:, 6 + q % 2, 0:2 * CAP].rearrange("p (k c) -> p k c", k=2)

        def a_bank(c):
            return ps[:, 4 + c % 2, 0:2 * CAP].rearrange("p (k c) -> p k c", k=2)

        def x_turn(pe, j, q):
            if q == 0:
                pe.wait_ge(x_in, 32 * (j + 1))
            pe.wait_ge(xt_lo, 4 * j + q + 1)
            for kk in range(2):
                c = (2 * q + kk) * P
                nc.tensor.transpose(x_bank(q)[:, kk, 0:BLOCK], xg[:, 0, c:c + P], k.ident[:, :])
                last = nc.tensor.transpose(x_bank(q)[:, kk, BLOCK:CAP], xg[0:REST, 1, c:c + P],
                                           k.ident[0:REST, 0:REST])
            last.then_inc(xt_turned, 1)

        def x_hi_part(act, j, q):
            act.wait_ge(xt_turned, 4 * j + q + 1)
            nc.scalar.copy(xp[:, 2 * q:2 * q + 2, 0:CAP], x_bank(q)).then_inc(xt_hi, 1)

        def low_parts(parts, q, bank, nb):
            for hi, lo in ((R_HI, R_LO), (B_HI, B_LO))[2 - nb:]:
                last = nc.vector.tensor_tensor(parts[:, 2 * q:2 * q + 2, lo], bank[:, :, hi],
                                               parts[:, 2 * q:2 * q + 2, hi].bitcast(f32), ALU.subtract)
            return last

        def x_lo_part(dve, j, q):
            dve.wait_ge(xt_hi, 4 * j + q + 1)
            low_parts(xp, q, x_bank(q), 2).then_inc(xt_lo, 1)

        def a_hi_part(act, i, c, nb):
            act.wait_ge(at_turned, 4 * i + c + 1)
            w = CAP if nb == 2 else BLOCK
            nc.scalar.copy(ap_[:, 2 * c:2 * c + 2, 0:w], a_bank(c)[:, :, 0:w]).then_inc(at_hi, 1)

        def a_lo_part(dve, i, c, nb):
            dve.wait_ge(at_hi, 4 * i + c + 1)
            low_parts(ap_, c, a_bank(c), nb).then_inc(at_lo, 1)

        def each_size(eng, rest, body):
            with eng.If(rest > 0):
                body(2)
            with eng.Else():
                body(1)

        with nc.Block() as block:
            @block.sync
            def _(sp):
                for u in range(RAW):
                    sp.sem_inc(w_in[u], 16)
                load(sp, 0, RAW)
                sp.wait_ge(x_in, 32)
                load(sp, 0, RAW + 1)
                items = n_items(sp)
                with sp.Fori(0, items) as i:
                    e = field(sp, i, E_FIELD, NE - 1)
                    e_next = field(sp, i + 1, E_FIELD, NE - 1)
                    for u in range(NU):
                        sp.wait_ge(lo_done, NU * i + u + 1)
                        load(sp, e if u + NR < NU else e_next, (u + NR) % NU)
                for u in range(NR):
                    sp.wait_ge(w_in[u], items * (16 * (NU // NR)) + 16)
                    sp.sem_inc(sp_passed, 1)

            @block.gpsimd
            def _(pool):
                def fetch_rows(j):
                    rest = field(pool, j, REST_FIELD, 1)
                    nc.gpsimd.tensor_copy(ridx[:, :].unsqueeze(1), k.rows[:, bass.ds(j, 1), :]).then_inc(ridx_done, 1)
                    pool.wait_ge(ridx_done, j + 1)
                    pool.sem_inc(pool_passed, 1)

                    def gather(b, inc):
                        nc.gpsimd.indirect_dma_start(
                            out=xg[0:ROWS[b], b, :], out_offset=None, in_=k.h_rows,
                            in_offset=bass.IndirectOffsetOnAxis(ap=ridx[0:ROWS[b], b:b + 1], axis=0)
                        ).then_inc(x_in, inc)

                    def body(nb):
                        for b in range(nb):
                            gather(b, 32 // nb)

                    each_size(pool, rest, body)

                pool.sem_inc(a_done, 1)
                pool.sem_inc(y_taken, 1)
                pool.wait_ge(xg_made, 1)
                fetch_rows(0)
                items = n_items(pool)
                with pool.Fori(0, items) as i:
                    rest = field(pool, i, REST_FIELD, 1)

                    def activations(c, nb):
                        pool.wait_ge(sg_done, 4 * i + c + 1)
                        pool.wait_ge(t_done, 4 * i + c + 1)
                        nc.gpsimd.tensor_tensor(gt[:, c % 2, 0:nb, :], up[:, 0:nb, :], sg[:, 0:nb, :],
                                                ALU.mult).then_inc(a_done, 1)

                    each_size(pool, rest, lambda nb: activations(0, nb))
                    pool.wait_ge(xt_turned, 4 * i + 4)
                    pool.sem_inc(pool_passed, 1)
                    fetch_rows(i + 1)

                    def body(nb):
                        for c in range(1, 4):
                            activations(c, nb)
                        nc.gpsimd.tensor_copy(sidx[:, :].unsqueeze(1), k.rows[:, bass.ds(i, 1), :]).then_inc(sidx_done, 1)
                        pool.wait_ge(y_free, 2 * i + 4)
                        pool.sem_inc(pool_passed, 1)
                        pool.wait_ge(sidx_done, i + 1)
                        pool.sem_inc(pool_passed, 1)
                        for b in range(nb):
                            nc.gpsimd.indirect_dma_start(
                                out=x_acc,
                                out_offset=bass.IndirectOffsetOnAxis(ap=sidx[0:ROWS[b], b:b + 1], axis=0),
                                in_=y[0:ROWS[b], b, :], in_offset=None, compute_op=ALU.add).then_inc(added, 32 // nb)
                        pool.wait_ge(added, 32 * i + 32)
                        pool.sem_inc(y_taken, 1)

                    each_size(pool, rest, body)
                pool.wait_ge(x_in, items * 32 + 32)
                pool.sem_inc(pool_passed, 1)

            @block.scalar
            def _(act):
                nc.scalar.preload_act_table_set("sigmoid_and_others")
                act.sem_inc(hi_done, RAW)
                split_hi(act, 0, RAW)
                for q in range(4):
                    x_hi_part(act, 0, q)
                items = n_items(act)
                with act.Fori(0, items) as i:
                    rest = field(act, i, REST_FIELD, 1)

                    def half_rest(c):
                        if c in (0, 5):
                            act.wait_ge(y_free, 2 * i + (2 if c == 0 else 3))
                        else:
                            act.wait_ge(up_free, 4 * i + c)
                        nc.scalar.copy(fold[:, :], ps[0:REST, 2 * (c % 2) + 1, :]).then_inc(halved, 1)

                    def body(nb):
                        for c in range(4):
                            act.wait_ge(chunk_done, 6 * i + c + 1)
                            if nb == 2:
                                half_rest(c)
                            split_hi(act, i, 2 * c + 5)
                            if c >= 1:
                                a_hi_part(act, i, c - 1, nb)
                            act.wait_ge(g_done, 4 * i + c + 1)
                            act.wait_ge(a_done, 4 * i + c + 1)
                            nc.scalar.activation(sg[:, 0:nb, :], gt[:, c % 2, 0:nb, :], ACT.Sigmoid,
                                                 scale=ALPHA).then_inc(sg_done, 1)
                            split_hi(act, i, 2 * c + 6)
                        x_hi_part(act, i + 1, 0)
                        x_hi_part(act, i + 1, 1)
                        a_hi_part(act, i, 3, nb)
                        x_hi_part(act, i + 1, 2)
                        x_hi_part(act, i + 1, 3)
                        split_hi(act, i, 13)
                        for c in (4, 5):
                            cols = slice((c - 4) * N, (c - 3) * N)
                            act.wait_ge(chunk_done, 6 * i + c + 1)
                            if c == 4:
                                act.wait_ge(y_taken, i + 1)
                            act.sem_inc(act_passed, 1)
                            last = nc.scalar.activation(y[:, 0, cols], ps[:, 2 * (c % 2), :], ACT.Copy,
                                                        scale=k.slot_gate[:, bass.ds(i, 1), 0])
                            if nb == 2:
                                half_rest(c)
                            if c == 4:
                                split_hi(act, i, 14)
                            if nb == 2:
                                act.wait_ge(folded, 6 * i + c + 1)
                                act.sem_inc(act_passed, 1)
                                last = nc.scalar.activation(y[0:REST, 1, cols], fold[:, :], ACT.Copy,
                                                            scale=k.slot_gate[0:REST, bass.ds(i, 1), 1])
                            last.then_inc(y_free, 1)
                            if c == 4:
                                split_hi(act, i, 15)
                        split_hi(act, i, 16)
                        if nb == 1:
                            act.sem_inc(halved, 6)

                    each_size(act, rest, body)

            @block.vector
            def _(dve):
                V = nc.vector
                V.memset(xg[0:REST, 1, :], 0.0).then_inc(xg_made, 1)
                V.memset(gt[:, :, 1, :], 0.0)
                V.memset(up[:, 1, :], 0.0)
                dve.sem_inc(y_free, 2)
                dve.sem_inc(xt_lo, 2)
                V.tensor_copy(sel[:, :], k.sel[:, 0:1].broadcast_to((3 * NE, P))).then_inc(sel_done, 1)
                dve.sem_inc(lo_done, SOME_LO)
                for u in range(SOME_LO, RAW + 1):
                    split_lo(dve, 0, u)
                for q in range(4):
                    x_lo_part(dve, 0, q)
                items = n_items(dve)
                with dve.Fori(0, items) as i:
                    rest = field(dve, i, REST_FIELD, 1)

                    def fold_rest(c):
                        bank = ps[:, 2 * (c % 2) + 1, :]
                        dve.wait_ge(halved, 6 * i + c + 1)
                        V.tensor_tensor(fold[:, :], bank[REST:2 * REST, :], fold[:, :], ALU.add
                                        ).then_inc(folded, 1)

                    def body(nb):
                        for c in range(4):
                            n = 4 * i + c + 1
                            dve.wait_ge(chunk_done, 6 * i + c + 1)
                            g, u_ = gt[:, c % 2, 0:nb, :], up[:, 0:nb, :]
                            if nb == 2:
                                fold_rest(c)
                                dve.wait_ge(folded, 6 * i + c + 1)
                                dve.wait_ge(a_done, 4 * i + c + 1)
                                f = fold[:, :]
                                V.tensor_scalar(gt[0:REST, c % 2, 1, :], f[:, 0:N:2], LIMIT, None, ALU.min)
                                V.tensor_scalar(up[0:REST, 1, :], f[:, 1:N:2], LIMIT, -LIMIT, ALU.min, ALU.max)
                            bank = ps[:, 2 * (c % 2), :]
                            V.tensor_scalar(gt[:, c % 2, 0, :], bank[:, 0:N:2], LIMIT, None, ALU.min
                                            ).then_inc(g_done, 1)
                            if nb == 1:
                                dve.wait_ge(a_done, 4 * i + c + 1)
                            V.tensor_scalar(up[:, 0, :], bank[:, 1:N:2], LIMIT, -LIMIT, ALU.min, ALU.max
                                            ).then_inc(up_free, 1)
                            dve.wait_ge(up_free, n)
                            dve.wait_ge(g_done, n)
                            V.scalar_tensor_tensor(out=u_, in0=u_, scalar=1.0, in1=g, op0=ALU.add, op1=ALU.mult
                                                   ).then_inc(t_done, 1)
                            split_lo(dve, i, 2 * c + 5)
                            if c >= 1:
                                a_lo_part(dve, i, c - 1, nb)
                            if c < 3:
                                split_lo(dve, i, 2 * c + 6)
                        x_lo_part(dve, i + 1, 0)
                        x_lo_part(dve, i + 1, 1)
                        split_lo(dve, i, 12)
                        a_lo_part(dve, i, 3, nb)
                        x_lo_part(dve, i + 1, 2)
                        x_lo_part(dve, i + 1, 3)
                        split_lo(dve, i, 13)
                        if nb == 2:
                            dve.wait_ge(chunk_done, 6 * i + 5)
                            fold_rest(4)
                        split_lo(dve, i, 14)
                        split_lo(dve, i, 15)
                        dve.wait_ge(chunk_done, 6 * i + 6)
                        if nb == 2:
                            fold_rest(5)
                        else:
                            dve.sem_inc(folded, 6)
                        V.tensor_copy(sel[:, :], k.sel[:, bass.ds(i + 1, 1)].broadcast_to((3 * NE, P))
                                      ).then_inc(sel_done, 1)
                        split_lo(dve, i, 16)

                    each_size(dve, rest, body)

            @block.tensor
            def _(pe):
                for q in range(4):
                    x_turn(pe, 0, q)
                items = n_items(pe)
                with pe.Fori(0, items) as i:
                    rest = field(pe, i, REST_FIELD, 1)

                    def body(nb):
                        def products(c, ks, first, final):
                            src = xp if c < 4 else ap_
                            out = ps[:, 2 * (c % 2), :]
                            bias_cols = bias[:, c * N:(c + 1) * N]

                            def w_at(kk):
                                s, cols = (2 * c + kk // 4) % NS, slice((kk % 4) * N, (kk % 4 + 1) * N)
                                return w_hi[s][:, cols], w_lo[s][:, cols]

                            for kk in ks:
                                last = mm3(nc, out, src[:, kk, B_HI], src[:, kk, B_LO], *w_at(kk),
                                           first and kk == ks[0], False)
                            if final:
                                if c == 0:
                                    pe.wait_ge(sel_done, i + 1)
                                last = nc.tensor.matmul(out, sel[:, :], bias_cols, start=False, stop=True)
                            if nb == 2:
                                out = ps[:, 2 * (c % 2) + 1, :]
                                for kk in ks:
                                    hi, lo = w_at(kk)
                                    both = src[:, kk, R_BOTH]
                                    opens, closes = first and kk == ks[0], final and kk == ks[-1]
                                    if opens:
                                        nc.tensor.matmul(out, both, hi, start=True, stop=False)
                                    last = nc.tensor.matmul(out[0:REST, :], src[:, kk, R_HI], lo, start=False,
                                                            stop=False)
                                    if closes:
                                        nc.tensor.matmul(out[0:REST, :], sel[:, 0:REST], bias_cols, start=False,
                                                         stop=False)
                                    if not opens:
                                        last = nc.tensor.matmul(out, both, hi, start=False, stop=closes)
                            if final:
                                last.then_inc(chunk_done, 1)

                        def act_turn(c):
                            pe.wait_ge(a_done, 4 * i + c + 2)
                            if c >= 2:
                                pe.wait_ge(at_lo, 4 * i + c - 1)
                            for kk in range(2):
                                for b in range(nb):
                                    r, at = ROWS[b], b * BLOCK
                                    last = nc.tensor.transpose(a_bank(c)[:, kk, at:at + r],
                                                               gt[0:r, c % 2, b, kk * P:(kk + 1) * P],
                                                               k.ident[0:r, 0:r])
                            last.then_inc(at_turned, 1)

                        def parts_ready(u):
                            pe.wait_ge(lo_done, NU * i + u + 1)

                        pe.wait_ge(xt_lo, 4 * i + 6)
                        for c in range(4):
                            if c < 2:
                                pe.wait_ge(y_free, 2 * i + c + 1)
                            else:
                                pe.wait_ge(up_free, 4 * i + c - 1)
                            parts_ready(2 * c + 1)
                            products(c, list(range(KT)), True, True)
                            if c >= 1:
                                act_turn(c - 1)
                        x_turn(pe, i + 1, 0)
                        x_turn(pe, i + 1, 1)
                        pe.wait_ge(up_free, 4 * i + 3)
                        pe.wait_ge(at_lo, 4 * i + 2)
                        parts_ready(8)
                        products(4, [0, 1, 2, 3], True, False)
                        pe.wait_ge(up_free, 4 * i + 4)
                        parts_ready(10)
                        products(5, [0, 1, 2, 3], True, False)
                        pe.wait_ge(at_lo, 4 * i + 3)
                        products(4, [4, 5], False, False)
                        act_turn(3)
                        x_turn(pe, i + 1, 2)
                        x_turn(pe, i + 1, 3)
                        pe.wait_ge(at_lo, 4 * i + 4)
                        products(4, [6, 7], False, True)
                        parts_ready(11)
                        products(5, [4, 5, 6, 7], False, True)

                    each_size(pe, rest, body)


def stage_final(nc, k, x_from, g_final, out):
    with Stage(nc) as ctx:
        def sb(nm, shape, dt=f32):
            return ctx.enter_context(nc.sbuf_tensor(f"c_{nm}", shape, dt))

        def sem(nm):
            return ctx.sem(f"c_{nm}")

        xt, gain, junk, stat = sb("xt", [P, TT, D]), sb("gain", [P, D]), sb("junk", [P, D]), sb("stat", [P, 3, TT])
        x_in = [sem(f"x_in{i}") for i in range(TT)]
        g_in, sumsq, root, inv, scaled, stored = (sem(s) for s in ("g_in", "sumsq", "root", "inv", "scaled", "stored"))
        with nc.Block() as block:
            @block.sync
            def _(sp):
                for t in range(TT):
                    sp.dma_start(xt[:, t, :], x_from[t * P:(t + 1) * P, :]).then_inc(x_in[t], 16)
                    if t == 0:
                        sp.dma_start(gain[:, :], gain_row(g_final)).then_inc(g_in, 16)
                for t in range(TT):
                    sp.wait_ge(scaled, t + 1)
                    sp.dma_start(out[0, t * P:(t + 1) * P, :], xt[:, t, :]).then_inc(stored, 16)
                sp.wait_ge(stored, 16 * TT)

            @block.scalar
            def _(act):
                nc.scalar.preload_act_table_set("sqrt_and_others")
                for t in range(TT):
                    act.wait_ge(x_in[t], 16)
                    if t:
                        act.wait_ge(sumsq, t)
                    nc.scalar.activation(junk[:, :], xt[:, t, :], ACT.Square, accum_out=stat[:, 0, t:t + 1]
                                         ).then_inc(sumsq, 1)
                    act.wait_ge(sumsq, t + 1)
                    nc.scalar.activation(stat[:, 1, t:t + 1], stat[:, 0, t:t + 1], ACT.Sqrt, scale=1.0 / D,
                                         bias=k.eps[:, 0:1]).then_inc(root, 1)

            @block.vector
            def _(dve):
                dve.wait_ge(g_in, 16)
                for t in range(TT):
                    dve.wait_ge(root, t + 1)
                    nc.vector.reciprocal(stat[:, 2, t:t + 1], stat[:, 1, t:t + 1]).then_inc(inv, 1)
                    dve.wait_ge(inv, t + 1)
                    nc.vector.scalar_tensor_tensor(out=xt[:, t, :], in0=xt[:, t, :], scalar=stat[:, 2, t:t + 1],
                                                   in1=gain[:, :], op0=ALU.mult, op1=ALU.mult).then_inc(scaled, 1)


def program(nc, x, mem, g_mix, w_in, w_conv, g_conv_out, g_sb_out, w_out, g_xattn, g_mem, w_xq, w_xkv, w_xo,
            g_ffn, w_router, b_router, w_gate_up, b_gate_up, w_down, b_down, g_final, out, until=99):
    k = Kit()

    def cols(w, width):
        v = w[0].rearrange("(k p) n -> p k n", p=P)
        return [v[:, :, c:c + 256] for c in range(0, width, 256)]

    def halves(w):
        v = w[0].rearrange("(k p) n -> p k n", p=P)
        return [v[:, 4 * h:4 * h + 4, n * N:(n + 1) * N] for n in range(2) for h in range(2)]

    w_in_units = cols(w_in, 3 * D)
    order = [0, 1, 4, 5, 2, 3, 6, 7, 8, 9, 10, 11]
    units = [w_in_units[i] for i in order] + cols(w_xkv, 2 * D) + halves(w_out) + cols(w_xq, D) + halves(w_xo)

    def dram(name, shape, dt=f32):
        return nc.dram_tensor(name, shape, dt, kind="Internal").ap()

    x1 = dram("x_mixed", (SEQ, D))
    x2 = dram("x_crossed", (SEQ + P, D))
    k.h_rows = dram("expert_inputs", (SEQ + P, D))
    k.table_dram = dram("item_table", (P, 8), i32)

    with ExitStack() as ctx:
        def sb(scope, name, shape, dt=f32):
            return scope.enter_context(nc.sbuf_tensor(name, shape, dt))

        k.logits = sb(ctx, "logits", [P, TT, NE])
        k.gates = sb(ctx, "gates", [P, TT, TOPK])
        k.slot_gate = sb(ctx, "slot_gate", [P, MAX_ITEMS + 1, 2])
        k.rows = sb(ctx, "rows_of_slots", [P, MAX_ITEMS + 1, 2], i32)
        k.sel = sb(ctx, "expert_of_item", [3 * NE, P], bf16)
        k.table = sb(ctx, "item_row", [1, P * 8], i32)
        constants(nc, ctx, k)
        k.ring = Ring(nc, ctx, units)
        with ExitStack() as dense:
            k.act_hi = sb(dense, "act_hi", [P, KT, SEQ], f32r)
            k.act_lo = sb(dense, "act_lo", [P, KT, SEQ], f32r)
            with ExitStack() as mixer:
                k.y, k.q, k.k = (sb(mixer, s, [P, 4, SEQ]) for s in ("mix_y", "mix_q", "mix_k"))
                k.v = sb(mixer, "mix_v", [P, TT, 512])
                k.o = k.q
                stage_projections(nc, k, x, g_mix, w_conv)
                if until >= 2:
                    stage_stick(nc, k)
                    stage_mixer_norms(nc, k, g_conv_out, g_sb_out)
            with ExitStack() as cross:
                if until >= 3:
                    k.mk = sb(cross, "mem_k", [P, KT, MEM])
                    k.mv = sb(cross, "mem_v", [P, 2, D])
                    stage_memory(nc, k, mem, g_mem, 12)
                    stage_residual(nc, k, "mix", x[0], x1, g_xattn, 20)
                if until >= 4:
                    stage_cross(nc, k, 24)
            if until >= 4:
                stage_residual(nc, k, "ffn", x1, x2, g_ffn, 28, router=(w_router, b_router))
        k.w_hi, k.w_lo = (sb(ctx, f"first_w_{s}", [P, n, UNIT], f32r) for s, n in (("hi", RAW), ("lo", SOME_LO)))
        k.bias = sb(ctx, "expert_bias", [3 * NE, 3 * D], bf16)
        if until >= 5:
            stage_routing(nc, k, w_gate_up, b_gate_up, b_down)
        if until >= 6:
            stage_experts(nc, k, x2, w_gate_up, w_down)
            stage_final(nc, k, x2, g_final, out)


_INS = ["x", "mem", "g_mix", "w_in", "w_conv", "g_conv_out", "g_sb_out", "w_out", "g_xattn", "g_mem", "w_xq", "w_xkv",
        "w_xo", "g_ffn", "w_router", "b_router", "w_gate_up", "b_gate_up", "w_down", "b_down", "g_final"]
_OUTS = [((1, SEQ, D), "float32")]


def kernel(**inputs):
    import numpy as _np
    import concourse.bacc as _bacc
    from concourse import mybir as _mybir
    from concourse.bass_utils import run_bass_kernel_spmd as _run

    nc = _bacc.Bacc("TRN2", target_bir_lowering=False, num_devices=1)
    arrays, args = {}, []
    for name in _INS:
        a = _np.ascontiguousarray(inputs[name])
        if a.ndim == 1:
            a = a.reshape(1, -1)
        arrays[f"in_{name}_dram"] = a
        args.append(nc.dram_tensor(f"in_{name}_dram", a.shape, _mybir.dt.from_np(a.dtype), kind="ExternalInput").ap())
    for i, (shape, dtype) in enumerate(_OUTS):
        dt = _mybir.dt.from_np(_np.dtype(dtype))
        args.append(nc.dram_tensor(f"out_{i}_dram", shape, dt, kind="ExternalOutput").ap())
    program(nc, *args)
    r = _run(nc, [arrays], core_ids=[0])
    return r.results[0]["out_0_dram"]
```

```python
from contextlib import ExitStack

import concourse.bass as bass
from concourse import mybir

f32 = mybir.dt.float32
f32r = mybir.dt.float32r
bf16 = mybir.dt.bfloat16
i32 = mybir.dt.int32
u32 = mybir.dt.uint32
ALU = mybir.AluOpType
ACT = mybir.ActivationFunctionType
AX = mybir.AxisListType.X

P = 128
D = 1024
SEQ = 1024
MEM = 256
KT = D // P
TT = SEQ // P
CW = 512
HEADS, HD = 8, 64
XH, XD = 4, 256
NE, TOPK = 32, 4
EPS = 1e-6
LIMIT, ALPHA = 7.0, 1.702
BLOCK = 128
REST = 64
CAP = BLOCK + REST
SOME_LO = 2
MAX_ITEMS = SEQ * TOPK // CAP + NE
N = 512
RAW = 4
UNIT = 2048


class Stage(ExitStack):

    cleared = {}

    def __init__(self, nc):
        super().__init__()
        self.nc, self.sems = nc, []

    def sem(self, name):
        self.sems.append(self.nc.alloc_semaphore(name))
        return self.sems[-1]

    def __exit__(self, *exc):
        if exc[0] is None:
            for s in self.sems:
                self.nc.gpsimd.sem_clear(s)
            for s in Stage.cleared.pop(id(self.nc), []):
                self.nc.release_semaphore(s)
            Stage.cleared[id(self.nc)] = self.sems
        return super().__exit__(*exc)


class Ring:

    def __init__(self, nc, ctx, units):
        self.nc, self.units = nc, units
        self.raw = ctx.enter_context(nc.sbuf_tensor("w_raw", [P, RAW, UNIT], f32))
        self.ready = [ctx.enter_context(nc.semaphore(f"w_loaded{s}")) for s in range(RAW)]
        self.hi_done = ctx.enter_context(nc.semaphore("w_hi_done"))
        self.lo_done = ctx.enter_context(nc.semaphore("w_lo_done"))

    def load(self, sp, n):
        if n >= len(self.units):
            return
        if n >= RAW:
            sp.wait_ge(self.lo_done, n - RAW + 1)
        ap = self.units[n]
        dst = self.raw[:, n % RAW, :].rearrange("p (k c) -> p k c", k=ap.shape[1])
        sp.dma_start(dst, ap).then_inc(self.ready[n % RAW], 16)

    def hi(self, act, n, dst):
        act.wait_ge(self.ready[n % RAW], 16 * (n // RAW + 1))
        self.nc.scalar.copy(dst, self.raw[:, n % RAW, :]).then_inc(self.hi_done, 1)

    def lo(self, dve, n, hi, dst):
        dve.wait_ge(self.hi_done, n + 1)
        self.nc.vector.tensor_tensor(dst, self.raw[:, n % RAW, :], hi.bitcast(f32),
                                     ALU.subtract).then_inc(self.lo_done, 1)


def mm3(nc, out, lh, ll, rh, rl, start, stop):
    nc.tensor.matmul(out, ll, rh, start=start, stop=False)
    nc.tensor.matmul(out, lh, rl, start=False, stop=False)
    return nc.tensor.matmul(out, lh, rh, start=False, stop=stop)


class RowNorm:

    def __init__(self, nc, ctx, name, src, ready, gain, gain_ready, ident, eps, banks, dest, hn_free=None, scratch=None):
        self.nc, self.src, self.ready, self.gain, self.gain_ready = nc, src, ready, gain, gain_ready
        self.ident, self.eps, self.banks, self.dest, self.hn_free = ident, eps, banks, dest, hn_free
        if scratch is None:
            self.junk = ctx.enter_context(nc.sbuf_tensor(f"{name}_square", [P, D], f32))
            self.hn = ctx.enter_context(nc.sbuf_tensor(f"{name}_rows", [P, 2, D], f32))
        else:
            self.junk, self.hn = scratch
        self.stat = ctx.enter_context(nc.sbuf_tensor(f"{name}_stat", [P, 3, TT], f32))
        self.sumsq_done, self.rms_done, self.inv_done, self.rows_done, self.turned, self.hi_done, \
            self.lo_done = [ctx.sem(f"{name}_{s}") for s in
                            ("sumsq", "rms", "inv", "rows", "turned", "hi", "lo")]

    def act_stats(self, act, t):
        nc = self.nc
        self.ready(act, t)
        if t:
            act.wait_ge(self.sumsq_done, t)
        nc.scalar.activation(self.junk[:, :], self.src(t), ACT.Square,
                             accum_out=self.stat[:, 0, t:t + 1]).then_inc(self.sumsq_done, 1)
        act.wait_ge(self.sumsq_done, t + 1)
        nc.scalar.activation(self.stat[:, 1, t:t + 1], self.stat[:, 0, t:t + 1], ACT.Sqrt,
                             scale=1.0 / D, bias=self.eps[:, 0:1]).then_inc(self.rms_done, 1)

    def dve_rows(self, dve, t):
        nc = self.nc
        dve.wait_ge(self.rms_done, t + 1)
        nc.vector.reciprocal(self.stat[:, 2, t:t + 1], self.stat[:, 1, t:t + 1]).then_inc(self.inv_done, 1)
        dve.wait_ge(self.inv_done, t + 1)
        self.ready(dve, t)
        if t == 0:
            self.gain_ready(dve)
        if t >= 2:
            dve.wait_ge(self.turned, 2 * (t - 1))
            if self.hn_free:
                self.hn_free(dve, t - 2)
        nc.vector.scalar_tensor_tensor(out=self.hn[:, t % 2, :], in0=self.src(t), scalar=self.stat[:, 2, t:t + 1],
                                       in1=self.gain, op0=ALU.mult, op1=ALU.mult).then_inc(self.rows_done, 1)

    def pe_turn(self, pe, t):
        pe.wait_ge(self.rows_done, t + 1)
        nb = len(self.banks)
        for q in range(2):
            n = 2 * t + q
            if n >= nb:
                pe.wait_ge(self.lo_done, n - nb + 1)
            bank = self.banks[n % nb]
            for k in range(4):
                c = (4 * q + k) * P
                last = self.nc.tensor.transpose(bank[:, k * P:(k + 1) * P], self.hn[:, t % 2, c:c + P],
                                                self.ident[:, :])
            last.then_inc(self.turned, 1)

    def bank(self, t, q):
        return self.banks[(2 * t + q) % len(self.banks)].rearrange("p (k c) -> p k c", k=4)

    def act_hi(self, act, t):
        for q in range(2):
            act.wait_ge(self.turned, 2 * t + q + 1)
            self.nc.scalar.copy(self.dest(t, q)[0], self.bank(t, q)).then_inc(self.hi_done, 1)

    def dve_lo(self, dve, t):
        for q in range(2):
            hi, lo = self.dest(t, q)
            dve.wait_ge(self.hi_done, 2 * t + q + 1)
            self.nc.vector.tensor_tensor(lo, self.bank(t, q), hi.bitcast(f32),
                                         ALU.subtract).then_inc(self.lo_done, 1)


class Kit:
    pass


def constants(nc, ctx, k):
    def sb(name, shape, dt=f32):
        return ctx.enter_context(nc.sbuf_tensor(name, shape, dt))

    k.ident = sb("ident", [P, P])
    k.ident_bf = sb("ident_bf", [P, P], bf16)
    k.eps = sb("eps", [P, 1])
    k.ps = ctx.enter_context(nc.psum_tensor("ps", [P, 8, N], f32))
    made = ctx.enter_context(nc.semaphore("consts_made"))
    with nc.Block() as block:
        @block.gpsimd
        def _(pool):
            nc.gpsimd.memset(k.ident[:, :], 0.0).then_inc(made, 1)
            nc.gpsimd.memset(k.eps[:, :], EPS).then_inc(made, 1)
            pool.wait_ge(made, 2)
            nc.gpsimd.affine_select(out=k.ident[:, :], in_=k.ident[:, :], compare_op=ALU.not_equal, fill=1.0,
                                    base=0, pattern=[[-1, P]], channel_multiplier=1).then_inc(made, 1)
            pool.wait_ge(made, 3)
            nc.gpsimd.tensor_copy(k.ident_bf[:, :], k.ident[:, :]).then_inc(made, 1)


def gain_row(ap):
    return ap[0, :].partition_broadcast(P)


def stage_projections(nc, k, x, g_mix, w_conv):
    with Stage(nc) as ctx:
        def sb(name, shape, dt=f32):
            return ctx.enter_context(nc.sbuf_tensor(name, shape, dt))

        def sem(name):
            return ctx.sem(name)

        SL = 2
        w_hi, w_lo = sb("p_whi", [P, SL, UNIT], f32r), sb("p_wlo", [P, SL, UNIT], f32r)
        acc = sb("conv_acc", [P, N])
        wc = sb("w_conv_t", [P, 3, 4])
        ps = k.ps
        mm_done, ev_act, ev_dve, conv_step, wc_in = (sem(s) for s in ("p_mm", "p_evac_act", "p_evac_dve",
                                                                       "conv_step", "wc_in"))
        x_in = [sem(f"p_x_in{i}") for i in range(2)]
        g_in = sem("p_g_in")
        xt = [k.y[:, 0, :], k.y[:, 1, :]]
        gain = k.y[:, 2, :]
        scratch = (k.y[:, 3, :], k.v[:, 0:4, :].rearrange("p (a b) c -> p a (b c)", a=2))

        def x_ready(eng, t):
            eng.wait_ge(x_in[t % 2], 16 * (t // 2 + 1))

        norm = RowNorm(nc, ctx, "p", lambda t: xt[t % 2], x_ready, gain, lambda e: e.wait_ge(g_in, 16),
                       k.ident, k.eps, [ps[:, b, :] for b in range(2)],
                       lambda t, q: (k.act_hi[:, 4 * q:4 * q + 4, t * P:(t + 1) * P],
                                     k.act_lo[:, 4 * q:4 * q + 4, t * P:(t + 1) * P]), scratch=scratch)

        kinds = ["u", "u", "c", "c", "b", "b", "q", "q", "k", "k", "v", "v"]
        groups = []
        for n, kind in enumerate(kinds):
            if kind == "v":
                groups += [(n, kind, n % 2, t) for t in range(TT)]
            else:
                halves = (1, 0) if kind == "b" else (0, 1)
                order = [(m, th) for m in range(2) for th in halves]
                if n == 0:
                    order.sort(key=lambda mt: mt[1])
                groups += [(n, kind, 2 * (n % 2) + m, th) for m, th in order]
        on_act = {"u", "q", "v"}
        count = {"act": 0, "dve": 0}
        done_at, index = [], {}
        for g, (n, kind, f, th) in enumerate(groups):
            e = "act" if kind in on_act else "dve"
            count[e] += 1
            done_at.append((e, count[e]))
            index[(kind, f, th)] = g
        unit_end = [max(g for g, x_ in enumerate(groups) if x_[0] == n) + 1 for n in range(12)]
        sem_of = {"act": ev_act, "dve": ev_dve}
        BK = 6

        def evacuated(eng, g):
            e, v = done_at[g]
            eng.wait_ge(sem_of[e], v)

        with nc.Block() as block:
            @block.sync
            def _(sp):
                sp.dma_start(gain, gain_row(g_mix)).then_inc(g_in, 16)
                for t in range(TT):
                    if t >= 2:
                        sp.wait_ge(norm.rows_done, t - 1)
                        sp.wait_ge(norm.sumsq_done, t - 1)
                    sp.dma_start(xt[t % 2], x[0, t * P:(t + 1) * P, :]).then_inc(x_in[t % 2], 16)
                    if t == 1:
                        for j in range(3):
                            with nc.allow_non_contiguous_dma(reason="512 taps a row, once"):
                                sp.dma_start(wc[:, j, :], w_conv[0, j, :].rearrange("(f p) -> p f", p=P)
                                             ).then_inc(wc_in, 16)
                    if t % 2:
                        k.ring.load(sp, t // 2)
                for n in range(RAW, 12 + RAW):
                    k.ring.load(sp, n)
                sp.wait_ge(wc_in, 48)

            @block.scalar
            def _(act):
                for t in range(TT + 1):
                    if t < TT:
                        norm.act_stats(act, t)
                    if t:
                        norm.act_hi(act, t - 1)
                    if t == TT // 2:
                        k.ring.hi(act, 0, w_hi[:, 0, :])
                k.ring.hi(act, 1, w_hi[:, 1, :])
                g = 0
                for n in range(12):
                    while g < len(groups) and groups[g][0] == n:
                        _, kind, f, th = groups[g]
                        if kind in on_act:
                            act.wait_ge(mm_done, g + 1)
                            bank = ps[:, 2 + g % BK, :]
                            if kind == "u":
                                nc.scalar.copy(k.y[:, f, th * N:(th + 1) * N], bank).then_inc(ev_act, 1)
                            elif kind == "q":
                                nc.scalar.activation(k.q[:, f, th * N:(th + 1) * N], bank, ACT.Copy,
                                                     scale=HD ** -0.5).then_inc(ev_act, 1)
                            else:
                                nc.scalar.copy(k.v[:, th, f * 256:(f + 1) * 256], bank[:, 0:256]
                                               ).then_inc(ev_act, 1)
                        g += 1
                    if n + SL < 12:
                        act.wait_ge(mm_done, unit_end[n])
                        k.ring.hi(act, n + SL, w_hi[:, n % SL, :])

            @block.vector
            def _(dve):
                for t in range(TT + 1):
                    if t < TT:
                        norm.dve_rows(dve, t)
                    if t:
                        norm.dve_lo(dve, t - 1)
                    if t == TT // 2:
                        k.ring.lo(dve, 0, w_hi[:, 0, :], w_lo[:, 0, :])
                k.ring.lo(dve, 1, w_hi[:, 1, :], w_lo[:, 1, :])
                dve.wait_ge(wc_in, 48)
                g = steps = 0
                for n in range(12):
                    while g < len(groups) and groups[g][0] == n:
                        _, kind, f, th = groups[g]
                        bank = ps[:, 2 + g % BK, :]
                        c0 = th * N
                        if kind == "c":
                            dve.wait_ge(mm_done, g + 1)
                            evacuated(dve, index[("u", f, th)])
                            here = k.y[:, f, c0:c0 + N]
                            nc.vector.tensor_tensor(here, bank, here, ALU.mult).then_inc(ev_dve, 1)
                        elif kind == "k":
                            dve.wait_ge(mm_done, g + 1)
                            nc.vector.tensor_copy(k.k[:, f, c0:c0 + N], bank).then_inc(ev_dve, 1)
                        elif kind == "b":
                            evacuated(dve, index[("c", f, 1)])
                            if steps:
                                dve.wait_ge(ev_dve, done_at[g - 1][1])
                            nc.vector.tensor_scalar(acc[:, :], k.y[:, f, c0:c0 + N], wc[:, 2, f:f + 1], None,
                                                    ALU.mult).then_inc(conv_step, 1)
                            for back in (1, 2):
                                dve.wait_ge(conv_step, steps + back)
                                o = back if th == 0 else 0
                                nc.vector.scalar_tensor_tensor(
                                    out=acc[:, o:N], in0=k.y[:, f, c0 + o - back:c0 + N - back],
                                    scalar=wc[:, 2 - back, f:f + 1], in1=acc[:, o:N], op0=ALU.mult,
                                    op1=ALU.add).then_inc(conv_step, 1)
                            steps += 3
                            dve.wait_ge(conv_step, steps)
                            dve.wait_ge(mm_done, g + 1)
                            nc.vector.tensor_tensor(k.y[:, f, c0:c0 + N], bank, acc[:, :], ALU.mult
                                                    ).then_inc(ev_dve, 1)
                        g += 1
                    if n + SL < 12:
                        k.ring.lo(dve, n + SL, w_hi[:, n % SL, :], w_lo[:, n % SL, :])

            @block.tensor
            def _(pe):
                for t in range(TT // 2):
                    norm.pe_turn(pe, t)
                pe.wait_ge(norm.lo_done, TT)
                for g, (n, kind, f, th) in enumerate(groups):
                    if g == 1:
                        norm.pe_turn(pe, 4)
                    if g == 2:
                        for t in range(5, TT):
                            norm.pe_turn(pe, t)
                        pe.wait_ge(norm.lo_done, 2 * TT)
                    if g == 0 or groups[g - 1][0] != n:
                        pe.wait_ge(k.ring.lo_done, n + 1)
                    if g >= BK:
                        evacuated(pe, g - BK)
                    wh = w_hi[:, n % SL, :].rearrange("p (k c) -> p k c", k=KT)
                    wl = w_lo[:, n % SL, :].rearrange("p (k c) -> p k c", k=KT)
                    for kk in range(KT):
                        if kind == "v":
                            out, tok = ps[:, 2 + g % BK, 0:256], slice(th * P, (th + 1) * P)
                            last = mm3(nc, out, k.act_hi[:, kk, tok], k.act_lo[:, kk, tok], wh[:, kk, :],
                                       wl[:, kk, :], kk == 0, kk == KT - 1)
                        else:
                            out, m = ps[:, 2 + g % BK, :], slice((f % 2) * P, (f % 2 + 1) * P)
                            tok = slice(th * N, (th + 1) * N)
                            last = mm3(nc, out, wh[:, kk, m], wl[:, kk, m], k.act_hi[:, kk, tok],
                                       k.act_lo[:, kk, tok], kk == 0, kk == KT - 1)
                    last.then_inc(mm_done, 1)


def stage_stick(nc, k):
    with Stage(nc) as ctx:
        def sb(name, shape, dt=f32):
            return ctx.enter_context(nc.sbuf_tensor(name, shape, dt))

        def sem(name):
            return ctx.sem(name)

        ps = k.ps
        NB, LAG = 4, 4
        E, S, A = (sb(f"stick_{s}", [P, NB, N]) for s in ("e", "sp", "a"))
        later = sb("stick_later", [P, 2, 2, N])
        neg_tri, neg_ones = sb("neg_tri", [P, P], f32r), sb("neg_ones", [P, P])
        tri = sb("neg_tri_made", [P, P])
        mask = sb("mask_bf", [P, P], bf16)
        kq_hi_done, kq_lo_done = sem("stick_kq_hi"), sem("stick_kq_lo")
        tri_done, part_hi_done, part_lo_done = (sem("stick_" + s) for s in ("tri", "part_hi", "part_lo"))
        made, z_done, e_done, cap_done, l_done, sp_done, later_done, cum_done, a_done, av_done, o_done = (
            sem("stick_" + s) for s in ("made", "z", "e", "cap", "l", "sp", "later", "cum", "a", "av", "o"))
        steps = []
        for pair in range(4):
            for T in range(2):
                for j in range(4 * T + 3, -1, -1):
                    for h in range(2):
                        steps.append((pair, T, j, h, max(0, j * P - T * N), j == 4 * T + 3, j == 0))
        NS, ZB = len(steps), 6
        later_count, c = [], 0
        for s in steps:
            c += 0 if s[6] else (1 if s[5] or s[4] == 0 and s[2] * P - s[1] * N < 0 else 2)
            later_count.append(c)

        def z(n):
            return ps[:, n % ZB, :]

        def sp_part(where, n, c0):
            s = n % NB
            return where[:, s // 2, s % 2 * N + c0:s % 2 * N + N]

        def sp_hi(n, c0):
            return sp_part(k.act_hi, n, c0)

        def sp_lo(n, c0):
            return sp_part(k.act_lo, n, c0)

        def own(h):
            return slice(HD * h, HD * (h + 1))

        def keys(pair, h):
            return k.act_hi[:, 4 + 2 * (pair % 2) + h, :]

        def queries(pair, h):
            return k.act_lo[:, 4 + 2 * (pair % 2) + h, :]

        def low_queries(pair):
            return k.act_hi[:, 2 + pair % 2, :]

        PAIR_STEPS = NS // 4

        def kq_hi(act, pair, m):
            h = m % 2
            if m == 0 and pair >= 2:
                act.wait_ge(z_done, PAIR_STEPS * (pair - 1))
            if m < 2:
                dst, src = keys(pair, h)[own(h)], k.k
            else:
                dst, src = queries(pair, h)[own(h if m < 4 else 1 - h)], k.q
            nc.scalar.copy(dst, src[own(h), pair, :]).then_inc(kq_hi_done, 1)

        def kq_lo(dve, pair, m):
            h = m % 2
            dve.wait_ge(kq_hi_done, 6 * pair + m + 1)
            if m < 2:
                dst, full, hi = keys(pair, h)[own(1 - h)], k.k, keys(pair, h)
            else:
                dst, full, hi = low_queries(pair)[own(h)], k.q, queries(pair, h)
            nc.vector.tensor_tensor(dst, full[own(h), pair, :], hi[own(h)].bitcast(f32), ALU.subtract
                                    ).then_inc(kq_lo_done, 1)

        def o_bank(n):
            return 6 + (steps[n][0] * 2 + steps[n][1]) % 2

        with nc.Block() as block:
            @block.gpsimd
            def _(pool):
                nc.gpsimd.memset(neg_ones[:, :], -1.0).then_inc(made, 1)
                nc.gpsimd.memset(mask[:, :], 0.0).then_inc(made, 1)
                pool.wait_ge(made, 2)
                nc.gpsimd.affine_select(out=tri[:, :], in_=neg_ones[:, :], compare_op=ALU.is_ge, fill=0.0,
                                        base=0, pattern=[[-1, P]], channel_multiplier=1).then_inc(made, 1)
                nc.gpsimd.affine_select(out=mask[:, :], in_=mask[:, :], compare_op=ALU.is_ge, fill=-1e30,
                                        base=-1, pattern=[[1, P]], channel_multiplier=-1).then_inc(made, 1)
                for n, (pair, T, j, h, c0, first, final) in enumerate(steps):
                    if final:
                        continue
                    pool.wait_ge(sp_done, n + 1)
                    if n >= 4:
                        pool.wait_ge(cum_done, n - 1)
                    new, old = later[:, h, j % 2, :], later[:, h, (j + 1) % 2, :]
                    if first:
                        nc.gpsimd.tensor_copy(new[:, c0:N], S[:, n % NB, c0:N]).then_inc(later_done, 1)
                        continue
                    p0 = max(0, (j + 1) * P - T * N)
                    pool.wait_ge(later_done, later_count[n - 2])
                    nc.gpsimd.tensor_tensor(new[:, p0:N], old[:, p0:N], S[:, n % NB, p0:N], ALU.add
                                            ).then_inc(later_done, 1)
                    if p0 > c0:
                        nc.gpsimd.tensor_copy(new[:, c0:p0], S[:, n % NB, c0:p0]).then_inc(later_done, 1)

            @block.tensor
            def _(pe):
                pe.wait_ge(made, 4)
                pe.wait_ge(tri_done, 1)
                for i in range(NS + LAG + 2):
                    if i < NS:
                        pair, T, j, h, c0, first, final = steps[i]
                        if i >= ZB:
                            pe.wait_ge(a_done, i - ZB + 1)
                        diag = j >= 4 * T
                        if i % PAIR_STEPS == 0:
                            pe.wait_ge(kq_hi_done, 6 * (pair + 1))
                            pe.wait_ge(kq_lo_done, 4 * (pair + 1))
                        ks, qs = slice(j * P, (j + 1) * P), slice(T * N + c0, (T + 1) * N)
                        nc.tensor.matmul(z(i)[:, c0:N], keys(pair, h)[:, ks], queries(pair, h)[:, qs], start=True,
                                         stop=False)
                        last = nc.tensor.matmul(z(i)[:, c0:N], keys(pair, h)[own(h), ks],
                                                low_queries(pair)[own(h), qs], start=False, stop=True)
                        if diag:
                            last = nc.tensor.matmul(z(i)[:, c0:c0 + P], k.ident_bf[:, :], mask[:, :],
                                                    start=False, stop=True, skip_group_check=True)
                        last.then_inc(z_done, 1)
                    n = i - LAG
                    if 0 <= n < NS:
                        pair, T, j, h, c0, first, final = steps[n]
                        pe.wait_ge(part_lo_done, n + 1)
                        for part in (sp_lo(n, c0), sp_hi(n, c0)):
                            last = nc.tensor.matmul(z(n)[:, c0:N], neg_tri[:, :], part, start=False, stop=True,
                                                    skip_group_check=True)
                        if not first:
                            p0 = max(0, (j + 1) * P - T * N)
                            pe.wait_ge(later_done, later_count[n - 2])
                            last = nc.tensor.matmul(z(n)[:, p0:N], neg_ones[:, :], later[:, h, (j + 1) % 2, p0:N],
                                                    start=False, stop=True, skip_group_check=True)
                        last.then_inc(cum_done, 1)
                    n = i - LAG - 2
                    if 0 <= n < NS:
                        pair, T, j, h, c0, first, final = steps[n]
                        unit = pair * 2 + T
                        if first and unit >= 2:
                            pe.wait_ge(o_done, unit - 1)
                        pe.wait_ge(a_done, n + 1)
                        nc.tensor.matmul(ps[64 * h:64 * h + 64, o_bank(n), c0:N],
                                         k.v[:, j, (2 * pair + h) * HD:(2 * pair + h + 1) * HD],
                                         A[:, n % NB, c0:N], start=first, stop=final,
                                         skip_group_check=True).then_inc(av_done, 1)

            @block.scalar
            def _(act):
                nc.scalar.preload_act_table_set("natural_log_exp_and_others")
                for m in range(6):
                    kq_hi(act, 0, m)
                for i in range(NS + LAG + 1):
                    m = (i % PAIR_STEPS - 6) // 2
                    if i % 2 == 0 and 0 <= m < 6 and i // PAIR_STEPS < 3:
                        kq_hi(act, i // PAIR_STEPS + 1, m)
                    if i < NS:
                        c0 = steps[i][4]
                        act.wait_ge(z_done, i + 1)
                        if i >= NB:
                            act.wait_ge(part_hi_done, i - NB + 1)
                        nc.scalar.activation(E[:, i % NB, c0:N], z(i)[:, c0:N], ACT.Exp).then_inc(e_done, 1)
                    n = i - 1
                    if 0 <= n < NS:
                        c0 = steps[n][4]
                        act.wait_ge(cap_done, n + 1)
                        nc.scalar.activation(E[:, n % NB, c0:N], E[:, n % NB, c0:N], ACT.Ln, bias=1.0
                                             ).then_inc(l_done, 1)
                    n = i - LAG - 1
                    if 0 <= n < NS:
                        c0 = steps[n][4]
                        act.wait_ge(cum_done, n + 1)
                        if n >= NB:
                            act.wait_ge(av_done, n - NB + 1)
                        nc.scalar.activation(A[:, n % NB, c0:N], z(n)[:, c0:N], ACT.Exp).then_inc(a_done, 1)

            @block.vector
            def _(dve):
                dve.wait_ge(made, 4)
                nc.vector.tensor_copy(neg_tri[:, :], tri[:, :]).then_inc(tri_done, 1)
                for m in range(4):
                    kq_lo(dve, 0, m)
                for i in range(NS + LAG + 4):
                    m = (i % PAIR_STEPS - 8) // 2
                    if i % 2 == 0 and 0 <= m < 4 and i // PAIR_STEPS < 3:
                        kq_lo(dve, i // PAIR_STEPS + 1, m)
                    if i < NS:
                        c0 = steps[i][4]
                        dve.wait_ge(e_done, i + 1)
                        nc.vector.tensor_scalar(E[:, i % NB, c0:N], E[:, i % NB, c0:N], 2.0 ** 60, None, ALU.min
                                                ).then_inc(cap_done, 1)
                    n = i - 1
                    if 0 <= n < NS:
                        c0 = steps[n][4]
                        dve.wait_ge(l_done, n + 1)
                        if n >= NB:
                            dve.wait_ge(part_lo_done, n - NB + 1)
                            dve.wait_ge(later_done, max(1, later_count[n - NB]))
                        nc.vector.tensor_tensor(S[:, n % NB, c0:N], z(n)[:, c0:N], E[:, n % NB, c0:N], ALU.max
                                                ).then_inc(sp_done, 1)
                        if n >= NB:
                            dve.wait_ge(cum_done, n - NB + 1)
                        nc.vector.tensor_tensor(sp_hi(n, c0), z(n)[:, c0:N], E[:, n % NB, c0:N], ALU.max
                                                ).then_inc(part_hi_done, 1)
                    n = i - 2
                    if 0 <= n < NS:
                        c0 = steps[n][4]
                        dve.wait_ge(part_hi_done, n + 1)
                        nc.vector.tensor_tensor(sp_lo(n, c0), S[:, n % NB, c0:N], sp_hi(n, c0).bitcast(f32),
                                                ALU.subtract).then_inc(part_lo_done, 1)
                    n = i - LAG - 4
                    if 0 <= n < NS and steps[n][6] and steps[n][3] == 1:
                        pair, T = steps[n][0:2]
                        dve.wait_ge(av_done, n + 1)
                        nc.vector.tensor_copy(k.o[:, pair, T * N:(T + 1) * N], ps[:, o_bank(n), :]
                                              ).then_inc(o_done, 1)


def stage_mixer_norms(nc, k, g_conv, g_sb):
    with Stage(nc) as ctx:
        def sb(name, shape, dt=f32):
            return ctx.enter_context(nc.sbuf_tensor(name, shape, dt))

        def sem(name):
            return ctx.sem(name)

        ps = k.ps
        G, R = 5, 9
        of_group, weight = sb("mn_of_group", [P, G * R]), sb("mn_weight", [P, G * R])
        spread = sb("mn_spread", [R, G, P])
        sq = k.k[:, :, :].rearrange("p a (b c) -> p (a b) c", b=2)
        root, inv = sb("mn_root", [R, 2, N]), sb("mn_inv", [R, 2, N])
        out = sb("mn_out", [P, 2, N])
        gt = sb("mn_gain", [P, 8])
        made, g_in, sq_done, ss_done, root_done, inv_done, turned, table_done, spread_done, out_done, hi_done, lo_done = (
            sem("mn_" + s) for s in ("made", "g_in", "sq", "ss", "root", "inv", "turned", "table", "spread", "out", "hi",
                                     "lo"))

        def src(f, th):
            return (k.y if f < 4 else k.o)[:, f % 4, th * N:(th + 1) * N]

        def group(f):
            return 0 if f < 4 else f - 3

        def columns(table, g):
            return table[:, g * R:(g + 1) * R]

        with nc.Block() as block:
            @block.sync
            def _(sp):
                with nc.allow_non_contiguous_dma(reason="1024 gains, once"):
                    sp.dma_start(gt[:, 0:4], g_conv[0, :].rearrange("(f p) -> p f", p=P)).then_inc(g_in, 16)
                    sp.dma_start(gt[:, 4:8], g_sb[0, :].rearrange("(f p) -> p f", p=P)).then_inc(g_in, 16)
                sp.wait_ge(g_in, 32)

            @block.gpsimd
            def _(pool):
                n = 0
                for table, y_value, head_value in ((weight, 1.0 / CW, 1.0 / HD), (of_group, 1.0, 1.0)):
                    for part, value in ((table[:, :], 0.0), (table[:, 0:1], y_value),
                                        (table[0:HD, R + 1:G * R:R + 2], head_value),
                                        (table[HD:P, R + 2:G * R:R + 2], head_value)):
                        if n:
                            pool.wait_ge(made, n)
                        nc.gpsimd.memset(part, value).then_inc(made, 1)
                        n += 1

            @block.scalar
            def _(act):
                nc.scalar.preload_act_table_set("sqrt_and_others")

                def square(f, th):
                    if th:
                        act.wait_ge(ss_done, f + 1)
                    nc.scalar.activation(sq[:, f, :], src(f, th), ACT.Square).then_inc(sq_done, 1)

                def roots(th):
                    act.wait_ge(ss_done, 8 * (th + 1))
                    nc.scalar.activation(root[:, th, :], ps[0:R, th, :], ACT.Sqrt, bias=k.eps[0:R, 0:1]
                                         ).then_inc(root_done, 1)

                for f in range(8):
                    square(f, 0)
                act.wait_ge(turned, 1)
                nc.scalar.copy(spread[:, :, :], ps[0:R, 2:2 + G, 0:P]).then_inc(table_done, 1)
                for f in range(8):
                    if f == 7:
                        roots(0)
                    square(f, 1)
                roots(1)
                for n in range(16):
                    f, th = n % 8, n // 8
                    act.wait_ge(out_done, n + 1)
                    nc.scalar.copy(k.act_hi[:, f, th * N:(th + 1) * N], out[:, n % 2, :]).then_inc(hi_done, 1)

            @block.tensor
            def _(pe):
                pe.wait_ge(made, 8)
                for g in range(G):
                    last = nc.tensor.transpose(ps[0:R, 2 + g, 0:P], columns(of_group, g), k.ident[:, :])
                last.then_inc(turned, 1)
                for th in range(2):
                    for f in range(8):
                        pe.wait_ge(sq_done, 8 * th + f + 1)
                        nc.tensor.matmul(ps[0:R, th, :], columns(weight, group(f)), sq[:, f, :], start=(f == 0),
                                         stop=(f == 7)).then_inc(ss_done, 1)
                pe.wait_ge(table_done, 1)
                for th in range(2):
                    pe.wait_ge(inv_done, th + 1)
                    for g in range(G):
                        if th:
                            pe.wait_ge(out_done, 4 + g)
                        nc.tensor.matmul(ps[:, 2 + g, :], spread[:, g, :], inv[:, th, :], start=True, stop=True
                                         ).then_inc(spread_done, 1)

            @block.vector
            def _(dve):
                def reciprocals(th):
                    dve.wait_ge(root_done, th + 1)
                    nc.vector.reciprocal(inv[:, th, :], root[:, th, :]).then_inc(inv_done, 1)

                def low(n):
                    f, cols = n % 8, slice(n // 8 * N, (n // 8 + 1) * N)
                    dve.wait_ge(hi_done, n + 1)
                    nc.vector.tensor_tensor(k.act_lo[:, f, cols], out[:, n % 2, :], k.act_hi[:, f, cols].bitcast(f32),
                                            ALU.subtract).then_inc(lo_done, 1)

                dve.wait_ge(g_in, 32)
                reciprocals(0)
                for n in range(16):
                    f, th = n % 8, n // 8
                    if n == 4:
                        reciprocals(1)
                    dve.wait_ge(spread_done, G * th + group(f) + 1)
                    if n >= 2:
                        dve.wait_ge(lo_done, n - 1)
                    nc.vector.scalar_tensor_tensor(out=out[:, n % 2, :], in0=src(f, th), scalar=gt[:, f:f + 1],
                                                   in1=ps[:, 2 + group(f), :], op0=ALU.mult, op1=ALU.mult
                                                   ).then_inc(out_done, 1)
                    if n:
                        low(n - 1)
                low(15)


def stage_memory(nc, k, mem, g_mem, first_unit):
    with Stage(nc) as ctx:
        def sb(name, shape, dt=f32):
            return ctx.enter_context(nc.sbuf_tensor(name, shape, dt))

        def sem(name):
            return ctx.sem(name)

        ps = k.ps
        SL = 2
        w_hi, w_lo = sb("m_whi", [P, SL, UNIT], f32r), sb("m_wlo", [P, SL, UNIT], f32r)
        m_hi, m_lo = sb("m_hi", [P, KT, MEM], f32r), sb("m_lo", [P, KT, MEM], f32r)
        xt, gain = sb("m_xt", [P, 2, D]), sb("m_gain", [P, D])
        x_in, g_in, mm_done, evac = (sem("m_" + s) for s in ("x_in", "g_in", "mm", "evac"))
        norm = RowNorm(nc, ctx, "m", lambda t: xt[:, t, :], lambda e, t: e.wait_ge(x_in, 32), gain[:, :],
                       lambda e: e.wait_ge(g_in, 16), k.ident, k.eps, [ps[:, b, :] for b in range(2)],
                       lambda t, q: (m_hi[:, 4 * q:4 * q + 4, t * P:(t + 1) * P],
                                     m_lo[:, 4 * q:4 * q + 4, t * P:(t + 1) * P]))
        BK = 6
        with nc.Block() as block:
            @block.sync
            def _(sp):
                sp.dma_start(gain[:, :], gain_row(g_mem)).then_inc(g_in, 16)
                for t in range(2):
                    sp.dma_start(xt[:, t, :], mem[0, t * P:(t + 1) * P, :]).then_inc(x_in, 16)
                for n in range(first_unit + RAW, first_unit + 8 + RAW):
                    k.ring.load(sp, n)

            @block.scalar
            def _(act):
                for t in range(3):
                    if t < 2:
                        norm.act_stats(act, t)
                    if t:
                        norm.act_hi(act, t - 1)
                for n in range(SL):
                    k.ring.hi(act, first_unit + n, w_hi[:, n, :])
                for n in range(8):
                    for m in range(2):
                        g = 2 * n + m
                        act.wait_ge(mm_done, g + 1)
                        bank = ps[:, 2 + g % BK, 0:256]
                        if n < 4:
                            nc.scalar.copy(k.mk[:, 2 * n + m, :], bank).then_inc(evac, 1)
                        else:
                            nc.scalar.copy(k.mv[:, m, (n - 4) * 256:(n - 3) * 256], bank).then_inc(evac, 1)
                    if n + SL < 8:
                        k.ring.hi(act, first_unit + n + SL, w_hi[:, n % SL, :])

            @block.vector
            def _(dve):
                for t in range(3):
                    if t < 2:
                        norm.dve_rows(dve, t)
                    if t:
                        norm.dve_lo(dve, t - 1)
                for n in range(8):
                    if n >= SL:
                        dve.wait_ge(mm_done, 2 * (n - SL) + 2)
                    k.ring.lo(dve, first_unit + n, w_hi[:, n % SL, :], w_lo[:, n % SL, :])

            @block.tensor
            def _(pe):
                for t in range(2):
                    norm.pe_turn(pe, t)
                pe.wait_ge(norm.lo_done, 4)
                for n in range(8):
                    pe.wait_ge(k.ring.lo_done, first_unit + n + 1)
                    wh = w_hi[:, n % SL, :].rearrange("p (k c) -> p k c", k=KT)
                    wl = w_lo[:, n % SL, :].rearrange("p (k c) -> p k c", k=KT)
                    for m in range(2):
                        g = 2 * n + m
                        if g >= BK:
                            pe.wait_ge(evac, g - BK + 1)
                        out, c = ps[:, 2 + g % BK, 0:256], slice(m * P, (m + 1) * P)
                        for kk in range(KT):
                            if n < 4:
                                last = mm3(nc, out, wh[:, kk, c], wl[:, kk, c], m_hi[:, kk, :], m_lo[:, kk, :],
                                           kk == 0, kk == KT - 1)
                            else:
                                last = mm3(nc, out, m_hi[:, kk, c], m_lo[:, kk, c], wh[:, kk, :], wl[:, kk, :],
                                           kk == 0, kk == KT - 1)
                        last.then_inc(mm_done, 1)


def stage_residual(nc, k, name, x_from, x_to, gain_ap, first_unit, router=None):
    with Stage(nc) as ctx:
        def sb(nm, shape, dt=f32):
            return ctx.enter_context(nc.sbuf_tensor(f"{name}_{nm}", shape, dt))

        def sem(nm):
            return ctx.sem(f"{name}_{nm}")

        ps = k.ps
        w_hi, w_lo = sb("whi", [P, 4, UNIT], f32r), sb("wlo", [P, 4, UNIT], f32r)
        xt, gain = sb("xt", [P, 2, D]), sb("gain", [P, D])
        g_in, mm_done, sum_done = sem("g_in"), sem("mm"), sem("sum")
        x_in = [sem(f"x_in{i}") for i in range(2)]
        stored = [sem(f"stored{i}") for i in range(2)]
        rows_stored = [sem(f"rows_stored{i}") for i in range(2)]
        if router is not None:
            w_router, b_router = router
            ht = sb("ht", [P, 2, KT, P])
            wr, br = sb("wr", [P, KT, NE]), sb("br", [P, NE])
            zero = sb("zero", [P, D])
            r_in, zero_made, logit_done, bias_done = sem("r_in"), sem("zero_made"), sem("logit"), sem("biased")

        def summed(eng, t):
            eng.wait_ge(sum_done, 2 * t + 2)

        norm = RowNorm(nc, ctx, name, lambda t: xt[:, t % 2, :], summed, gain[:, :],
                       lambda e: e.wait_ge(g_in, 16), k.ident, k.eps, [ps[:, b, :] for b in range(2)],
                       lambda t, q: (k.act_hi[:, 4 * q:4 * q + 4, t * P:(t + 1) * P],
                                     k.act_lo[:, 4 * q:4 * q + 4, t * P:(t + 1) * P]),
                       hn_free=None if router is None else
                       (lambda e, t: e.wait_ge(rows_stored[t % 2], 16 * (t // 2 + 1))))

        with nc.Block() as block:
            @block.sync
            def _(sp):
                sp.dma_start(gain[:, :], gain_row(gain_ap)).then_inc(g_in, 16)
                if router is not None:
                    sp.wait_ge(zero_made, 1)
                    for spare in (x_to, k.h_rows):
                        sp.dma_start(spare[SEQ:SEQ + P, :], zero[:, :]).then_inc(r_in, 16)
                    sp.dma_start(wr[:, :, :], w_router[0].rearrange("(k p) n -> p k n", p=P)).then_inc(r_in, 16)
                    sp.dma_start(br[:, :], b_router[0, :].partition_broadcast(P)).then_inc(r_in, 16)
                for t in range(2):
                    sp.dma_start(xt[:, t, :], x_from[t * P:(t + 1) * P, :]).then_inc(x_in[t], 16)
                for n in range(first_unit + RAW, first_unit + 4 + RAW):
                    k.ring.load(sp, n)
                for t in range(TT):
                    summed(sp, t)
                    sp.dma_start(x_to[t * P:(t + 1) * P, :], xt[:, t % 2, :]).then_inc(stored[t % 2], 16)
                    sp.wait_ge(norm.rows_done, t + 1)
                    if router is not None:
                        sp.dma_start(k.h_rows[t * P:(t + 1) * P, :], norm.hn[:, t % 2, :]
                                     ).then_inc(rows_stored[t % 2], 16)
                    if t + 2 < TT:
                        sp.wait_ge(norm.sumsq_done, t + 1)
                        sp.wait_ge(stored[t % 2], 16 * (t // 2 + 1))
                        sp.dma_start(xt[:, t % 2, :], x_from[(t + 2) * P:(t + 3) * P, :]
                                     ).then_inc(x_in[t % 2], 16)
                for b in range(2):
                    sp.wait_ge(stored[b], 16 * (TT // 2))
                    if router is not None:
                        sp.wait_ge(rows_stored[b], 16 * (TT // 2))

            @block.gpsimd
            def _(pool):
                if router is not None:
                    nc.gpsimd.memset(zero[:, :], 0.0).then_inc(zero_made, 1)

            @block.scalar
            def _(act):
                for n in range(4):
                    k.ring.hi(act, first_unit + n, w_hi[:, n, :])
                for t in range(TT + 1):
                    if t < TT:
                        norm.act_stats(act, t)
                    if t and router is None:
                        norm.act_hi(act, t - 1)
                    elif t:
                        for q in range(2):
                            act.wait_ge(norm.turned, 2 * (t - 1) + q + 1)
                            if t >= 3:
                                act.wait_ge(logit_done, t - 2)
                            nc.scalar.copy(ht[:, (t - 1) % 2, 4 * q:4 * q + 4, :], norm.bank(t - 1, q)
                                           ).then_inc(norm.lo_done, 1)

            @block.vector
            def _(dve):
                for n in range(4):
                    k.ring.lo(dve, first_unit + n, w_hi[:, n, :], w_lo[:, n, :])
                for t in range(TT + 1):
                    if t < TT:
                        dve.wait_ge(x_in[t % 2], 16 * (t // 2 + 1))
                        for nh in range(2):
                            g = 2 * t + nh
                            dve.wait_ge(mm_done, g + 1)
                            half = xt[:, t % 2, nh * N:(nh + 1) * N]
                            nc.vector.tensor_tensor(half, ps[:, 2 + g % 4, :], half, ALU.add
                                                    ).then_inc(sum_done, 1)
                        norm.dve_rows(dve, t)
                    if t and router is None:
                        norm.dve_lo(dve, t - 1)
                if router is not None:
                    dve.wait_ge(r_in, 64)
                    dve.wait_ge(logit_done, TT)
                    nc.vector.tensor_tensor(
                        k.logits[:, :, :], ps[:, 6, 0:TT * NE].rearrange("p (t e) -> p t e", e=NE),
                        br[:, :].unsqueeze(1).broadcast_to((P, TT, NE)), ALU.add).then_inc(bias_done, 1)

            @block.tensor
            def _(pe):
                for t in range(TT + 2):
                    if t < TT:
                        tok = slice(t * P, (t + 1) * P)
                        for nh in range(2):
                            g = 2 * t + nh
                            if g >= 4:
                                pe.wait_ge(sum_done, g - 3)
                            for kk in range(KT):
                                u = 2 * nh + kk // 4
                                if t == 0 and kk % 4 == 0:
                                    pe.wait_ge(k.ring.lo_done, first_unit + u + 1)
                                c = slice((kk % 4) * N, (kk % 4 + 1) * N)
                                last = mm3(nc, ps[:, 2 + g % 4, :], k.act_hi[:, kk, tok], k.act_lo[:, kk, tok],
                                           w_hi[:, u, c], w_lo[:, u, c], kk == 0, kk == KT - 1)
                            last.then_inc(mm_done, 1)
                    if 1 <= t <= TT:
                        norm.pe_turn(pe, t - 1)
                    if router is not None and t >= 2:
                        if t == 2:
                            pe.wait_ge(r_in, 64)
                        pe.wait_ge(norm.lo_done, 2 * (t - 1))
                        for kk in range(KT):
                            last = nc.tensor.matmul(ps[:, 6, (t - 2) * NE:(t - 1) * NE], ht[:, (t - 2) % 2, kk, :],
                                                    wr[:, kk, :], start=(kk == 0), stop=(kk == KT - 1))
                        last.then_inc(logit_done, 1)


def stage_cross(nc, k, first_unit):
    with Stage(nc) as ctx:
        def sb(nm, shape, dt=f32):
            return ctx.enter_context(nc.sbuf_tensor(f"x_{nm}", shape, dt))

        def sem(nm):
            return ctx.sem(f"x_{nm}")

        ps = k.ps
        SL, BK = 2, 4
        w_hi, w_lo = sb("whi", [P, SL, UNIT], f32r), sb("wlo", [P, SL, UNIT], f32r)
        qt = sb("qt", [P, KT, SEQ])
        p = sb("p", [P, 4, MEM])
        pt = sb("pt", [P, 2, 2, N])
        st = sb("st", [P, 4, XH * TT])
        mm_done, evac, sc_done, max_done, nm_done, exp_done, inv_done, p_done, turned, pt_done, o_done, \
            hi_done, lo_done = (sem(s) for s in ("mm", "evac", "sc", "max", "nm", "exp", "inv", "p", "turned",
                                                 "pt", "o", "hi", "lo"))
        steps = [(h, t) for h in range(XH) for t in range(TT)]
        NSX = len(steps)
        scale = XD ** -0.5

        with nc.Block() as block:
            @block.sync
            def _(sp):
                for n in range(first_unit + RAW, first_unit + 4 + RAW):
                    k.ring.load(sp, n)

            @block.scalar
            def _(act):
                for n in range(SL):
                    k.ring.hi(act, first_unit + n, w_hi[:, n, :])
                for n in range(4):
                    for m in range(4):
                        g = 4 * n + m
                        act.wait_ge(mm_done, g + 1)
                        nc.scalar.copy(qt[:, 2 * n + m // 2, (m % 2) * N:(m % 2 + 1) * N], ps[:, g % BK, :]
                                       ).then_inc(evac, 1)
                    if n + SL < 4:
                        k.ring.hi(act, first_unit + n + SL, w_hi[:, n % SL, :])
                for i in range(NSX + 3):
                    if i < NSX:
                        act.wait_ge(nm_done, i + 1)
                        if i >= 4:
                            act.wait_ge(turned, i - 3)
                        nc.scalar.activation(p[:, i % 4, :], ps[:, 4 + i % 2, 0:MEM], ACT.Exp, scale=scale,
                                             bias=st[:, 1, i:i + 1], accum_out=st[:, 2, i:i + 1]
                                             ).then_inc(exp_done, 1)
                    n = i - 2
                    if 0 <= n < NSX:
                        h, t = steps[n]
                        u = n // 4
                        act.wait_ge(turned, n + 1)
                        if u >= 2:
                            act.wait_ge(o_done, 2 * (u - 1))
                        nc.scalar.copy(pt[:, u % 2, :, (t % 4) * P:(t % 4 + 1) * P],
                                       ps[:, 6 + n % 2, 0:MEM].rearrange("p (m c) -> p m c", m=2)
                                       ).then_inc(pt_done, 1)
                    n = i - 3
                    if 0 <= n < NSX and n % 4 == 3:
                        u = n // 4
                        h, th = u // 2, u % 2
                        for d in range(2):
                            g = 2 * u + d
                            act.wait_ge(o_done, g + 1)
                            nc.scalar.copy(k.act_hi[:, 2 * h + d, th * N:(th + 1) * N], ps[:, g % 4, :]
                                           ).then_inc(hi_done, 1)

            @block.vector
            def _(dve):
                for n in range(4):
                    if n >= SL:
                        dve.wait_ge(mm_done, 4 * (n - SL + 1))
                    k.ring.lo(dve, first_unit + n, w_hi[:, n % SL, :], w_lo[:, n % SL, :])
                for i in range(NSX + 3):
                    if i < NSX:
                        dve.wait_ge(sc_done, i + 1)
                        nc.vector.reduce_max(st[:, 0, i:i + 1], ps[:, 4 + i % 2, 0:MEM], AX).then_inc(max_done, 1)
                        dve.wait_ge(max_done, i + 1)
                        nc.vector.tensor_scalar(st[:, 1, i:i + 1], st[:, 0, i:i + 1], -scale, None, ALU.mult
                                                ).then_inc(nm_done, 1)
                    n = i - 1
                    if 0 <= n < NSX:
                        dve.wait_ge(exp_done, n + 1)
                        nc.vector.reciprocal(st[:, 3, n:n + 1], st[:, 2, n:n + 1]).then_inc(inv_done, 1)
                        dve.wait_ge(inv_done, n + 1)
                        nc.vector.tensor_scalar(p[:, n % 4, :], p[:, n % 4, :], st[:, 3, n:n + 1], None, ALU.mult
                                                ).then_inc(p_done, 1)
                    n = i - 3
                    if 0 <= n < NSX and n % 4 == 3:
                        u = n // 4
                        h, th = u // 2, u % 2
                        for d in range(2):
                            g = 2 * u + d
                            c = slice(th * N, (th + 1) * N)
                            dve.wait_ge(hi_done, g + 1)
                            nc.vector.tensor_tensor(k.act_lo[:, 2 * h + d, c], ps[:, g % 4, :],
                                                    k.act_hi[:, 2 * h + d, c].bitcast(f32), ALU.subtract
                                                    ).then_inc(lo_done, 1)

            @block.tensor
            def _(pe):
                for n in range(4):
                    pe.wait_ge(k.ring.lo_done, first_unit + n + 1)
                    wh = w_hi[:, n % SL, :].rearrange("p (k c) -> p k c", k=KT)
                    wl = w_lo[:, n % SL, :].rearrange("p (k c) -> p k c", k=KT)
                    for m in range(4):
                        g = 4 * n + m
                        if g >= BK:
                            pe.wait_ge(evac, g - BK + 1)
                        c, tok = slice((m // 2) * P, (m // 2 + 1) * P), slice((m % 2) * N, (m % 2 + 1) * N)
                        for kk in range(KT):
                            last = mm3(nc, ps[:, g % BK, :], wh[:, kk, c], wl[:, kk, c], k.act_hi[:, kk, tok],
                                       k.act_lo[:, kk, tok], kk == 0, kk == KT - 1)
                        last.then_inc(mm_done, 1)
                pe.wait_ge(evac, 16)
                for i in range(NSX + 3):
                    if i < NSX:
                        h, t = steps[i]
                        if i >= 2:
                            pe.wait_ge(exp_done, i - 1)
                        for d in range(2):
                            last = nc.tensor.matmul(ps[:, 4 + i % 2, 0:MEM], qt[:, 2 * h + d, t * P:(t + 1) * P],
                                                    k.mk[:, 2 * h + d, :], start=(d == 0), stop=(d == 1))
                        last.then_inc(sc_done, 1)
                    n = i - 2
                    if 0 <= n < NSX:
                        pe.wait_ge(p_done, n + 1)
                        if n >= 2:
                            pe.wait_ge(pt_done, n - 1)
                        for m in range(2):
                            last = nc.tensor.transpose(ps[:, 6 + n % 2, m * P:(m + 1) * P],
                                                       p[:, n % 4, m * P:(m + 1) * P], k.ident[:, :])
                        last.then_inc(turned, 1)
                    n = i - 3
                    if 0 <= n < NSX and n % 4 == 3:
                        u = n // 4
                        h = u // 2
                        pe.wait_ge(pt_done, n + 1)
                        for d in range(2):
                            g = 2 * u + d
                            if g >= 4:
                                pe.wait_ge(lo_done, g - 3)
                            for m in range(2):
                                last = nc.tensor.matmul(ps[:, g % 4, :],
                                                        k.mv[:, m, h * XD + d * P:h * XD + (d + 1) * P],
                                                        pt[:, u % 2, m, :], start=(m == 0), stop=(m == 1))
                            last.then_inc(o_done, 1)


def expert_unit(w, n):
    c, h = n // 2, n % 2
    return w.rearrange("o (k p) n -> (o p) k n", p=P)[:, 4 * h:4 * h + 4, c * N:(c + 1) * N]


def stage_routing(nc, k, w_gate_up, b_gate_up, b_down):
    with Stage(nc) as ctx:
        def sb(nm, shape, dt=f32):
            return ctx.enter_context(nc.sbuf_tensor(f"r_{nm}", shape, dt))

        def sem(nm):
            return ctx.sem(f"r_{nm}")

        ps = k.ps
        Q = TT * TOPK
        ITEMS = MAX_ITEMS + 1
        best, besti = sb("best", [P, TT, 8]), sb("besti", [P, TT, 8], u32)
        idf, rel, ex = sb("idf", [P, TT, TOPK]), sb("rel", [P, TT, TOPK]), sb("ex", [P, TT, TOPK])
        tot, inv = sb("tot", [P, TT]), sb("inv", [P, TT])
        count_row = sb("count_row", [P, CAP])
        part = sb("part", [P, 1])
        mult_row = sb("mult_row", [P, 8])
        tokid = sb("tokid", [P, Q])
        hot = sb("hot", [P, TT, TOPK, NE])
        pick = sb("pick", [P, TT, TOPK, NE])
        member = sb("member", [P, TT, NE])
        upper, ones = sb("upper", [P, P]), sb("ones", [P, P])
        base = sb("base", [P, TT + 1, NE])
        pos = sb("pos", [P, TT, NE])
        cmp8 = sb("cmp8", [P, NE, 8])
        one32 = sb("one32", [P, NE])
        some, nitem, end_i, start_i = (sb(s, [P, NE]) for s in ("some", "nitem", "end_i", "start_i"))
        posj, startj, pb, off, itemj = (sb(s, [P, Q]) for s in ("posj", "startj", "pb", "off", "itemj"))
        cmpq = sb("cmpq", [P, Q, 8])
        in_item = sb("in_item", [P, Q, ITEMS])
        worth = sb("worth", [P, Q, 2, ITEMS])
        spare = sb("spare", [P, ITEMS, 2])
        in_off = sb("in_off", [P, Q, CAP])
        cmpe = sb("cmpe", [P, NE])
        ie, ie3 = sb("ie", [P, 1]), sb("ie3", [P, 3, NE])
        t32 = sb("t32", [P, NE])
        fields = sb("fields", [P, 8])
        si, ni, ji, left = (sb(s, [P, 1]) for s in ("si", "ni", "ji", "left"))
        fi = sb("fi", [P, 8], i32)
        b_left, b_part = sb("b_left", [NE, 3 * D]), sb("b_part", [NE, D], bf16)
        b_in, b_copied, b_less = sem("b_in"), sem("b_copied"), sem("b_less")
        w_in = [sem(f"w_in{s}") for s in range(RAW)]
        w_hi_done, w_lo_done = sem("w_hi"), sem("w_lo")
        v, made, ex_done, mm_done, table_io = sem("v"), sem("made"), sem("ex"), sem("mm"), sem("table_io")
        marks = {}

        def bc(ap, shape, *dims):
            for d in dims:
                ap = ap.unsqueeze(d)
            return ap.broadcast_to(shape)

        with nc.Block() as block:
            @block.gpsimd
            def _(pool):
                nc.gpsimd.iota(count_row[:, :], [[1, CAP]], base=0, channel_multiplier=0,
                               allow_small_or_imprecise_dtypes=True).then_inc(made, 1)
                nc.gpsimd.iota(part[:, :], [[0, 1]], base=0, channel_multiplier=1,
                               allow_small_or_imprecise_dtypes=True).then_inc(made, 1)
                nc.gpsimd.iota(mult_row[:, :], [[CAP, 8]], base=0, channel_multiplier=0,
                               allow_small_or_imprecise_dtypes=True).then_inc(made, 1)
                nc.gpsimd.iota(tokid[:, :], [[P, TT], [0, TOPK]], base=-SEQ, channel_multiplier=1,
                               allow_small_or_imprecise_dtypes=True).then_inc(made, 1)
                nc.gpsimd.memset(ones[:, :], 1.0).then_inc(made, 1)
                nc.gpsimd.memset(one32[:, :], 1.0).then_inc(made, 1)
                pool.wait_ge(made, 6)
                nc.gpsimd.affine_select(out=upper[:, :], in_=ones[:, :], compare_op=ALU.is_ge, fill=0.0, base=-1,
                                        pattern=[[1, P]], channel_multiplier=-1).then_inc(made, 1)
                for c in range(3):
                    for p, part_ in enumerate((k.bias[0:NE, c * D:(c + 1) * D], b_part[:, :])):
                        pool.wait_ge(b_copied, 4 * c + 1 + 2 * p)
                        nc.gpsimd.tensor_tensor(b_left[:, c * D:(c + 1) * D], b_left[:, c * D:(c + 1) * D], part_, ALU.subtract
                                                ).then_inc(b_less, 1)

            @block.vector
            def _(dve):
                n = [0]

                def step(ins, mark=None):
                    n[0] += 1
                    ins.then_inc(v, 1)
                    dve.wait_ge(v, n[0])
                    if mark:
                        marks[mark] = n[0]

                V = nc.vector

                def split_lo(u):
                    dve.wait_ge(w_hi_done, u + 1)
                    V.tensor_tensor(k.w_lo[:, u, :], k.ring.raw[:, u, :], k.w_hi[:, u, :].bitcast(f32), ALU.subtract
                                    ).then_inc(w_lo_done, 1)

                step(V.memset(fields[:, :], 0.0))
                for t in range(TT):
                    step(V.max(best[:, t, :], k.logits[:, t, :]))
                    step(V.max_index(besti[:, t, :], best[:, t, :], k.logits[:, t, :]))
                step(V.tensor_tensor(rel[:, :, :], best[:, :, 0:TOPK],
                                     best[:, :, 0:1].broadcast_to((P, TT, TOPK)), ALU.subtract), "rel")
                step(V.tensor_copy(idf[:, :, :], besti[:, :, 0:TOPK]))
                dve.wait_ge(made, 7)
                step(V.tensor_tensor(hot[:, :, :, :].rearrange("p t j e -> p (t j) e"),
                                     bc(count_row[:, 0:NE], (P, Q, NE), 1),
                                     bc(idf[:, :, :].rearrange("p t j -> p (t j)"), (P, Q, NE), 2), ALU.is_equal))
                step(V.tensor_tensor(member[:, :, :], hot[:, :, 0, :], hot[:, :, 1, :], ALU.add))
                for j in range(2, TOPK):
                    step(V.tensor_tensor(member[:, :, :], member[:, :, :], hot[:, :, j, :], ALU.add))
                marks["member"] = n[0]
                dve.wait_ge(ex_done, 1)
                step(V.tensor_reduce(tot[:, :], ex[:, :, :], AX, ALU.add))
                step(V.reciprocal(inv[:, :], tot[:, :]))
                step(V.tensor_tensor(k.gates[:, :, :], ex[:, :, :], bc(inv[:, :], (P, TT, TOPK), 2), ALU.mult))
                dve.wait_ge(mm_done, 2)
                total = ps[:, 1, 0:TT * NE].rearrange("p (t e) -> p t e", e=NE)
                before = ps[:, 0, 0:TT * NE].rearrange("p (t e) -> p t e", e=NE)
                step(V.memset(base[:, 0, :], 0.0))
                for t in range(TT):
                    step(V.tensor_tensor(base[:, t + 1, :], base[:, t, :], total[:, t, :], ALU.add))
                step(V.tensor_tensor(pos[:, :, :], before, base[:, 0:TT, :], ALU.add))
                counts = base[:, TT, :]
                step(V.tensor_scalar(some[:, :], counts, 1.0, None, ALU.max))
                step(V.tensor_tensor(cmp8[:, :, :], bc(some[:, :], (P, NE, 8), 2), bc(mult_row[:, :], (P, NE, 8), 1),
                                     ALU.is_gt))
                step(V.tensor_reduce(nitem[:, :], cmp8[:, :, :], AX, ALU.add))
                step(V.tensor_tensor_scan(end_i[:, :], one32[:, :], nitem[:, :], 0.0, ALU.mult, ALU.add))
                step(V.tensor_tensor(start_i[:, :], end_i[:, :], nitem[:, :], ALU.subtract))
                pk = pick[:, :, :, :]
                pk3 = pk.rearrange("p t j e -> p (t j) e")
                for j in range(TOPK):
                    step(V.tensor_tensor(pick[:, :, j, :], hot[:, :, j, :], pos[:, :, :], ALU.mult))
                step(V.tensor_reduce(posj[:, :], pk3, AX, ALU.add))
                step(V.tensor_tensor(pk3, hot[:, :, :, :].rearrange("p t j e -> p (t j) e"),
                                     bc(start_i[:, :], (P, Q, NE), 1), ALU.mult))
                step(V.tensor_reduce(startj[:, :], pk3, AX, ALU.add))
                step(V.tensor_tensor(cmpq[:, :, :], bc(posj[:, :], (P, Q, 8), 2), bc(mult_row[:, :], (P, Q, 8), 1),
                                     ALU.is_ge))
                step(V.tensor_reduce(pb[:, :], cmpq[:, :, :], AX, ALU.add))
                step(V.tensor_scalar(pb[:, :], pb[:, :], -1.0, None, ALU.add))
                step(V.scalar_tensor_tensor(out=off[:, :], in0=pb[:, :], scalar=-float(CAP), in1=posj[:, :],
                                            op0=ALU.mult, op1=ALU.add))
                step(V.tensor_tensor(itemj[:, :], pb[:, :], startj[:, :], ALU.add))
                for h in range(0, Q, Q // 4):
                    q4 = slice(h, h + Q // 4)
                    off4, item4, tok4, gate4 = (ap[:, q4] for ap in (
                        off, itemj, tokid, k.gates[:, :, :].rearrange("p t j -> p (t j)")))
                    wide, narrow = (P, Q // 4, CAP), (P, Q // 4, ITEMS)
                    V.tensor_tensor(in_off[:, q4, :], bc(count_row[:, :], wide, 1), bc(off4, wide, 2), ALU.is_equal)
                    step(V.tensor_tensor(in_item[:, q4, :], bc(count_row[:, 0:ITEMS], narrow, 1),
                                         bc(item4, narrow, 2), ALU.is_equal))
                    V.tensor_tensor(worth[:, q4, 0, :], in_item[:, q4, :], bc(tok4, narrow, 2), ALU.mult)
                    step(V.tensor_tensor(worth[:, q4, 1, :], in_item[:, q4, :], bc(gate4, narrow, 2), ALU.mult),
                         f"worth{h}")
                step(V.tensor_scalar(cmpe[:, :], end_i[:, :], part[:, 0:1], None, ALU.is_le))
                step(V.tensor_reduce(ie[:, :], cmpe[:, :], AX, ALU.add))
                step(V.tensor_tensor(ie3[:, :, :], bc(count_row[:, 0:NE], (P, 3, NE), 1),
                                     bc(ie[:, 0:1], (P, 3, NE), 2), ALU.is_equal), "ie3")
                for row, got in ((start_i[:, :], si), (counts, ni)):
                    step(V.tensor_tensor(t32[:, :], ie3[:, 0, :], row, ALU.mult))
                    step(V.tensor_reduce(got[:, :], t32[:, :], AX, ALU.add))
                step(V.tensor_tensor(ji[:, :], part[:, :], si[:, :], ALU.subtract))
                step(V.scalar_tensor_tensor(out=left[:, :], in0=ji[:, :], scalar=-float(CAP), in1=ni[:, :], op0=ALU.mult,
                                            op1=ALU.add))
                step(V.tensor_scalar(fields[:, 0:1], ie[:, :], float(NE - 1), None, ALU.min))
                step(V.tensor_scalar(fields[:, 1:2], left[:, :], float(BLOCK), None, ALU.is_gt))
                step(V.tensor_copy(fields[:, 2:3], end_i[:, NE - 1:NE]))
                step(V.tensor_copy(fi[:, :], fields[:, :]), "fields")
                for u in range(SOME_LO):
                    split_lo(u)
                dve.wait_ge(mm_done, 3)
                step(V.memset(k.rows[:, :, 1], 0))
                step(V.memset(k.slot_gate[:, :, 1], 0))
                for b, n_at in ((0, BLOCK), (1, REST)):
                    token, gate = (ps[0:n_at, 2 + b, c * ITEMS:(c + 1) * ITEMS] for c in range(2))
                    step(V.tensor_copy(k.slot_gate[0:n_at, :, b], gate))
                    step(V.tensor_scalar(spare[0:n_at, :, b], token, 0.0, part[0:n_at, 0:1], ALU.is_ge, ALU.mult))
                    step(V.scalar_tensor_tensor(out=k.rows[0:n_at, :, b], in0=token, scalar=float(SEQ),
                                                in1=spare[0:n_at, :, b], op0=ALU.add, op1=ALU.add))
                dve.wait_ge(mm_done, 4)
                step(V.tensor_copy(k.sel[:, :], ps[0:3 * NE, 4, 0:P]))

            @block.tensor
            def _(pe):
                pe.wait_ge(made, 7)
                pe.wait_ge(v, marks["member"])
                m = member[:, :, :].rearrange("p t e -> p (t e)")
                nc.tensor.matmul(ps[:, 0, 0:TT * NE], upper[:, :], m, start=True, stop=True).then_inc(mm_done, 1)
                nc.tensor.matmul(ps[:, 1, 0:TT * NE], ones[:, :], m, start=True, stop=True).then_inc(mm_done, 1)
                for q in range(Q):
                    if q % (Q // 4) == 0:
                        pe.wait_ge(v, marks[f"worth{q}"])
                    for b, at in ((0, slice(0, BLOCK)), (1, slice(BLOCK, CAP))):
                        last = nc.tensor.matmul(ps[0:at.stop - at.start, 2 + b, 0:2 * ITEMS], in_off[:, q, at],
                                                worth[:, q, :, :].rearrange("p a b -> p (a b)"), start=(q == 0),
                                                stop=(q == Q - 1))
                last.then_inc(mm_done, 1)
                pe.wait_ge(v, marks["ie3"])
                nc.tensor.transpose(ps[0:3 * NE, 4, 0:P], ie3[:, :, :].rearrange("p a e -> p (a e)"), k.ident[:, :]
                                    ).then_inc(mm_done, 1)

            @block.scalar
            def _(act):
                nc.scalar.preload_act_table_set("natural_log_exp_and_others")

                def biases(c):
                    cols, n = slice(c * D, (c + 1) * D), 4 * c
                    nc.scalar.copy(k.bias[0:NE, cols], b_left[:, c * D:(c + 1) * D]).then_inc(b_copied, 1)
                    act.wait_ge(b_less, 2 * c + 1)
                    nc.scalar.copy(b_part[:, :], b_left[:, c * D:(c + 1) * D]).then_inc(b_copied, 1)
                    act.wait_ge(b_copied, n + 2)
                    nc.scalar.copy(k.bias[NE:2 * NE, cols], b_part[:, :]).then_inc(b_copied, 1)
                    act.wait_ge(b_less, 2 * c + 2)
                    nc.scalar.copy(k.bias[2 * NE:3 * NE, cols], b_left[:, c * D:(c + 1) * D]).then_inc(b_copied, 1)

                def split_hi(u):
                    act.wait_ge(w_in[u], 16)
                    nc.scalar.copy(k.w_hi[:, u, :], k.ring.raw[:, u, :]).then_inc(w_hi_done, 1)

                act.wait_ge(v, marks["rel"])
                nc.scalar.activation(ex[:, :, :], rel[:, :, :], ACT.Exp).then_inc(ex_done, 1)
                act.wait_ge(b_in, 32)
                for u in range(RAW):
                    split_hi(u)
                    if u < 3:
                        biases(u)

            @block.sync
            def _(sp):
                for u in range(RAW):
                    sp.dma_start(k.ring.raw[:, u, :].rearrange("p (k c) -> p k c", k=4),
                                 expert_unit(w_gate_up[0, 0:1], u)).then_inc(w_in[u], 16)
                    if u == 0:
                        sp.dma_start(b_left[:, 0:2 * D], b_gate_up[0]).then_inc(b_in, 16)
                        sp.dma_start(b_left[:, 2 * D:3 * D], b_down[0]).then_inc(b_in, 16)
                sp.wait_ge(v, marks["fields"])
                sp.dma_start(k.table_dram, fi[:, :]).then_inc(table_io, 16)
                sp.wait_ge(table_io, 16)
                sp.dma_start(k.table[0:1, :], k.table_dram.rearrange("(o i) f -> o (i f)", o=1)).then_inc(table_io, 16)
                sp.wait_ge(table_io, 32)


E_FIELD, REST_FIELD, N_FIELD = range(3)


def stage_experts(nc, k, x_acc, w_gate_up, w_down):
    with Stage(nc) as ctx:
        def sb(nm, shape, dt=f32):
            return ctx.enter_context(nc.sbuf_tensor(f"e_{nm}", shape, dt))

        def sem(nm):
            return ctx.sem(f"e_{nm}")

        ps = k.ps
        NR, NS, NU = 6, 6, 12
        ROWS = (BLOCK, REST)
        B_HI, R_HI = slice(0, BLOCK), slice(BLOCK, CAP)
        R_LO, B_LO = slice(CAP, CAP + REST), slice(CAP + REST, 2 * CAP)
        R_BOTH = slice(BLOCK, CAP + REST)
        bias = k.bias
        xp, ap_ = sb("x_parts", [P, KT, 2 * CAP], f32r), sb("a_parts", [P, KT, 2 * CAP], f32r)
        fold = sb("fold", [REST, N])
        xg = sb("xg", [P, 2, D])
        ridx, sidx = sb("ridx", [P, 2], i32), sb("sidx", [P, 2], i32)
        y = sb("y", [P, 2, D])
        gt, up, sg = sb("gt", [P, 2, 2, 256]), sb("up", [P, 2, 256]), sb("sg", [P, 2, 256])
        sel = sb("sel", [3 * NE, P], bf16)
        more_raw = sb("more_raw", [P, NR - RAW, UNIT])
        more_hi, more_lo = (sb(f"more_{s}", [P, NS - n, UNIT], f32r) for s, n in (("hi", RAW), ("lo", SOME_LO)))
        raws, w_hi, w_lo = ([a[:, s, :] if s < n else b[:, s - n, :] for s in range(m)] for a, b, n, m in (
            (k.ring.raw, more_raw, RAW, NR), (k.w_hi, more_hi, RAW, NS), (k.w_lo, more_lo, SOME_LO, NS)))

        w_in = [sem(f"w_in{s}") for s in range(NR)]
        hi_done, lo_done, chunk_done, up_free, y_free = (sem(s) for s in ("w_hi", "w_lo", "chunk", "up_free", "y_free"))
        g_done, sg_done, t_done, a_done = (sem(s) for s in ("gate", "sigmoid", "prod", "act"))
        at_turned, at_hi, at_lo = sem("at_turned"), sem("at_hi"), sem("at_lo")
        x_in, ridx_done, xt_turned, xt_hi, xt_lo = (sem(s) for s in ("x_in", "ridx", "xt_turned", "xt_hi", "xt_lo"))
        sel_done, sidx_done, added, folded = sem("sel"), sem("sidx"), sem("added"), sem("folded")
        y_taken, halved = sem("y_taken"), sem("halved")
        xg_made = sem("xg_made")
        sp_passed, pool_passed, act_passed = sem("sp_passed"), sem("pool_passed"), sem("act_passed")

        def field(eng, i, f, top):
            return eng.value_load(k.table[0:1, bass.ds(i * 8 + f, 1)], min_val=0, max_val=top)

        def n_items(eng):
            return eng.value_load(k.table[0:1, N_FIELD:N_FIELD + 1], min_val=1, max_val=MAX_ITEMS)

        def load(sp, e, u):
            if u < 8:
                src = expert_unit(w_gate_up[0, bass.ds(e, 1)], u)
            else:
                src = expert_unit(w_down[0, bass.ds(e, 1)], u - 8)
            sp.dma_start(raws[u % NR].rearrange("p (k c) -> p k c", k=4), src).then_inc(w_in[u % NR], 16)

        def split_hi(act, i, u):
            act.wait_ge(w_in[u % NR], 16 * (NU // NR * i + u // NR + 1))
            nc.scalar.copy(w_hi[u % NS], raws[u % NR]).then_inc(hi_done, 1)

        def split_lo(dve, i, u):
            dve.wait_ge(hi_done, NU * i + u + 1)
            nc.vector.tensor_tensor(w_lo[u % NS], raws[u % NR], w_hi[u % NS].bitcast(f32),
                                    ALU.subtract).then_inc(lo_done, 1)

        def x_bank(q):
            return ps[:, 6 + q % 2, 0:2 * CAP].rearrange("p (k c) -> p k c", k=2)

        def a_bank(c):
            return ps[:, 4 + c % 2, 0:2 * CAP].rearrange("p (k c) -> p k c", k=2)

        def x_turn(pe, j, q):
            if q == 0:
                pe.wait_ge(x_in, 32 * (j + 1))
            pe.wait_ge(xt_lo, 4 * j + q + 1)
            for kk in range(2):
                c = (2 * q + kk) * P
                nc.tensor.transpose(x_bank(q)[:, kk, 0:BLOCK], xg[:, 0, c:c + P], k.ident[:, :])
                last = nc.tensor.transpose(x_bank(q)[:, kk, BLOCK:CAP], xg[0:REST, 1, c:c + P],
                                           k.ident[0:REST, 0:REST])
            last.then_inc(xt_turned, 1)

        def x_hi_part(act, j, q):
            act.wait_ge(xt_turned, 4 * j + q + 1)
            nc.scalar.copy(xp[:, 2 * q:2 * q + 2, 0:CAP], x_bank(q)).then_inc(xt_hi, 1)

        def low_parts(parts, q, bank, nb):
            for hi, lo in ((R_HI, R_LO), (B_HI, B_LO))[2 - nb:]:
                last = nc.vector.tensor_tensor(parts[:, 2 * q:2 * q + 2, lo], bank[:, :, hi],
                                               parts[:, 2 * q:2 * q + 2, hi].bitcast(f32), ALU.subtract)
            return last

        def x_lo_part(dve, j, q):
            dve.wait_ge(xt_hi, 4 * j + q + 1)
            low_parts(xp, q, x_bank(q), 2).then_inc(xt_lo, 1)

        def a_hi_part(act, i, c, nb):
            act.wait_ge(at_turned, 4 * i + c + 1)
            w = CAP if nb == 2 else BLOCK
            nc.scalar.copy(ap_[:, 2 * c:2 * c + 2, 0:w], a_bank(c)[:, :, 0:w]).then_inc(at_hi, 1)

        def a_lo_part(dve, i, c, nb):
            dve.wait_ge(at_hi, 4 * i + c + 1)
            low_parts(ap_, c, a_bank(c), nb).then_inc(at_lo, 1)

        def each_size(eng, rest, body):
            with eng.If(rest > 0):
                body(2)
            with eng.Else():
                body(1)

        with nc.Block() as block:
            @block.sync
            def _(sp):
                for u in range(RAW):
                    sp.sem_inc(w_in[u], 16)
                load(sp, 0, RAW)
                sp.wait_ge(x_in, 32)
                load(sp, 0, RAW + 1)
                items = n_items(sp)
                with sp.Fori(0, items) as i:
                    e = field(sp, i, E_FIELD, NE - 1)
                    e_next = field(sp, i + 1, E_FIELD, NE - 1)
                    for u in range(NU):
                        sp.wait_ge(lo_done, NU * i + u + 1)
                        load(sp, e if u + NR < NU else e_next, (u + NR) % NU)
                for u in range(NR):
                    sp.wait_ge(w_in[u], items * (16 * (NU // NR)) + 16)
                    sp.sem_inc(sp_passed, 1)

            @block.gpsimd
            def _(pool):
                def fetch_rows(j):
                    rest = field(pool, j, REST_FIELD, 1)
                    nc.gpsimd.tensor_copy(ridx[:, :].unsqueeze(1), k.rows[:, bass.ds(j, 1), :]).then_inc(ridx_done, 1)
                    pool.wait_ge(ridx_done, j + 1)
                    pool.sem_inc(pool_passed, 1)

                    def gather(b, inc):
                        nc.gpsimd.indirect_dma_start(
                            out=xg[0:ROWS[b], b, :], out_offset=None, in_=k.h_rows,
                            in_offset=bass.IndirectOffsetOnAxis(ap=ridx[0:ROWS[b], b:b + 1], axis=0)
                        ).then_inc(x_in, inc)

                    def body(nb):
                        for b in range(nb):
                            gather(b, 32 // nb)

                    each_size(pool, rest, body)

                pool.sem_inc(a_done, 1)
                pool.wait_ge(xg_made, 1)
                fetch_rows(0)
                items = n_items(pool)
                with pool.Fori(0, items) as i:
                    rest = field(pool, i, REST_FIELD, 1)

                    def activations(c, nb):
                        pool.wait_ge(sg_done, 4 * i + c + 1)
                        pool.wait_ge(t_done, 4 * i + c + 1)
                        nc.gpsimd.tensor_tensor(gt[:, c % 2, 0:nb, :], up[:, 0:nb, :], sg[:, 0:nb, :],
                                                ALU.mult).then_inc(a_done, 1)

                    each_size(pool, rest, lambda nb: activations(0, nb))
                    with pool.If(i > 0):
                        pool.wait_ge(added, 32 * i)
                        pool.sem_inc(pool_passed, 1)
                    pool.sem_inc(y_taken, 1)
                    pool.wait_ge(xt_turned, 4 * i + 4)
                    pool.sem_inc(pool_passed, 1)
                    fetch_rows(i + 1)

                    def body(nb):
                        for c in range(1, 4):
                            activations(c, nb)
                        nc.gpsimd.tensor_copy(sidx[:, :].unsqueeze(1), k.rows[:, bass.ds(i, 1), :]).then_inc(sidx_done, 1)
                        pool.wait_ge(y_free, 2 * i + 4)
                        pool.sem_inc(pool_passed, 1)
                        pool.wait_ge(sidx_done, i + 1)
                        pool.sem_inc(pool_passed, 1)
                        for b in range(nb):
                            nc.gpsimd.indirect_dma_start(
                                out=x_acc,
                                out_offset=bass.IndirectOffsetOnAxis(ap=sidx[0:ROWS[b], b:b + 1], axis=0),
                                in_=y[0:ROWS[b], b, :], in_offset=None, compute_op=ALU.add).then_inc(added, 32 // nb)

                    each_size(pool, rest, body)
                pool.wait_ge(added, items * 32)
                pool.sem_inc(pool_passed, 1)
                pool.wait_ge(x_in, items * 32 + 32)
                pool.sem_inc(pool_passed, 1)

            @block.scalar
            def _(act):
                nc.scalar.preload_act_table_set("sigmoid_and_others")
                act.sem_inc(hi_done, RAW)
                split_hi(act, 0, RAW)
                for q in range(4):
                    x_hi_part(act, 0, q)
                items = n_items(act)
                with act.Fori(0, items) as i:
                    rest = field(act, i, REST_FIELD, 1)

                    def half_rest(c):
                        if c in (0, 5):
                            act.wait_ge(y_free, 2 * i + (2 if c == 0 else 3))
                        else:
                            act.wait_ge(up_free, 4 * i + c)
                        nc.scalar.copy(fold[:, :], ps[0:REST, 2 * (c % 2) + 1, :]).then_inc(halved, 1)

                    def body(nb):
                        for c in range(4):
                            act.wait_ge(chunk_done, 6 * i + c + 1)
                            if nb == 2:
                                half_rest(c)
                            split_hi(act, i, 2 * c + 5)
                            if c >= 1:
                                a_hi_part(act, i, c - 1, nb)
                            act.wait_ge(g_done, 4 * i + c + 1)
                            act.wait_ge(a_done, 4 * i + c + 1)
                            nc.scalar.activation(sg[:, 0:nb, :], gt[:, c % 2, 0:nb, :], ACT.Sigmoid,
                                                 scale=ALPHA).then_inc(sg_done, 1)
                            split_hi(act, i, 2 * c + 6)
                        x_hi_part(act, i + 1, 0)
                        x_hi_part(act, i + 1, 1)
                        a_hi_part(act, i, 3, nb)
                        x_hi_part(act, i + 1, 2)
                        x_hi_part(act, i + 1, 3)
                        split_hi(act, i, 13)
                        for c in (4, 5):
                            cols = slice((c - 4) * N, (c - 3) * N)
                            act.wait_ge(chunk_done, 6 * i + c + 1)
                            if c == 4:
                                act.wait_ge(y_taken, i + 1)
                            act.sem_inc(act_passed, 1)
                            last = nc.scalar.activation(y[:, 0, cols], ps[:, 2 * (c % 2), :], ACT.Copy,
                                                        scale=k.slot_gate[:, bass.ds(i, 1), 0])
                            if nb == 2:
                                half_rest(c)
                            if c == 4:
                                split_hi(act, i, 14)
                            if nb == 2:
                                act.wait_ge(folded, 6 * i + c + 1)
                                act.sem_inc(act_passed, 1)
                                last = nc.scalar.activation(y[0:REST, 1, cols], fold[:, :], ACT.Copy,
                                                            scale=k.slot_gate[0:REST, bass.ds(i, 1), 1])
                            last.then_inc(y_free, 1)
                            if c == 4:
                                split_hi(act, i, 15)
                        split_hi(act, i, 16)
                        if nb == 1:
                            act.sem_inc(halved, 6)

                    each_size(act, rest, body)

            @block.vector
            def _(dve):
                V = nc.vector
                V.memset(xg[0:REST, 1, :], 0.0).then_inc(xg_made, 1)
                V.memset(gt[:, :, 1, :], 0.0)
                V.memset(up[:, 1, :], 0.0)
                dve.sem_inc(y_free, 2)
                dve.sem_inc(xt_lo, 2)
                V.tensor_copy(sel[:, :], k.sel[:, 0:1].broadcast_to((3 * NE, P))).then_inc(sel_done, 1)
                dve.sem_inc(lo_done, SOME_LO)
                for u in range(SOME_LO, RAW + 1):
                    split_lo(dve, 0, u)
                for q in range(4):
                    x_lo_part(dve, 0, q)
                items = n_items(dve)
                with dve.Fori(0, items) as i:
                    rest = field(dve, i, REST_FIELD, 1)

                    def fold_rest(c):
                        bank = ps[:, 2 * (c % 2) + 1, :]
                        dve.wait_ge(halved, 6 * i + c + 1)
                        V.tensor_tensor(fold[:, :], bank[REST:2 * REST, :], fold[:, :], ALU.add
                                        ).then_inc(folded, 1)

                    def body(nb):
                        for c in range(4):
                            n = 4 * i + c + 1
                            dve.wait_ge(chunk_done, 6 * i + c + 1)
                            g, u_ = gt[:, c % 2, 0:nb, :], up[:, 0:nb, :]
                            if nb == 2:
                                fold_rest(c)
                                dve.wait_ge(folded, 6 * i + c + 1)
                                dve.wait_ge(a_done, 4 * i + c + 1)
                                f = fold[:, :]
                                V.tensor_scalar(gt[0:REST, c % 2, 1, :], f[:, 0:N:2], LIMIT, None, ALU.min)
                                V.tensor_scalar(up[0:REST, 1, :], f[:, 1:N:2], LIMIT, -LIMIT, ALU.min, ALU.max)
                            bank = ps[:, 2 * (c % 2), :]
                            V.tensor_scalar(gt[:, c % 2, 0, :], bank[:, 0:N:2], LIMIT, None, ALU.min
                                            ).then_inc(g_done, 1)
                            if nb == 1:
                                dve.wait_ge(a_done, 4 * i + c + 1)
                            V.tensor_scalar(up[:, 0, :], bank[:, 1:N:2], LIMIT, -LIMIT, ALU.min, ALU.max
                                            ).then_inc(up_free, 1)
                            dve.wait_ge(up_free, n)
                            dve.wait_ge(g_done, n)
                            V.scalar_tensor_tensor(out=u_, in0=u_, scalar=1.0, in1=g, op0=ALU.add, op1=ALU.mult
                                                   ).then_inc(t_done, 1)
                            split_lo(dve, i, 2 * c + 5)
                            if c >= 1:
                                a_lo_part(dve, i, c - 1, nb)
                            if c < 3:
                                split_lo(dve, i, 2 * c + 6)
                        x_lo_part(dve, i + 1, 0)
                        x_lo_part(dve, i + 1, 1)
                        split_lo(dve, i, 12)
                        a_lo_part(dve, i, 3, nb)
                        x_lo_part(dve, i + 1, 2)
                        x_lo_part(dve, i + 1, 3)
                        split_lo(dve, i, 13)
                        if nb == 2:
                            dve.wait_ge(chunk_done, 6 * i + 5)
                            fold_rest(4)
                        split_lo(dve, i, 14)
                        split_lo(dve, i, 15)
                        dve.wait_ge(chunk_done, 6 * i + 6)
                        if nb == 2:
                            fold_rest(5)
                        else:
                            dve.sem_inc(folded, 6)
                        V.tensor_copy(sel[:, :], k.sel[:, bass.ds(i + 1, 1)].broadcast_to((3 * NE, P))
                                      ).then_inc(sel_done, 1)
                        split_lo(dve, i, 16)

                    each_size(dve, rest, body)

            @block.tensor
            def _(pe):
                for q in range(4):
                    x_turn(pe, 0, q)
                items = n_items(pe)
                with pe.Fori(0, items) as i:
                    rest = field(pe, i, REST_FIELD, 1)

                    def body(nb):
                        def products(c, ks, first, final):
                            src = xp if c < 4 else ap_
                            out = ps[:, 2 * (c % 2), :]
                            bias_cols = bias[:, c * N:(c + 1) * N]

                            def w_at(kk):
                                s, cols = (2 * c + kk // 4) % NS, slice((kk % 4) * N, (kk % 4 + 1) * N)
                                return w_hi[s][:, cols], w_lo[s][:, cols]

                            for kk in ks:
                                last = mm3(nc, out, src[:, kk, B_HI], src[:, kk, B_LO], *w_at(kk),
                                           first and kk == ks[0], False)
                            if final:
                                if c == 0:
                                    pe.wait_ge(sel_done, i + 1)
                                last = nc.tensor.matmul(out, sel[:, :], bias_cols, start=False, stop=True)
                            if nb == 2:
                                out = ps[:, 2 * (c % 2) + 1, :]
                                for kk in ks:
                                    hi, lo = w_at(kk)
                                    both = src[:, kk, R_BOTH]
                                    opens, closes = first and kk == ks[0], final and kk == ks[-1]
                                    if opens:
                                        nc.tensor.matmul(out, both, hi, start=True, stop=False)
                                    last = nc.tensor.matmul(out[0:REST, :], src[:, kk, R_HI], lo, start=False,
                                                            stop=False)
                                    if closes:
                                        nc.tensor.matmul(out[0:REST, :], sel[:, 0:REST], bias_cols, start=False,
                                                         stop=False)
                                    if not opens:
                                        last = nc.tensor.matmul(out, both, hi, start=False, stop=closes)
                            if final:
                                last.then_inc(chunk_done, 1)

                        def act_turn(c):
                            pe.wait_ge(a_done, 4 * i + c + 2)
                            if c >= 2:
                                pe.wait_ge(at_lo, 4 * i + c - 1)
                            for kk in range(2):
                                for b in range(nb):
                                    r, at = ROWS[b], b * BLOCK
                                    last = nc.tensor.transpose(a_bank(c)[:, kk, at:at + r],
                                                               gt[0:r, c % 2, b, kk * P:(kk + 1) * P],
                                                               k.ident[0:r, 0:r])
                            last.then_inc(at_turned, 1)

                        def parts_ready(u):
                            pe.wait_ge(lo_done, NU * i + u + 1)

                        pe.wait_ge(xt_lo, 4 * i + 6)
                        for c in range(4):
                            if c < 2:
                                pe.wait_ge(y_free, 2 * i + c + 1)
                            else:
                                pe.wait_ge(up_free, 4 * i + c - 1)
                            parts_ready(2 * c + 1)
                            products(c, list(range(KT)), True, True)
                            if c >= 1:
                                act_turn(c - 1)
                        x_turn(pe, i + 1, 0)
                        x_turn(pe, i + 1, 1)
                        pe.wait_ge(up_free, 4 * i + 3)
                        pe.wait_ge(at_lo, 4 * i + 2)
                        parts_ready(8)
                        products(4, [0, 1, 2, 3], True, False)
                        pe.wait_ge(up_free, 4 * i + 4)
                        parts_ready(10)
                        products(5, [0, 1, 2, 3], True, False)
                        pe.wait_ge(at_lo, 4 * i + 3)
                        products(4, [4, 5], False, False)
                        act_turn(3)
                        x_turn(pe, i + 1, 2)
                        x_turn(pe, i + 1, 3)
                        pe.wait_ge(at_lo, 4 * i + 4)
                        products(4, [6, 7], False, True)
                        parts_ready(11)
                        products(5, [4, 5, 6, 7], False, True)

                    each_size(pe, rest, body)


def stage_final(nc, k, x_from, g_final, out):
    with Stage(nc) as ctx:
        def sb(nm, shape, dt=f32):
            return ctx.enter_context(nc.sbuf_tensor(f"c_{nm}", shape, dt))

        def sem(nm):
            return ctx.sem(f"c_{nm}")

        xt, gain, junk, stat = sb("xt", [P, TT, D]), sb("gain", [P, D]), sb("junk", [P, D]), sb("stat", [P, 3, TT])
        x_in = [sem(f"x_in{i}") for i in range(TT)]
        g_in, sumsq, root, inv, scaled, stored = (sem(s) for s in ("g_in", "sumsq", "root", "inv", "scaled", "stored"))
        with nc.Block() as block:
            @block.sync
            def _(sp):
                for t in range(TT):
                    sp.dma_start(xt[:, t, :], x_from[t * P:(t + 1) * P, :]).then_inc(x_in[t], 16)
                    if t == 0:
                        sp.dma_start(gain[:, :], gain_row(g_final)).then_inc(g_in, 16)
                for t in range(TT):
                    sp.wait_ge(scaled, t + 1)
                    sp.dma_start(out[0, t * P:(t + 1) * P, :], xt[:, t, :]).then_inc(stored, 16)
                sp.wait_ge(stored, 16 * TT)

            @block.scalar
            def _(act):
                nc.scalar.preload_act_table_set("sqrt_and_others")
                for t in range(TT):
                    act.wait_ge(x_in[t], 16)
                    if t:
                        act.wait_ge(sumsq, t)
                    nc.scalar.activation(junk[:, :], xt[:, t, :], ACT.Square, accum_out=stat[:, 0, t:t + 1]
                                         ).then_inc(sumsq, 1)
                    act.wait_ge(sumsq, t + 1)
                    nc.scalar.activation(stat[:, 1, t:t + 1], stat[:, 0, t:t + 1], ACT.Sqrt, scale=1.0 / D,
                                         bias=k.eps[:, 0:1]).then_inc(root, 1)

            @block.vector
            def _(dve):
                dve.wait_ge(g_in, 16)
                for t in range(TT):
                    dve.wait_ge(root, t + 1)
                    nc.vector.reciprocal(stat[:, 2, t:t + 1], stat[:, 1, t:t + 1]).then_inc(inv, 1)
                    dve.wait_ge(inv, t + 1)
                    nc.vector.scalar_tensor_tensor(out=xt[:, t, :], in0=xt[:, t, :], scalar=stat[:, 2, t:t + 1],
                                                   in1=gain[:, :], op0=ALU.mult, op1=ALU.mult).then_inc(scaled, 1)


def program(nc, x, mem, g_mix, w_in, w_conv, g_conv_out, g_sb_out, w_out, g_xattn, g_mem, w_xq, w_xkv, w_xo,
            g_ffn, w_router, b_router, w_gate_up, b_gate_up, w_down, b_down, g_final, out, until=99):
    k = Kit()

    def cols(w, width):
        v = w[0].rearrange("(k p) n -> p k n", p=P)
        return [v[:, :, c:c + 256] for c in range(0, width, 256)]

    def halves(w):
        v = w[0].rearrange("(k p) n -> p k n", p=P)
        return [v[:, 4 * h:4 * h + 4, n * N:(n + 1) * N] for n in range(2) for h in range(2)]

    w_in_units = cols(w_in, 3 * D)
    order = [0, 1, 4, 5, 2, 3, 6, 7, 8, 9, 10, 11]
    units = [w_in_units[i] for i in order] + cols(w_xkv, 2 * D) + halves(w_out) + cols(w_xq, D) + halves(w_xo)

    def dram(name, shape, dt=f32):
        return nc.dram_tensor(name, shape, dt, kind="Internal").ap()

    x1 = dram("x_mixed", (SEQ, D))
    x2 = dram("x_crossed", (SEQ + P, D))
    k.h_rows = dram("expert_inputs", (SEQ + P, D))
    k.table_dram = dram("item_table", (P, 8), i32)

    with ExitStack() as ctx:
        def sb(scope, name, shape, dt=f32):
            return scope.enter_context(nc.sbuf_tensor(name, shape, dt))

        k.logits = sb(ctx, "logits", [P, TT, NE])
        k.gates = sb(ctx, "gates", [P, TT, TOPK])
        k.slot_gate = sb(ctx, "slot_gate", [P, MAX_ITEMS + 1, 2])
        k.rows = sb(ctx, "rows_of_slots", [P, MAX_ITEMS + 1, 2], i32)
        k.sel = sb(ctx, "expert_of_item", [3 * NE, P], bf16)
        k.table = sb(ctx, "item_row", [1, P * 8], i32)
        constants(nc, ctx, k)
        k.ring = Ring(nc, ctx, units)
        with ExitStack() as dense:
            k.act_hi = sb(dense, "act_hi", [P, KT, SEQ], f32r)
            k.act_lo = sb(dense, "act_lo", [P, KT, SEQ], f32r)
            with ExitStack() as mixer:
                k.y, k.q, k.k = (sb(mixer, s, [P, 4, SEQ]) for s in ("mix_y", "mix_q", "mix_k"))
                k.v = sb(mixer, "mix_v", [P, TT, 512])
                k.o = k.q
                stage_projections(nc, k, x, g_mix, w_conv)
                if until >= 2:
                    stage_stick(nc, k)
                    stage_mixer_norms(nc, k, g_conv_out, g_sb_out)
            with ExitStack() as cross:
                if until >= 3:
                    k.mk = sb(cross, "mem_k", [P, KT, MEM])
                    k.mv = sb(cross, "mem_v", [P, 2, D])
                    stage_memory(nc, k, mem, g_mem, 12)
                    stage_residual(nc, k, "mix", x[0], x1, g_xattn, 20)
                if until >= 4:
                    stage_cross(nc, k, 24)
            if until >= 4:
                stage_residual(nc, k, "ffn", x1, x2, g_ffn, 28, router=(w_router, b_router))
        k.w_hi, k.w_lo = (sb(ctx, f"first_w_{s}", [P, n, UNIT], f32r) for s, n in (("hi", RAW), ("lo", SOME_LO)))
        k.bias = sb(ctx, "expert_bias", [3 * NE, 3 * D], bf16)
        if until >= 5:
            stage_routing(nc, k, w_gate_up, b_gate_up, b_down)
        if until >= 6:
            stage_experts(nc, k, x2, w_gate_up, w_down)
            stage_final(nc, k, x2, g_final, out)


_INS = ["x", "mem", "g_mix", "w_in", "w_conv", "g_conv_out", "g_sb_out", "w_out", "g_xattn", "g_mem", "w_xq", "w_xkv",
        "w_xo", "g_ffn", "w_router", "b_router", "w_gate_up", "b_gate_up", "w_down", "b_down", "g_final"]
_OUTS = [((1, SEQ, D), "float32")]


def kernel(**inputs):
    import numpy as _np
    import concourse.bacc as _bacc
    from concourse import mybir as _mybir
    from concourse.bass_utils import run_bass_kernel_spmd as _run

    nc = _bacc.Bacc("TRN2", target_bir_lowering=False, num_devices=1)
    arrays, args = {}, []
    for name in _INS:
        a = _np.ascontiguousarray(inputs[name])
        if a.ndim == 1:
            a = a.reshape(1, -1)
        arrays[f"in_{name}_dram"] = a
        args.append(nc.dram_tensor(f"in_{name}_dram", a.shape, _mybir.dt.from_np(a.dtype), kind="ExternalInput").ap())
    for i, (shape, dtype) in enumerate(_OUTS):
        dt = _mybir.dt.from_np(_np.dtype(dtype))
        args.append(nc.dram_tensor(f"out_{i}_dram", shape, dt, kind="ExternalOutput").ap())
    program(nc, *args)
    r = _run(nc, [arrays], core_ids=[0])
    return r.results[0]["out_0_dram"]
```
